# Optimizing a Trainium2 kernel written in Bass

```python
import math
import jax, jax.numpy as jnp
from jax import lax
import numpy as np

D_MODEL = 1024
BATCH = 1
SEQ = 256
DEPTH = 2

CHUNK = 64
HEAD_DIM = 64
D_POOL = D_MODEL // 4
POOL_WINDOWS = (2, 4, 8, 16)
N_POOL_GROUPS = len(POOL_WINDOWS)
POOL_GROUP = D_POOL // N_POOL_GROUPS
D_CHUNK = 3 * D_MODEL // 8
N_CHUNK_HEADS = D_CHUNK // HEAD_DIM
LEFT_CHUNKS = 8
BAND = (LEFT_CHUNKS + 1) * CHUNK
REL_CLIP = 128
D_SB = D_MODEL - D_POOL - D_CHUNK
N_SB_HEADS = D_SB // HEAD_DIM
SB_BLOCK = 128
D_IN = D_POOL + 3 * D_CHUNK + 3 * D_SB
D_FF = ((8 * D_MODEL // 3 + 127) // 128) * 128
N_EXPERTS = 8
TOP_K = 2
D_FF_EXPERT = D_FF
N_DENSE = (DEPTH + 1) // 2
N_MOE = DEPTH // 2
ALPHA = (2.0 * DEPTH) ** 0.25
BETA = (8.0 * DEPTH) ** -0.25
LN_EPS = 1e-5
RMS_EPS = 1e-6
NEG_INF = -1e30


def layer_norm(x, g, b):
    xf = x.astype(jnp.float32)
    mu = jnp.mean(xf, axis=-1, keepdims=True)
    xc = xf - mu
    var = jnp.mean(xc * xc, axis=-1, keepdims=True)
    y = xc * lax.rsqrt(var + LN_EPS) * g.astype(jnp.float32) + b.astype(jnp.float32)
    return y.astype(x.dtype)

def rms_normalise(y):
    yf = y.astype(jnp.float32)
    return yf * lax.rsqrt(jnp.mean(yf * yf, axis=-1, keepdims=True) + RMS_EPS)

def pool_mixer(u, pool_w, pool_scale):
    B, S, _ = u.shape
    uf = u.astype(jnp.float32)
    cs = jnp.cumsum(uf, axis=1)
    t = jnp.arange(S, dtype=jnp.float32)[None, :, None]
    outs = []
    for g, w in enumerate(POOL_WINDOWS):
        c = cs[..., g * POOL_GROUP:(g + 1) * POOL_GROUP]
        lag = jnp.pad(c[:, :-w], ((0, 0), (w, 0), (0, 0)))
        cnt = jnp.minimum(t + 1.0, float(w))
        outs.append((c - lag) / cnt)
    pooled = jnp.concatenate(outs, axis=-1) - uf
    pooled = pooled.reshape(B, S, N_POOL_GROUPS, POOL_GROUP)
    y = jnp.einsum('bsgc,gcd->bsgd', pooled, pool_w.astype(jnp.float32))
    return y.reshape(B, S, D_POOL) * pool_scale.astype(jnp.float32)

def chunk_attention(q, k, v, rel_bias):
    B, S, H, d = q.shape
    nc = S // CHUNK
    qc = q.reshape(B, nc, CHUNK, H, d).astype(jnp.float32)
    pad = ((0, 0), (LEFT_CHUNKS, 0), (0, 0), (0, 0), (0, 0))
    kc = jnp.pad(k.reshape(B, nc, CHUNK, H, d).astype(jnp.float32), pad)
    vc = jnp.pad(v.reshape(B, nc, CHUNK, H, d).astype(jnp.float32), pad)
    kband = jnp.concatenate([kc[:, j:j + nc] for j in range(LEFT_CHUNKS + 1)], axis=2)
    vband = jnp.concatenate([vc[:, j:j + nc] for j in range(LEFT_CHUNKS + 1)], axis=2)
    scores = jnp.einsum('bnqhd,bnkhd->bhnqk', qc, kband) * (1.0 / math.sqrt(d))
    qi = jnp.arange(CHUNK)[:, None]
    kj = jnp.arange(BAND)[None, :]
    rel = jnp.clip(qi + LEFT_CHUNKS * CHUNK - kj, -REL_CLIP, REL_CLIP) + REL_CLIP
    bias = rel_bias.astype(jnp.float32)[:, rel]
    key_chunk = jnp.arange(nc)[:, None] - LEFT_CHUNKS + jnp.arange(BAND)[None, :] // CHUNK
    valid = key_chunk >= 0
    scores = scores + bias[None, :, None, :, :]
    scores = jnp.where(valid[None, None, :, None, :], scores, NEG_INF)
    p = jax.nn.softmax(scores, axis=-1)
    o = jnp.einsum('bhnqk,bnkhd->bnqhd', p, vband)
    return o.reshape(B, S, H * d)

def stick_breaking_attention(q, k, v):
    B, S, H, d = q.shape
    qh = q.transpose(0, 2, 1, 3).astype(jnp.float32)
    kh = k.transpose(0, 2, 1, 3).astype(jnp.float32)
    vh = v.transpose(0, 2, 1, 3).astype(jnp.float32)
    scale = 1.0 / math.sqrt(d)
    outs = []
    for blk in range(S // SB_BLOCK):
        lo = blk * SB_BLOCK
        hi = lo + SB_BLOCK
        z = jnp.einsum('bhqd,bhkd->bhqk', qh[:, :, lo:hi], kh[:, :, :hi]) * scale
        t = lo + jnp.arange(SB_BLOCK)[:, None]
        s = jnp.arange(hi)[None, :]
        before = s < t
        log_keep = jnp.where(before, jax.nn.log_sigmoid(-z), 0.0)
        suffix = lax.cumsum(log_keep, axis=3, reverse=True) - log_keep
        w = jnp.where(before, jnp.exp(jax.nn.log_sigmoid(z) + suffix), 0.0)
        outs.append(jnp.einsum('bhqk,bhkd->bhqd', w, vh[:, :, :hi]))
    o = jnp.concatenate(outs, axis=2)
    return o.transpose(0, 2, 1, 3).reshape(B, S, H * d)

def hybrid_mixer(x, w_in, pool_w, pool_scale, rel_bias, g_mix, w_out):
    B, S, _ = x.shape
    h = x @ w_in
    u_pool = h[..., :D_POOL]
    qkv_c = h[..., D_POOL:D_POOL + 3 * D_CHUNK]
    qkv_s = h[..., D_POOL + 3 * D_CHUNK:]
    y_pool = pool_mixer(u_pool, pool_w, pool_scale)
    qc, kc, vc = [a.reshape(B, S, N_CHUNK_HEADS, HEAD_DIM) for a in jnp.split(qkv_c, 3, axis=-1)]
    y_chunk = chunk_attention(qc, kc, vc, rel_bias)
    qs, ks, vs = [a.reshape(B, S, N_SB_HEADS, HEAD_DIM) for a in jnp.split(qkv_s, 3, axis=-1)]
    y_sb = stick_breaking_attention(qs, ks, vs)
    y = jnp.concatenate([rms_normalise(y_pool), rms_normalise(y_chunk), rms_normalise(y_sb)], axis=-1)
    y = (y * g_mix.astype(jnp.float32)).astype(x.dtype)
    return y @ w_out

def swiglu(x, wg, wu, wd):
    return (jax.nn.silu(x @ wg) * (x @ wu)) @ wd

def moe_swiglu(x, router, wg, wu, wd):
    B, S, D = x.shape
    xt = x.reshape(B * S, D)
    logits = (xt @ router).astype(jnp.float32)
    top_val, top_idx = lax.top_k(logits, TOP_K)
    top_w = jax.nn.softmax(top_val, axis=-1)
    gates = jnp.sum(jax.nn.one_hot(top_idx, N_EXPERTS, dtype=jnp.float32) * top_w[..., None], axis=1)
    out = jnp.zeros((B * S, D), jnp.float32)
    for e in range(N_EXPERTS):
        out = out + gates[:, e:e + 1] * swiglu(xt, wg[e], wu[e], wd[e]).astype(jnp.float32)
    return out.reshape(B, S, D).astype(x.dtype)

def first_inputs(seed: int = 0) -> dict:
    key = jax.random.key(seed)
    ks = jax.random.split(key, 20)
    f32 = jnp.float32
    n = lambda k, shape, s: jax.random.normal(k, shape, f32) * s
    x = jax.random.normal(ks[0], (BATCH, SEQ, D_MODEL), f32)
    w_in = n(ks[1], (DEPTH, D_MODEL, D_IN), D_MODEL ** -0.5)
    pool_w = n(ks[2], (DEPTH, N_POOL_GROUPS, POOL_GROUP, POOL_GROUP), POOL_GROUP ** -0.5)
    pool_scale = 1.0 + n(ks[3], (DEPTH, D_POOL), 0.05)
    rel_bias = n(ks[4], (DEPTH, N_CHUNK_HEADS, 2 * REL_CLIP + 1), 0.3)
    g_mix = 1.0 + n(ks[5], (DEPTH, D_MODEL), 0.05)
    w_out = n(ks[6], (DEPTH, D_MODEL, D_MODEL), BETA * D_MODEL ** -0.5)
    ln1_g = 1.0 + n(ks[7], (DEPTH, D_MODEL), 0.05)
    ln1_b = n(ks[8], (DEPTH, D_MODEL), 0.02)
    ln2_g = 1.0 + n(ks[9], (DEPTH, D_MODEL), 0.05)
    ln2_b = n(ks[10], (DEPTH, D_MODEL), 0.02)
    ffn_wg = n(ks[11], (N_DENSE, D_MODEL, D_FF), D_MODEL ** -0.5)
    ffn_wu = n(ks[12], (N_DENSE, D_MODEL, D_FF), D_MODEL ** -0.5)
    ffn_wd = n(ks[13], (N_DENSE, D_FF, D_MODEL), BETA * D_FF ** -0.5)
    moe_router = n(ks[14], (N_MOE, D_MODEL, N_EXPERTS), D_MODEL ** -0.5)
    moe_wg = n(ks[15], (N_MOE, N_EXPERTS, D_MODEL, D_FF_EXPERT), D_MODEL ** -0.5)
    moe_wu = n(ks[16], (N_MOE, N_EXPERTS, D_MODEL, D_FF_EXPERT), D_MODEL ** -0.5)
    moe_wd = n(ks[17], (N_MOE, N_EXPERTS, D_FF_EXPERT, D_MODEL), BETA * D_FF_EXPERT ** -0.5)
    return {"x": x, "w_in": w_in, "pool_w": pool_w, "pool_scale": pool_scale, "rel_bias": rel_bias,
            "g_mix": g_mix, "w_out": w_out, "ln1_g": ln1_g, "ln1_b": ln1_b, "ln2_g": ln2_g, "ln2_b": ln2_b,
            "ffn_wg": ffn_wg, "ffn_wu": ffn_wu, "ffn_wd": ffn_wd, "moe_router": moe_router,
            "moe_wg": moe_wg, "moe_wu": moe_wu, "moe_wd": moe_wd}

def first_block(x, w_in, pool_w, pool_scale, rel_bias, g_mix, w_out, ln1_g, ln1_b, ln2_g, ln2_b,
              ffn_wg, ffn_wu, ffn_wd, moe_router, moe_wg, moe_wu, moe_wd):
    for i in range(DEPTH):
        m = hybrid_mixer(x, w_in[i], pool_w[i], pool_scale[i], rel_bias[i], g_mix[i], w_out[i])
        x = layer_norm(ALPHA * x + m, ln1_g[i], ln1_b[i])
        j = i // 2
        if i % 2 == 0:
            f = swiglu(x, ffn_wg[j], ffn_wu[j], ffn_wd[j])
        else:
            f = moe_swiglu(x, moe_router[j], moe_wg[j], moe_wu[j], moe_wd[j])
        x = layer_norm(ALPHA * x + f, ln2_g[i], ln2_b[i])
    return x


DEPTH_2 = 4

N_MIXERS = 3
ROT_DIM = HEAD_DIM // 4
ROPE_THETA = 500000.0
NORM_EPS = 1e-6
D_FF_2 = 4 * D_MODEL

DIFF_HEADS = D_MODEL // (2 * HEAD_DIM)
DIFF_QK_WIDTH = DIFF_HEADS * 2 * HEAD_DIM
DIFF_V_DIM = 2 * HEAD_DIM
DIFF_IN = 2 * DIFF_QK_WIDTH + DIFF_HEADS * DIFF_V_DIM
DENSE_Q_BLOCK = 128

MOBA_HEADS = D_MODEL // HEAD_DIM
MOBA_BLOCK = 256
MOBA_TOPK = 3
MOBA_Q_CHUNK = 32
MOBA_IN = 3 * MOBA_HEADS * HEAD_DIM

SWA_HEADS = D_MODEL // HEAD_DIM
SWA_KV_HEADS = SWA_HEADS // 8
SWA_WINDOW = 128
SWA_Q_BLOCK = SWA_WINDOW
SWA_IN = (SWA_HEADS + 2 * SWA_KV_HEADS) * HEAD_DIM

N_DIFF = (DEPTH_2 + 2) // 3
N_MOBA = (DEPTH_2 + 1) // 3
N_SWA = DEPTH_2 // 3


def rms_norm(x, g):
    xf = x.astype(jnp.float32)
    y = xf * lax.rsqrt(jnp.mean(xf * xf, axis=-1, keepdims=True) + NORM_EPS)
    return (y * g.astype(jnp.float32)).astype(x.dtype)

def rope_tables(positions):
    inv = ROPE_THETA ** (-jnp.arange(0, ROT_DIM, 2, dtype=jnp.float32) / ROT_DIM)
    ang = positions.astype(jnp.float32)[..., None] * inv
    return jnp.cos(ang), jnp.sin(ang)

def apply_partial_rope(x, cos, sin):
    half = ROT_DIM // 2
    c = cos[:, :, None, :].astype(x.dtype)
    s = sin[:, :, None, :].astype(x.dtype)
    x1 = x[..., :half]
    x2 = x[..., half:ROT_DIM]
    return jnp.concatenate([x1 * c - x2 * s, x2 * c + x1 * s, x[..., ROT_DIM:]], axis=-1)

def diff_attention(h, w_in, w_out, lam_q1, lam_k1, lam_q2, lam_k2, sub_g, cos, sin, lambda_init):
    B, S, _ = h.shape
    H = DIFF_HEADS
    qkv = h @ w_in
    q, k, v = jnp.split(qkv, [DIFF_QK_WIDTH, 2 * DIFF_QK_WIDTH], axis=-1)
    q = apply_partial_rope(q.reshape(B, S, 2 * H, HEAD_DIM), cos, sin) * (HEAD_DIM ** -0.5)
    k = apply_partial_rope(k.reshape(B, S, 2 * H, HEAD_DIM), cos, sin)
    q = q.reshape(B, S, H, 2, HEAD_DIM)
    k = k.reshape(B, S, H, 2, HEAD_DIM)
    v = v.reshape(B, S, H, DIFF_V_DIM)
    f32 = jnp.float32
    lam = (jnp.exp(jnp.sum(lam_q1.astype(f32) * lam_k1.astype(f32)))
           - jnp.exp(jnp.sum(lam_q2.astype(f32) * lam_k2.astype(f32))) + lambda_init)
    nqb = S // DENSE_Q_BLOCK
    qb = q.reshape(B, nqb, DENSE_Q_BLOCK, H, 2, HEAD_DIM).transpose(1, 0, 2, 3, 4, 5)
    key_pos = jnp.arange(S)

    def block(args):
        qi, blk = args
        q_pos = blk * DENSE_Q_BLOCK + jnp.arange(DENSE_Q_BLOCK)
        s = jnp.einsum('bqhcd,bkhcd->bhcqk', qi, k).astype(f32)
        causal = key_pos[None, :] <= q_pos[:, None]
        s = jnp.where(causal, s, -jnp.inf)
        p = jax.nn.softmax(s, axis=-1)
        p = p[:, :, 0] - lam * p[:, :, 1]
        return jnp.einsum('bhqk,bkhe->bqhe', p.astype(v.dtype), v)

    o = lax.map(block, (qb, jnp.arange(nqb)))
    o = o.transpose(1, 0, 2, 3, 4).reshape(B, S, H, DIFF_V_DIM)
    o = rms_norm(o, sub_g) * (1.0 - lambda_init)
    return o.reshape(B, S, H * DIFF_V_DIM) @ w_out

def moba_attention(h, w_in, w_out, cos, sin):
    B, S, _ = h.shape
    H, D, Bk = MOBA_HEADS, HEAD_DIM, MOBA_BLOCK
    f32 = jnp.float32
    q, k, v = jnp.split(h @ w_in, 3, axis=-1)
    q = apply_partial_rope(q.reshape(B, S, H, D), cos, sin) * (D ** -0.5)
    k = apply_partial_rope(k.reshape(B, S, H, D), cos, sin)
    v = v.reshape(B, S, H, D)
    nb = -(-S // Bk)
    pad = nb * Bk - S
    k = jnp.pad(k, ((0, 0), (0, pad), (0, 0), (0, 0)))
    v = jnp.pad(v, ((0, 0), (0, pad), (0, 0), (0, 0)))
    K = min(MOBA_TOPK, nb)
    kb = k.reshape(B, nb, Bk, H, D).transpose(0, 3, 1, 2, 4)
    vb = v.reshape(B, nb, Bk, H, D).transpose(0, 3, 1, 2, 4)
    k_mean = jnp.mean(kb.astype(f32), axis=3).astype(k.dtype)
    nqc = S // MOBA_Q_CHUNK
    qc = q.reshape(B, nqc, MOBA_Q_CHUNK, H, D).transpose(1, 0, 3, 2, 4)
    b_idx = jnp.arange(B)[:, None, None, None]
    h_idx = jnp.arange(H)[None, :, None, None]
    blk_ids = jnp.arange(nb)
    in_blk = jnp.arange(Bk)

    def chunk(args):
        qi, ci = args
        q_pos = ci * MOBA_Q_CHUNK + jnp.arange(MOBA_Q_CHUNK)
        own = (ci * MOBA_Q_CHUNK) // Bk
        gate = jnp.einsum('bhqd,bhnd->bhqn', qi, k_mean).astype(f32)
        gate = jnp.where(blk_ids < own, gate, -jnp.inf)
        _, sel = lax.top_k(gate, K)
        valid = jnp.arange(K) < own
        ks = kb[b_idx, h_idx, sel]
        vs = vb[b_idx, h_idx, sel]
        s_sel = jnp.einsum('bhqd,bhqnkd->bhqnk', qi, ks).astype(f32)
        s_sel = jnp.where(valid[:, None], s_sel, -jnp.inf).reshape(B, H, MOBA_Q_CHUNK, K * Bk)
        k_own = lax.dynamic_index_in_dim(kb, own, axis=2, keepdims=False)
        v_own = lax.dynamic_index_in_dim(vb, own, axis=2, keepdims=False)
        s_own = jnp.einsum('bhqd,bhkd->bhqk', qi, k_own).astype(f32)
        own_pos = own * Bk + in_blk
        s_own = jnp.where(own_pos[None, :] <= q_pos[:, None], s_own, -jnp.inf)
        p = jax.nn.softmax(jnp.concatenate([s_sel, s_own], axis=-1), axis=-1).astype(v.dtype)
        p_sel = p[..., :K * Bk].reshape(B, H, MOBA_Q_CHUNK, K, Bk)
        p_own = p[..., K * Bk:]
        return (jnp.einsum('bhqnk,bhqnkd->bhqd', p_sel, vs)
                + jnp.einsum('bhqk,bhkd->bhqd', p_own, v_own))

    o = lax.map(chunk, (qc, jnp.arange(nqc)))
    o = o.transpose(1, 0, 3, 2, 4).reshape(B, S, H * D)
    return o @ w_out

def swa_sink_attention(h, w_in, b_in, sinks, w_out, cos, sin):
    B, S, _ = h.shape
    KV, D, Qb = SWA_KV_HEADS, HEAD_DIM, SWA_Q_BLOCK
    G = SWA_HEADS // KV
    f32 = jnp.float32
    qkv = h @ w_in + b_in
    q, k, v = jnp.split(qkv, [SWA_HEADS * D, (SWA_HEADS + KV) * D], axis=-1)
    q = apply_partial_rope(q.reshape(B, S, SWA_HEADS, D), cos, sin) * (D ** -0.5)
    k = apply_partial_rope(k.reshape(B, S, KV, D), cos, sin)
    v = v.reshape(B, S, KV, D)
    nb = S // Qb
    qb = q.reshape(B, nb, Qb, KV, G, D)
    kb = k.reshape(B, nb, Qb, KV, D)
    vb = v.reshape(B, nb, Qb, KV, D)
    pad_k = jnp.zeros_like(kb[:, :1])
    pad_v = jnp.zeros_like(vb[:, :1])
    k2 = jnp.concatenate([jnp.concatenate([pad_k, kb[:, :-1]], axis=1), kb], axis=2)
    v2 = jnp.concatenate([jnp.concatenate([pad_v, vb[:, :-1]], axis=1), vb], axis=2)
    s = jnp.einsum('bnqkgd,bnjkd->bnkgqj', qb, k2).astype(f32)
    qi = jnp.arange(Qb)[:, None] + Qb
    kj = jnp.arange(2 * Qb)[None, :]
    dist = qi - kj
    band = (dist >= 0) & (dist < SWA_WINDOW)
    prev_ok = (jnp.arange(nb)[:, None] > 0) | (jnp.arange(2 * Qb)[None, :] >= Qb)
    mask = band[None, :, :] & prev_ok[:, None, :]
    s = jnp.where(mask[None, :, None, None], s, -jnp.inf)
    sink = sinks.astype(f32).reshape(KV, G)[None, None, :, :, None, None]
    m = jnp.maximum(jnp.max(s, axis=-1, keepdims=True), sink)
    e = jnp.exp(s - m)
    p = (e / (jnp.sum(e, axis=-1, keepdims=True) + jnp.exp(sink - m))).astype(v.dtype)
    o = jnp.einsum('bnkgqj,bnjkd->bnqkgd', p, v2).reshape(B, S, SWA_HEADS * D)
    return o @ w_out

def sqrelu_mlp(h, w_up, w_down):
    a = jnp.maximum(h @ w_up, 0)
    return (a * a) @ w_down

def second_inputs(seed: int = 0) -> dict:
    key = jax.random.key(seed)
    ks = jax.random.split(key, 24)
    f32 = jnp.float32
    nrm = lambda k, shape, scale: jax.random.normal(k, shape, f32) * scale
    x = jax.random.normal(ks[0], (BATCH, SEQ, D_MODEL), f32)
    positions = jnp.broadcast_to(jnp.arange(SEQ, dtype=jnp.int32)[None, :], (BATCH, SEQ))
    return {
        "x": x,
        "positions": positions,
        "attn_norm_g": 1.0 + nrm(ks[1], (DEPTH_2, D_MODEL), 0.02),
        "mlp_norm_g": 1.0 + nrm(ks[2], (DEPTH_2, D_MODEL), 0.02),
        "diff_w_in": nrm(ks[3], (N_DIFF, D_MODEL, DIFF_IN), D_MODEL ** -0.5),
        "diff_w_out": nrm(ks[4], (N_DIFF, DIFF_HEADS * DIFF_V_DIM, D_MODEL), (DIFF_HEADS * DIFF_V_DIM) ** -0.5),
        "diff_lam_q1": nrm(ks[5], (N_DIFF, HEAD_DIM), 0.1),
        "diff_lam_k1": nrm(ks[6], (N_DIFF, HEAD_DIM), 0.1),
        "diff_lam_q2": nrm(ks[7], (N_DIFF, HEAD_DIM), 0.1),
        "diff_lam_k2": nrm(ks[8], (N_DIFF, HEAD_DIM), 0.1),
        "diff_subln_g": 1.0 + nrm(ks[9], (N_DIFF, DIFF_V_DIM), 0.02),
        "moba_w_in": nrm(ks[10], (N_MOBA, D_MODEL, MOBA_IN), D_MODEL ** -0.5),
        "moba_w_out": nrm(ks[11], (N_MOBA, MOBA_HEADS * HEAD_DIM, D_MODEL), (MOBA_HEADS * HEAD_DIM) ** -0.5),
        "swa_w_in": nrm(ks[12], (N_SWA, D_MODEL, SWA_IN), D_MODEL ** -0.5),
        "swa_b_in": nrm(ks[13], (N_SWA, SWA_IN), 0.02),
        "swa_sinks": nrm(ks[14], (N_SWA, SWA_HEADS), 0.5),
        "swa_w_out": nrm(ks[15], (N_SWA, SWA_HEADS * HEAD_DIM, D_MODEL), (SWA_HEADS * HEAD_DIM) ** -0.5),
        "mlp_w_up": nrm(ks[16], (DEPTH_2, D_MODEL, D_FF_2), D_MODEL ** -0.5),
        "mlp_w_down": nrm(ks[17], (DEPTH_2, D_FF_2, D_MODEL), 0.5 * D_FF_2 ** -0.5),
        "final_norm_g": 1.0 + nrm(ks[18], (D_MODEL,), 0.02),
    }

def second_block(x, positions, attn_norm_g, mlp_norm_g, diff_w_in, diff_w_out, diff_lam_q1, diff_lam_k1,
              diff_lam_q2, diff_lam_k2, diff_subln_g, moba_w_in, moba_w_out, swa_w_in, swa_b_in,
              swa_sinks, swa_w_out, mlp_w_up, mlp_w_down, final_norm_g):
    cos, sin = rope_tables(positions)
    h = x
    for i in range(DEPTH_2):
        mixer = i % N_MIXERS
        slot = i // N_MIXERS
        a = rms_norm(h, attn_norm_g[i])
        if mixer == 0:
            lambda_init = 0.8 - 0.6 * math.exp(-0.3 * i)
            y = diff_attention(a, diff_w_in[slot], diff_w_out[slot], diff_lam_q1[slot], diff_lam_k1[slot],
                               diff_lam_q2[slot], diff_lam_k2[slot], diff_subln_g[slot], cos, sin, lambda_init)
        elif mixer == 1:
            y = moba_attention(a, moba_w_in[slot], moba_w_out[slot], cos, sin)
        else:
            y = swa_sink_attention(a, swa_w_in[slot], swa_b_in[slot], swa_sinks[slot], swa_w_out[slot], cos, sin)
        h = h + y
        h = h + sqrelu_mlp(rms_norm(h, mlp_norm_g[i]), mlp_w_up[i], mlp_w_down[i])
    return rms_norm(h, final_norm_g)


def setup_inputs(seed=0):
    out = dict(first_inputs(seed))
    for name, value in second_inputs(seed + 1).items():
        if name != "x":
            out[name + "_2"] = value
    return out


def reference(
    x, w_in, pool_w, pool_scale, rel_bias, g_mix, w_out, ln1_g, ln1_b, ln2_g, ln2_b, ffn_wg,
    ffn_wu, ffn_wd, moe_router, moe_wg, moe_wu, moe_wd, positions_2, attn_norm_g_2,
    mlp_norm_g_2, diff_w_in_2, diff_w_out_2, diff_lam_q1_2, diff_lam_k1_2, diff_lam_q2_2,
    diff_lam_k2_2, diff_subln_g_2, moba_w_in_2, moba_w_out_2, swa_w_in_2, swa_b_in_2,
    swa_sinks_2, swa_w_out_2, mlp_w_up_2, mlp_w_down_2, final_norm_g_2,
):
    x = first_block(
        x, w_in, pool_w, pool_scale, rel_bias, g_mix, w_out, ln1_g, ln1_b, ln2_g, ln2_b, ffn_wg,
        ffn_wu, ffn_wd, moe_router, moe_wg, moe_wu, moe_wd,
    )
    return second_block(
        x, positions_2, attn_norm_g_2, mlp_norm_g_2, diff_w_in_2, diff_w_out_2, diff_lam_q1_2,
        diff_lam_k1_2, diff_lam_q2_2, diff_lam_k2_2, diff_subln_g_2, moba_w_in_2, moba_w_out_2,
        swa_w_in_2, swa_b_in_2, swa_sinks_2, swa_w_out_2, mlp_w_up_2, mlp_w_down_2,
        final_norm_g_2,
    )


_drawn_inputs = setup_inputs


def setup_inputs(seed=0):
    import zlib

    import numpy as np

    out = dict(_drawn_inputs(seed))
    spreads = {}
    factors = {'pool_scale': 3.129,
     'mlp_norm_g_2': 3.296,
     'diff_lam_q2_2': 4.708,
     'diff_subln_g_2': 3.842,
     'swa_b_in_2': 26.092,
     'swa_sinks_2': 18.114,
     'final_norm_g_2': 7.827}
    for name, (base, spread) in spreads.items():
        noise = np.random.default_rng([zlib.crc32(name.encode()), seed]).standard_normal(out[name].shape)
        drawn = base * np.exp(spread * noise) if base else spread * noise
        out[name] = __import__('jax').numpy.asarray(drawn.astype(out[name].dtype))
    for name, factor in factors.items():
        out[name] = (out[name] * factor).astype(out[name].dtype)
    return out
```

```python
import math
from contextlib import ExitStack

import concourse.bass as bass
from concourse import mybir

F32 = mybir.dt.float32
F32R = mybir.dt.float32r
I32 = mybir.dt.int32
U32 = mybir.dt.uint32
ALU = mybir.AluOpType
ACT = mybir.ActivationFunctionType
AX = mybir.AxisListType

P = 128
S, D = 256, 1024
NT = S // P
KT = D // P
UC = 256
HD = 64
D_POOL, D_CHUNK, D_SB = 256, 384, 384
F_MOE = 2816
F_MLP = 4096
N_EXP = 8
GE = F_MOE // UC
ALPHA = 4.0 ** 0.25
LN_EPS, RMS_EPS, NORM_EPS = 1e-5, 1e-6, 1e-6
SCALE = HD ** -0.5
REL = 257
REVW = 384

HYB, DIFF, MOBA, SWA = range(4)
KIND = [HYB, HYB, DIFF, MOBA, SWA, DIFF]
NL = len(KIND)
NPROJ = {HYB: 10, DIFF: 12, MOBA: 12, SWA: 5}
NSOFT = {HYB: 6, DIFF: 16, MOBA: 16, SWA: 16}
NSTICK = {HYB: 6, DIFF: 0, MOBA: 0, SWA: 0}
VW = {HYB: 64, DIFF: 128, MOBA: 64, SWA: 64}
OGRP = {HYB: 3, DIFF: 2, MOBA: 4, SWA: 4}
DIFF_INDEX = {2: 0, 5: 3}
LAMBDA_INIT = {l: 0.8 - 0.6 * math.exp(-0.3 * i) for l, i in DIFF_INDEX.items()}
DIFF_SLOT = {2: 0, 5: 1}


def groups(l):
    return {0: GE, 1: N_EXP * GE}.get(l, F_MLP // UC)


def before(per_layer):
    return [sum(per_layer[:l]) for l in range(len(per_layer) + 1)]


PROJ0 = before([NPROJ[k] for k in KIND])
SOFT0 = before([NSOFT[k] for k in KIND])
STICK0 = before([NSTICK[k] for k in KIND])
HEAD0 = before([NSOFT[k] + NSTICK[k] for k in KIND])
OG0 = before([(NSOFT[k] + NSTICK[k]) // OGRP[k] for k in KIND])
GRP0 = before([groups(l) for l in range(NL)])
ROOTS = [w for l in range(NL) for w in (
    [6, 1, 1, 1, 1] if KIND[l] == HYB else [1, 1] + [16] * (KIND[l] == DIFF) + [1, 1])] + [1, 1]


def plan_slots():
    turns, at, plan = [0, 0, 0], [0], []

    def take(n=1):
        out = []
        for _ in range(n):
            s = at[0] % 3
            out.append((s, turns[s]))
            turns[s] += 1
            at[0] += 1
        return out

    for l in range(NL):
        proj = take(NPROJ[KIND[l]])
        out = take(4)
        first = take(3)
        g = groups(l)
        if KIND[l] == HYB:
            for s, _ in first:
                turns[s] += g - 1
        else:
            for (s, _), n in zip(first, (g // 2 - 1, g // 2 - 1, g - 1)):
                turns[s] += n
        plan.append((proj, out, first))
    return plan


PLAN = plan_slots()
LAST_UNIT = [u for l in range(NL) for u in (PLAN[l][1][3], (PLAN[l][2][2][0], PLAN[l][2][2][1] + groups(l) - 1))]

C_ID, C_TRI, C_ONE, C_FLIP = 0, 128, 256, 384
C_CAUSAL, C_CHUNK, C_WINDOW, C_STRICT, C_STRICTNEG = (512 + 384 * i for i in range(5))
C_IOTA = 512 + 384 * 5
C_INV = C_IOTA + 8
C_HALF = C_INV + 8
C_ONECOL = C_HALF + 16
C_N = C_ONECOL + 1
NEG = -1e30
TWO_PI_1, TWO_PI_2 = 6.28125, 2 * math.pi - 6.28125
PI_SAFE = 3.1415925


def build(nc, A, out, bias_scratch):
    with ExitStack() as ctx:
        def sb(name, shape, dt=F32, scope=ctx):
            return scope.enter_context(nc.sbuf_tensor(name, shape, dt))

        def sem(name):
            return ctx.enter_context(nc.semaphore(name))

        raw = [sb(f"raw{s}", [P, 2048]) for s in range(3)]
        whi = [sb(f"whi{s}", [P, 2048], F32R) for s in range(3)]
        wlo = [sb(f"wlo{s}", [P, 2048], F32R) for s in range(3)]
        xt_hi = sb("xt_hi", [P, KT, S], F32R)
        xt_lo = sb("xt_lo", [P, KT, S], F32R)
        x = sb("x", [P, NT, D])
        y = sb("y", [P, NT, D])
        gain = [sb(f"gain{i}", [P, D]) for i in range(3)]
        cst = sb("cst", [P, C_N])
        sinks = sb("sinks", [P, 16])
        pool_scale = sb("pool_scale", [P, 2, D_POOL])
        pool_w = sb("pool_w", [HD, 2, 4, HD])
        lam_in = sb("lam_in", [P, 4, 2, HD])
        lam = sb("lam", [P, 16])
        subg = sb("subg", [P, 2, 2 * HD])
        rel_in = sb("rel_in", [12, REL])
        rel_rev = sb("rel_rev", [12, REVW])
        pos_i = sb("pos_i", [P, NT], I32)
        rope_f = sb("rope_f", [P, 6, NT, 8])
        rope_k = sb("rope_k", [P, NT, 8], I32)
        cos_sin = sb("cos_sin", [P, 2, NT, 8])
        router_w = sb("router_w", [P, KT, N_EXP])
        router_hi = sb("router_hi", [P, KT, N_EXP], F32R)
        router_lo = sb("router_lo", [P, KT, N_EXP], F32R)
        stats = sb("stats", [P, NT, 2, 6])
        mv = sb("mv", [P, NT, 2])
        mv6 = sb("mv6", [P, NT, 3])
        var = sb("var", [P, 8, 16])
        rstd = sb("rstd", [P, 8, 16])
        mx = sb("mx", [P, NT, 16])
        nmx = sb("nmx", [P, NT, 16])
        sums = sb("sums", [P, NT, 16])
        esink = sb("esink", [P, NT, 16])
        rinv = sb("rinv", [P, NT, 16])
        sq = sb("sq", [P, NT, 8])
        lg = sb("lg", [P, NT, 8])
        top = sb("top", [P, NT, 8])
        topi = sb("topi", [P, NT, 8], U32)
        topf = sb("topf", [P, NT, 8])
        gw = sb("gw", [P, NT, 8])
        gt = sb("gt", [8, S])
        with ExitStack() as mix:
            h_in = sb("h_in", [P, NT, 3072], scope=mix)
            qk = sb("qk", [HD, 4, 512], scope=mix)
            z = sb("z", [P, 4, 384], scope=mix)
            pt = sb("pt", [P, 4, 384], scope=mix)
            with ExitStack() as hyb_only:
                toep = sb("toep", [P, 6, S], scope=hyb_only)
            swa_bias = sb("swa_bias", [P, 6 * S], scope=mix)[:, 0:1280]
            o_tmp = sb("o_tmp", [P, NT, 2, P], scope=mix)
            with ExitStack() as early:
                pool_m = sb("pool_m", [P, NT, 4, S], scope=early)
                pool_t = sb("pool_t", [HD, 4, S], scope=early)
            zs = sb("zs", [P, 2, 384], scope=mix)
            es = sb("es", [P, 2, 384], scope=mix)
            sps = sb("sps", [P, 2, 384], scope=mix)
            zm = sb("zm", [P, 2, 384], scope=mix)
        with ExitStack() as ffn:
            sg = sb("sg", [P, 2 * S], scope=ffn)
            h_f = sb("h_f", [P, 2, 2 * S], scope=ffn)
            h_hi = sb("h_hi", [P, 2, 2, S], F32R, scope=ffn)
            h_lo = sb("h_lo", [P, 2, 2, S], F32R, scope=ffn)
            gate = sb("gate", [P, N_EXP, S], scope=ffn)
            sel = sb("sel", [N_EXP, N_EXP, P], scope=ffn)
        rt = [z[:, 0:4, :].rearrange("p a b -> p (a b)")[:, 0:512], z[:, 0:4, :].rearrange("p a b -> p (a b)")[:, 512:1024],
              pt[:, 0:4, :].rearrange("p a b -> p (a b)")[:, 0:512], pt[:, 0:4, :].rearrange("p a b -> p (a b)")[:, 512:1024]]
        bank = [ctx.enter_context(nc.psum_tensor(f"bank{i}", [P, 512], F32)) for i in range(8)]

        ident = cst[:, C_ID:C_ID + P]
        tri = cst[:, C_TRI:C_TRI + P]
        ones = cst[:, C_ONE:C_ONE + P]
        flip8 = cst[:, C_FLIP:C_FLIP + P]

        loaded = [sem(f"raw_loaded{s}") for s in range(3)]
        hi_ready = [sem(f"hi_ready{s}") for s in range(3)]
        lo_ready = [sem(f"lo_ready{s}") for s in range(3)]
        used = [sem(f"unit_used{s}") for s in range(3)]
        gain_loaded = [sem(f"gain_loaded{i}") for i in range(3)]
        gain_used = sem("gain_used")
        cst_loaded = sem("cst_loaded")
        x_loaded = sem("x_loaded")
        names = ["swa_bias", "sinks", "pool_scale", "pool_w", "lam", "subg", "rel", "pos", "router", "pool_m",
                 "toep", "sel"]
        got = {n: sem(f"{n}_loaded") for n in names}
        rel_done, rel_stored = sem("rel_reversed"), sem("rel_stored")
        dchain, achain, pchain = sem("vector_chain"), sem("scalar_chain"), sem("gpsimd_chain")
        nat_ready = sem("natural_ready")
        turned = sem("turned")
        t_hi, t_lo = sem("t_hi"), sem("t_lo")
        proj_done, proj_ev = sem("proj_done"), sem("proj_evacuated")
        acc_done = sem("acc_done")
        var_ready, root_ready = sem("var_ready"), sem("root_ready")
        rope_done = sem("rope_done")
        qk_turned, qk_ready = sem("qk_turned"), sem("qk_ready")
        scored, z_read = sem("scored"), sem("z_read")
        nmx_ready, p_ready = sem("nmx_ready"), sem("p_ready")
        pt_done, pt_ready = sem("pt_done"), sem("pt_ready")
        pv_done, o_read = sem("pv_done"), sem("o_read")
        sp_log, sp_ready, zm_ready = sem("stick_log"), sem("stick_sp"), sem("stick_zm")
        c_done, arg_ready, w_ready = sem("stick_sums"), sem("stick_arg"), sem("stick_w")
        pool_done, pool_copied, pool_out = sem("pool_done"), sem("pool_copied"), sem("pool_out")
        act_done, h_mid, h_ready = sem("act_done"), sem("h_mid"), sem("h_ready")
        hh_ready, hl_ready = sem("hh_ready"), sem("hl_ready")
        lam_dot, lam_exp = sem("lam_dot"), sem("lam_exp")
        rope_arg, rope_sin = sem("rope_arg"), sem("rope_sin")
        router_hi_s, router_lo_s = sem("router_hi_ready"), sem("router_lo_ready")
        logits, gap, gap_exp, gates = sem("logits"), sem("gap"), sem("gap_exp"), sem("gates")
        g_turned, g_copied, g_spread, g_stored = sem("g_turned"), sem("g_copied"), sem("g_spread"), sem("g_stored")
        y_done, stored = sem("y_done"), sem("stored")

        w_in = [A["w_in"][0], A["w_in"][1], A["diff_w_in_2"][0], A["moba_w_in_2"][0], A["swa_w_in_2"][0],
                A["diff_w_in_2"][1]]
        w_out = [A["w_out"][0], A["w_out"][1], A["diff_w_out_2"][0], A["moba_w_out_2"][0], A["swa_w_out_2"][0],
                 A["diff_w_out_2"][1]]

        def as_k(t):
            return t[:, :].rearrange("p (k f) -> p k f", k=KT)

        def as_rows(t):
            return t[:, :].rearrange("p (k d) -> p k d", k=2)

        def head_cols(l, j):
            k = KIND[l]
            if k == HYB:
                return D_POOL + j * HD, D_POOL + D_CHUNK + j * HD, D_POOL + 2 * D_CHUNK + j * HD
            if k == DIFF:
                return j * HD, D + j * HD, 2 * D + (j // 2) * 2 * HD
            if k == MOBA:
                return j * HD, D + j * HD, 2 * D + j * HD
            return j * HD, D + (j // 8) * HD, D + 2 * HD + (j // 8) * HD

        def stick_cols(j):
            base = D_POOL + 3 * D_CHUNK
            return base + j * HD, base + D_SB + j * HD, base + 2 * D_SB + j * HD

        block = ctx.enter_context(nc.Block())

        @block.sync
        def _(sp):
            sp.dma_start(x[:], A["x"][0].rearrange("(t p) d -> p t d", p=P)).then_inc(x_loaded, 16)
            sp.dma_start(cst[:], A["cst"]).then_inc(cst_loaded, 16)

            def load(place, src, k):
                slot, turn = place
                if not isinstance(turn, int) or turn > 0:
                    sp.wait_ge(lo_ready[slot], turn * 2)
                sp.dma_start(raw[slot][:, :].rearrange("p (k f) -> p k f", k=k), src).then_inc(loaded[slot], 16)

            def cols(w, c):
                return w.rearrange("(k p) f -> p k f", p=P)[:, :, c]

            def rows(w, r):
                return w[r, :].rearrange("(k p) d -> p k d", p=P)

            gains = [A["g_mix"][0], A["ln1_g"][0], A["ln1_b"][0], A["ln2_g"][0], A["ln2_b"][0],
                     A["g_mix"][1], A["ln1_g"][1], A["ln1_b"][1], A["ln2_g"][1], A["ln2_b"][1]]
            for l in range(4):
                gains += [A["attn_norm_g_2"][l], A["mlp_norm_g_2"][l]]
            gains.append(A["final_norm_g_2"])
            next_gain = [0]

            def load_gains(n):
                for _ in range(n):
                    u = next_gain[0]
                    if u >= 3:
                        sp.wait_ge(gain_used, u - 2)
                    sp.dma_start(gain[u % 3][:], gains[u].partition_broadcast(P)).then_inc(gain_loaded[u % 3], 16)
                    next_gain[0] += 1

            def load_swiglu(l, wg, wu, wd, expert):
                g = groups(l)
                (sg_, tg), (su, tu), (sd, td) = PLAN[l][2]

                def up(w, i):
                    if expert:
                        return w[bass.ds(i // GE, 1), :, bass.ds((i % GE) * UC, UC)].rearrange(
                            "a (k p) f -> p (a k) f", p=P)
                    return w[:, bass.ds(i * UC, UC)].rearrange("(k p) f -> p k f", p=P)

                def down(i):
                    return wd[bass.ds(i * UC, UC), :].rearrange("(k p) d -> p k d", p=P)

                load((sg_, tg), up(wg, 0), KT)
                load((su, tu), up(wu, 0), KT)
                load((sd, td), down(0), 2)
                load((sg_, tg + 1), up(wg, 1), KT)
                load((su, tu + 1), up(wu, 1), KT)
                load_gains(3 if l == 1 else 2)
                with sp.Fori(1, g - 1) as i:
                    load((sg_, i + (tg + 1)), up(wg, i + 1), KT)
                    load((su, i + (tu + 1)), up(wu, i + 1), KT)
                    load((sd, i + td), down(i), 2)
                load((sd, td + g - 1), down(g - 1), 2)

            def load_mlp(l):
                g = groups(l)
                wu, wd = A["mlp_w_up_2"][l - 2], A["mlp_w_down_2"][l - 2]
                (s0, t0), (s1, t1), (sd, td) = PLAN[l][2]
                us, ut = (s0, s1), (t0, t1)

                def up(i, par, turn):
                    load((us[par], ut[par] + turn), wu[:, bass.ds(i * UC, UC)].rearrange("(k p) f -> p k f", p=P), KT)

                def down(i, ):
                    load((sd, i + td), wd[bass.ds(i * UC, UC), :].rearrange("(k p) d -> p k d", p=P), 2)

                up(0, 0, 0)
                up(1, 1, 0)
                down(0)
                up(2, 0, 1)
                load_gains(1)
                with sp.Fori(0, 6) as j:
                    up(j * 2 + 3, 1, j + 1)
                    down(j * 2 + 1)
                    up(j * 2 + 4, 0, j + 2)
                    down(j * 2 + 2)
                up(g - 1, 1, g // 2 - 1)
                down(g - 3)
                down(g - 2)
                down(g - 1)

            def small():
                sp.dma_start(rel_in[:], A["rel_bias"].rearrange("l h n -> (l h) n")).then_inc(got["rel"], 16)
                sp.dma_start(pool_m[:], A["pool_m"]).then_inc(got["pool_m"], 16)
                sp.dma_start(pool_w[:], A["pool_w"].rearrange("l g c d -> c l g d")).then_inc(got["pool_w"], 16)
                sp.dma_start(pool_scale[:], A["pool_scale"].partition_broadcast(P)).then_inc(got["pool_scale"], 16)
                sp.dma_start(pos_i[:], A["positions_2"][0].rearrange("(t p) -> p t", p=P),
                             allow_slow_non_contiguous=True).then_inc(got["pos"], 16)
                for i, n in enumerate(("diff_lam_q1_2", "diff_lam_k1_2", "diff_lam_q2_2", "diff_lam_k2_2")):
                    if i:
                        sp.wait_ge(got["lam"], 16 * i)
                    sp.dma_start(lam_in[:, i], A[n].partition_broadcast(P)).then_inc(got["lam"], 16)
                sp.dma_start(subg[:], A["diff_subln_g_2"].partition_broadcast(P)).then_inc(got["subg"], 16)
                sp.dma_start(router_w[:], A["moe_router"][0].rearrange("(k p) e -> p k e", p=P)).then_inc(
                    got["router"], 16)
                sp.dma_start(sinks[:], A["swa_sinks_2"][0].partition_broadcast(P)).then_inc(got["sinks"], 16)

            def load_toeplitz(l):
                sp.dma_start(toep[:], bass.AP(bias_scratch.tensor, l * 6 * REVW,
                                              [[1, P], [REVW, 6], [1, S]])).then_inc(got["toep"], 16)

            for l in range(NL):
                proj, outp, _ = PLAN[l]
                for c in range(NPROJ[KIND[l]]):
                    load(proj[c], cols(w_in[l], slice(c * UC, (c + 1) * UC)), KT)
                    if c == 2 and l == 0:
                        small()
                    if c == 4:
                        load_gains(3 if KIND[l] == HYB else 1)
                        if l == 2:
                            sp.wait_ge(nat_ready, 8)
                            sp.dma_start(swa_bias, A["swa_b_in_2"][0].partition_broadcast(P)).then_inc(
                                got["swa_bias"], 16)
                        if l == 1:
                            sp.dma_start(pool_m[:], A["pool_m"]).then_inc(got["pool_m"], 16)
                            load_toeplitz(1)
                if l == 0:
                    sp.wait_ge(rel_done, 2)
                    sp.dma_start(bias_scratch, rel_rev[:]).then_inc(rel_stored, 16)
                    sp.wait_ge(rel_stored, 16)
                    load_toeplitz(0)
                for o in range(4):
                    load(outp[o], rows(w_out[l], slice(o * UC, (o + 1) * UC)), 2)
                if l == 0:
                    load_swiglu(0, A["ffn_wg"][0], A["ffn_wu"][0], A["ffn_wd"][0], False)
                elif l == 1:
                    sp.wait_ge(nat_ready, 2 * 3 * l + 2)
                    sp.dma_start(sel[:], A["sel"]).then_inc(got["sel"], 16)
                    load_swiglu(1, A["moe_wg"][0], A["moe_wu"][0],
                                A["moe_wd"][0].rearrange("e f d -> (e f) d"), True)
                else:
                    load_mlp(l)
            for t in range(NT):
                sp.wait_ge(y_done, t + 1)
                sp.dma_start(out[0, t * P:(t + 1) * P, :], y[:, t]).then_inc(stored, 16)
            sp.wait_ge(stored, 16 * NT)

        @block.gpsimd
        def _(pool):
            pool.wait_ge(cst_loaded, 16)
            done = [0]

            def roots(n):
                for _ in range(n):
                    r = done[0]
                    w = ROOTS[r]
                    pool.wait_ge(var_ready, r + 1)
                    pool.tensor_tensor(rstd[:, r % 8, 0:w], var[:, r % 8, 0:w], cst[:, C_HALF:C_HALF + w],
                                       ALU.pow).then_inc(root_ready, 1)
                    done[0] += 1

            def stick_masks(l):
                for h in range(NSTICK[KIND[l]]):
                    b = STICK0[l] + h
                    pool.wait_ge(z_read, HEAD0[l] + NSOFT[KIND[l]] + h + 1)
                    if b >= 2:
                        pool.wait_ge(pv_done, SOFT0[l] + NSOFT[KIND[l]] + b - 1)
                    pool.tensor_tensor(zm[:, b % 2], zs[:, b % 2], cst[:, C_STRICTNEG:C_STRICTNEG + 384],
                                       ALU.add).then_inc(zm_ready, 1)

            for l in range(NL):
                stick_masks(l)
                roots(5 if KIND[l] == HYB else 5 if KIND[l] == DIFF else 4)
            roots(2)

        @block.tensor
        def _(pe):
            pe.wait_ge(cst_loaded, 16)

            def to_t(q, src):
                for t in range(NT):
                    if q == 0:
                        pe.wait_ge(x_loaded, 16)
                    else:
                        pe.wait_ge(nat_ready, 2 * (q - 1) + t + 1)
                    for kq in range(2):
                        for k in range(4):
                            mm = pe.transpose(bank[2 * t + kq][:, k * P:(k + 1) * P],
                                              src[:, t, (4 * kq + k) * P:(4 * kq + k + 1) * P], ident)
                        mm.then_inc(turned, 1)

            def t_ready(q):
                pe.wait_ge(t_lo, 4 * (q + 1))

            def unit_ready(place):
                slot, turn = place
                pe.wait_ge(lo_ready[slot], turn * 2 + 2)

            def project(l):
                for c in range(NPROJ[KIND[l]]):
                    slot, turn = PLAN[l][0][c]
                    unit_ready(PLAN[l][0][c])
                    n = PROJ0[l] + c
                    if c >= 4:
                        pe.wait_ge(proj_ev, n - 3)
                    hi, lo = as_k(whi[slot]), as_k(wlo[slot])
                    for t in range(NT):
                        for k in range(KT):
                            for i, (a, b) in enumerate(((xt_hi, hi), (xt_lo, hi), (xt_hi, lo))):
                                mm = pe.matmul(bank[4 + c % 4][:, t * UC:(t + 1) * UC],
                                               a[:, k, t * P:(t + 1) * P], b[:, k, :],
                                               start=(k == 0 and i == 0), stop=(k == KT - 1 and i == 2))
                    mm.then_inc(used[slot], 1)

            def down(place, at, a_hi, a_lo, first, last):
                slot, _ = place
                hi, lo = as_rows(whi[slot]), as_rows(wlo[slot])
                for t in range(NT):
                    for kk in range(2):
                        for i, (a, b) in enumerate(((a_hi, hi), (a_lo, hi), (a_hi, lo))):
                            for half in range(2):
                                mm = pe.matmul(bank[4 + 2 * t + half][:, :], a[:, at + kk, t * P:(t + 1) * P],
                                               b[:, kk, half * 512:(half + 1) * 512],
                                               start=first and kk == 0 and i == 0, stop=last and kk == 1 and i == 2)
                    if last and t == 0:
                        mm.then_inc(acc_done, 1)
                return mm

            def out_project(l):
                for o in range(4):
                    unit_ready(PLAN[l][1][o])
                    mm = down(PLAN[l][1][o], 2 * o, xt_hi, xt_lo, o == 0, o == 3)
                    mm.then_inc(used[PLAN[l][1][o][0]], 1)

            def up(place, b):
                slot, _ = place
                hi, lo = as_k(whi[slot]), as_k(wlo[slot])
                for f in range(2):
                    for k in range(KT):
                        for i, (a, w) in enumerate(((xt_hi, hi), (xt_lo, hi), (xt_hi, lo))):
                            mm = pe.matmul(bank[b][:, f * S:(f + 1) * S], w[:, k, f * P:(f + 1) * P], a[:, k, :],
                                           start=(k == 0 and i == 0), stop=(k == KT - 1 and i == 2))
                mm.then_inc(used[slot], 1)

            def router():
                pe.wait_ge(router_lo_s, 1)
                for t in range(NT):
                    for k in range(KT):
                        for i, (a, w) in enumerate(((xt_hi, router_hi), (xt_lo, router_hi), (xt_hi, router_lo),
                                                    (xt_lo, router_lo))):
                            mm = pe.matmul(bank[2][:, t * 8:(t + 1) * 8], a[:, k, t * P:(t + 1) * P], w[:, k, :],
                                           start=(k == 0 and i == 0), stop=(k == KT - 1 and i == 3))
                mm.then_inc(logits, 1)

            def spread_gates():
                pe.wait_ge(gates, 1)
                for t in range(NT):
                    mm = pe.transpose(bank[2][0:8, 256 + t * P:256 + (t + 1) * P], gw[:, t, :], ident)
                mm.then_inc(g_turned, 1)
                pe.wait_ge(g_copied, 1)
                pe.wait_ge(got["sel"], 16)
                for j in range(4):
                    if j >= 2:
                        pe.wait_ge(g_stored, j - 1)
                    for e in range(2):
                        mm = pe.matmul(bank[2 + j % 2][:, e * S:(e + 1) * S], sel[:, 2 * j + e, :], gt[:],
                                       start=True, stop=True)
                    mm.then_inc(g_spread, 1)

            def swiglu(l):
                g, hb = groups(l), GRP0[l]
                (sg_, tg), (su, tu), (sd, td) = PLAN[l][2]

                def pair(i):
                    unit_ready((sg_, i + tg))
                    if not isinstance(i, int) or i > 0:
                        pe.wait_ge(h_mid, i + hb)
                    up((sg_, None), 0)
                    if isinstance(i, int) and i == 0 and l == 1:
                        spread_gates()
                    unit_ready((su, i + tu))
                    up((su, None), 1)

                def fold(i, first=False, last=False):
                    unit_ready((sd, i + td))
                    pe.wait_ge(hl_ready, i + (hb + 1))
                    down((sd, None), 0, h_hi[:, 0], h_lo[:, 0], first, last).then_inc(used[sd], 1)

                if l == 1:
                    router()
                pair(0)
                pair(1)
                fold(0, first=True)
                with pe.Fori(2, g) as i:
                    pair(i)
                    fold(i - 1)
                fold(g - 1, last=True)

            def mlp(l):
                g, hb = groups(l), GRP0[l]
                (s0, t0), (s1, t1), (sd, td) = PLAN[l][2]
                us, ut = (s0, s1), (t0, t1)

                def rise(par, turn, i):
                    unit_ready((us[par], turn + ut[par]))
                    if not isinstance(i, int) or i >= 2:
                        pe.wait_ge(act_done, i + (hb - 1))
                    up((us[par], None), par)

                def fold(par, i, first=False, last=False):
                    unit_ready((sd, i + td))
                    pe.wait_ge(hl_ready, i + (hb + 1))
                    down((sd, None), 0, h_hi[:, par], h_lo[:, par], first, last).then_inc(used[sd], 1)

                rise(0, 0, 0)
                rise(1, 0, 1)
                fold(0, 0, first=True)
                with pe.Fori(1, g // 2) as j:
                    rise(0, j, j * 2)
                    fold(1, j * 2 - 1)
                    rise(1, j, j * 2 + 1)
                    fold(0, j * 2)
                fold(1, g - 1, last=True)

            def turn_heads(l, j, qcol, kcol, g):
                if g >= 2:
                    pe.wait_ge(qk_ready, g - 1)
                for i, col in enumerate((qcol, kcol)):
                    for t in range(NT):
                        mm = pe.transpose(bank[2 + g % 2][0:HD, (2 * i + t) * P:(2 * i + t + 1) * P],
                                          h_in[:, t, col:col + HD], ident)
                mm.then_inc(qk_turned, 1)

            def soft_heads(l):
                kind = KIND[l]
                n, dv, og = NSOFT[kind], VW[kind], OGRP[kind]
                for i in range(n + 4):
                    if i < n:
                        turn_heads(l, i, *head_cols(l, i)[0:2], HEAD0[l] + i)
                    j = i - 1
                    if 0 <= j < n:
                        g = HEAD0[l] + j
                        pe.wait_ge(qk_ready, g + 1)
                        if g >= 2:
                            pe.wait_ge(z_read, g - 1)
                        b = bank[g % 2]
                        q = qk[:, g % 4]
                        plain = kind != HYB
                        pe.matmul(b[:, 0:P], q[:, 0:P], q[:, 2 * P:3 * P], start=True, stop=plain)
                        if not plain:
                            pe.wait_ge(got["toep"], 16 * (l + 1))
                            pe.matmul(b[:, 0:P], flip8, toep[:, j, P:2 * P], start=False, stop=True)
                        mm = pe.matmul(b[:, P:3 * P], q[:, P:2 * P], q[:, 2 * P:4 * P], start=True, stop=plain)
                        if not plain:
                            mm = pe.matmul(b[:, P:3 * P], flip8, toep[:, j, :], start=False, stop=True)
                        mm.then_inc(scored, 1)
                    j = i - 3
                    if 0 <= j < n:
                        s = SOFT0[l] + j
                        pe.wait_ge(p_ready, s + 1)
                        if s >= 2:
                            pe.wait_ge(pt_ready, s - 1)
                        for m in range(3):
                            mm = pe.transpose(bank[4 + s % 2][:, m * P:(m + 1) * P],
                                              z[:, s % 4, m * P:(m + 1) * P], ident)
                        mm.then_inc(pt_done, 1)
                    j = i - 4
                    if 0 <= j < n:
                        s = SOFT0[l] + j
                        pe.wait_ge(pt_ready, s + 1)
                        values(l, j, pt[:, s % 4], dv, og, j, head_cols(l, j)[2])

            def values(l, j, w, dv, og, order, vcol):
                o = OG0[l] + order // og
                if order % og == 0 and o >= 2:
                    pe.wait_ge(o_read, o - 1)
                b = bank[6 + o % 2]
                at = (order % og) * dv
                half = og * dv
                pe.matmul(b[:, at:at + dv], w[:, 0:P], h_in[:, 0, vcol:vcol + dv], start=True, stop=True)
                pe.matmul(b[:, half + at:half + at + dv], w[:, P:2 * P], h_in[:, 0, vcol:vcol + dv],
                          start=True, stop=False)
                pe.matmul(b[:, half + at:half + at + dv], w[:, 2 * P:3 * P], h_in[:, 1, vcol:vcol + dv],
                          start=False, stop=True).then_inc(pv_done, 1)

            def pool_mix(l):
                pe.wait_ge(got["pool_m"], 16 * (l + 1))
                pe.wait_ge(got["pool_w"], 16)
                for gp in range(2):
                    for g in range(2):
                        c = (2 * gp + g) * HD
                        for t in range(NT):
                            mm = pe.matmul(bank[4 + gp][0:HD, g * S:(g + 1) * S], h_in[:, t, c:c + HD],
                                           pool_m[:, t, 2 * gp + g, :], start=(t == 0), stop=(t == NT - 1))
                    mm.then_inc(pool_done, 1)
                pe.wait_ge(pool_copied, 2 * l + 2)
                for t in range(NT):
                    for g in range(4):
                        mm = pe.matmul(bank[6][:, t * D_POOL + g * HD:t * D_POOL + (g + 1) * HD],
                                       pool_t[:, g, t * P:(t + 1) * P], pool_w[:, l, g, :], start=True, stop=True)
                mm.then_inc(pool_out, 1)

            def stick_heads(l):
                n = NSTICK[HYB]
                for i in range(n + 5):
                    if i < n:
                        turn_heads(l, i, *stick_cols(i)[0:2], HEAD0[l] + NSOFT[HYB] + i)
                    h = i - 1
                    if 0 <= h < n:
                        g = HEAD0[l] + NSOFT[HYB] + h
                        pe.wait_ge(qk_ready, g + 1)
                        pe.wait_ge(z_read, g - 1)
                        q = qk[:, g % 4]
                        pe.matmul(bank[g % 2][:, 0:2 * P], q[:, 2 * P:3 * P], q[:, 0:2 * P], start=True, stop=True)
                        pe.matmul(bank[g % 2][:, 2 * P:3 * P], q[:, 3 * P:4 * P], q[:, P:2 * P],
                                  start=True, stop=True).then_inc(scored, 1)
                    h = i - 3
                    if 0 <= h < n:
                        b = STICK0[l] + h
                        pe.wait_ge(sp_ready, b + 1)
                        if h >= 2:
                            pe.wait_ge(arg_ready, b - 1)
                        o = bank[4 + b % 2]
                        pe.matmul(o[:, 0:2 * P], tri, sps[:, b % 2, 0:2 * P], start=True, stop=False,
                                  skip_group_check=True)
                        pe.matmul(o[:, P:2 * P], ones, sps[:, b % 2, 2 * P:3 * P], start=False, stop=True,
                                  skip_group_check=True)
                        pe.matmul(o[:, 2 * P:3 * P], tri, sps[:, b % 2, 2 * P:3 * P], start=True,
                                  stop=True).then_inc(c_done, 1)
                    h = i - 5
                    if 0 <= h < n:
                        b = STICK0[l] + h
                        pe.wait_ge(w_ready, b + 1)
                        values(l, h, zm[:, b % 2], HD, OGRP[HYB], NSOFT[HYB] + h, stick_cols(h)[2])

            for l in range(NL):
                to_t(3 * l, x if KIND[l] == HYB else y)
                t_ready(3 * l)
                project(l)
                pe.wait_ge(proj_ev, PROJ0[l + 1])
                if KIND[l] == HYB:
                    pool_mix(l)
                else:
                    pe.wait_ge(rope_done, l - 1)
                soft_heads(l)
                if KIND[l] == HYB:
                    stick_heads(l)
                to_t(3 * l + 1, y)
                t_ready(3 * l + 1)
                out_project(l)
                to_t(3 * l + 2, x if KIND[l] == HYB else y)
                t_ready(3 * l + 2)
                (swiglu if KIND[l] == HYB else mlp)(l)

        @block.scalar
        def _(act):
            chain = [0]

            def link(ins):
                chain[0] += 1
                ins.then_inc(achain, 1)
                act.wait_ge(achain, chain[0])

            def hi(place):
                slot, turn = place
                if not isinstance(turn, int) or turn > 0:
                    act.wait_ge(used[slot], turn)
                act.wait_ge(loaded[slot], turn * 16 + 16)
                for half in range(2):
                    act.activation(whi[slot][:, half * 1024:(half + 1) * 1024], raw[slot][:, half * 1024:(half + 1) * 1024],
                                   ACT.Copy).then_inc(hi_ready[slot], 1)

            def to_t(q):
                for n in range(4):
                    act.wait_ge(turned, 4 * q + n + 1)
                    t, kq = divmod(n, 2)
                    act.activation(xt_hi[:, 4 * kq:4 * kq + 4, t * P:(t + 1) * P],
                                   bank[n][:, :].rearrange("p (k s) -> p k s", k=4), ACT.Copy).then_inc(t_hi, 1)

            def project(l):
                proj = PLAN[l][0]
                for c in range(len(proj)):
                    if KIND[l] != SWA:
                        act.wait_ge(used[proj[c][0]], proj[c][1] + 1)
                        act.activation(h_in[:, :, c * UC:(c + 1) * UC],
                                       bank[4 + c % 4][:, :].rearrange("p (t c) -> p t c", t=NT),
                                       ACT.Copy).then_inc(proj_ev, 1)
                    if c + 3 < len(proj):
                        hi(proj[c + 3])

            def copy_qk(g):
                act.wait_ge(qk_turned, g + 1)
                if g >= 4:
                    act.wait_ge(scored, g - 3)
                act.activation(qk[:, g % 4], bank[2 + g % 2][0:HD, :], ACT.Copy).then_inc(qk_ready, 1)

            def soft_heads(l):
                kind = KIND[l]
                n = NSOFT[kind]
                for i in range(n + 2):
                    if i < n:
                        copy_qk(HEAD0[l] + i)
                    j = i - 2
                    if 0 <= j < n:
                        s = SOFT0[l] + j
                        act.wait_ge(nmx_ready, s + 1)
                        ins = act.activation(z[:, s % 4, 0:P], z[:, s % 4, 0:P], ACT.Exp, bias=nmx[:, 0, j:j + 1],
                                             accum_out=sums[:, 0, j:j + 1])
                        ins = act.activation(z[:, s % 4, P:3 * P], z[:, s % 4, P:3 * P], ACT.Exp,
                                             bias=nmx[:, 1, j:j + 1], accum_out=sums[:, 1, j:j + 1])
                        if kind == SWA:
                            ins = act.activation(esink[:, :, j], nmx[:, :, j], ACT.Exp, bias=sinks[:, j:j + 1])
                        ins.then_inc(p_ready, 1)
                    if i in (1, 3, 5):
                        hi(PLAN[l][1][i // 2])

            def stick_heads(l):
                n = NSTICK[HYB]
                for i in range(n + 4):
                    if i < n:
                        copy_qk(HEAD0[l] + NSOFT[HYB] + i)
                    h = i - 2
                    if 0 <= h < n:
                        b = STICK0[l] + h
                        e = es[:, b % 2]
                        act.wait_ge(z_read, HEAD0[l] + NSOFT[HYB] + h + 1)
                        if h >= 2:
                            act.wait_ge(sp_ready, b - 1)
                        link(act.activation(e, zs[:, b % 2], ACT.Abs))
                        link(act.activation(e, e, ACT.Exp, scale=-1.0))
                        act.activation(e, e, ACT.Ln, bias=cst[:, C_ONECOL:C_ONECOL + 1]).then_inc(sp_log, 1)
                    h = i - 4
                    if 0 <= h < n:
                        b = STICK0[l] + h
                        act.wait_ge(arg_ready, b + 1)
                        act.activation(zm[:, b % 2], zm[:, b % 2], ACT.Exp).then_inc(w_ready, 1)

            def hidden_hi(par, i, hb, sd, td, back, gated=False):
                if gated:
                    act.wait_ge(h_ready, i + 1)
                else:
                    act.wait_ge(h_mid, i + (hb + 1))
                if not isinstance(i, int) or i >= back:
                    act.wait_ge(used[sd], i + (td + 1 - back))
                act.activation(h_hi[:, par], h_f[:, par, :].rearrange("p (f s) -> p f s", f=2), ACT.Copy).then_inc(hh_ready, 1)

            def swiglu(l):
                g, hb = groups(l), GRP0[l]
                (sg_, tg), (su, tu), (sd, td) = PLAN[l][2]

                def silu(i):
                    act.wait_ge(used[su], i + (tu + 1))
                    if not isinstance(i, int) or i > 0:
                        act.wait_ge(h_mid, i + hb)
                    act.activation(sg[:], bank[0][:, :], ACT.Silu).then_inc(act_done, 1)

                hi((sg_, tg + 1))
                silu(0)
                hi((su, tu + 1))
                hidden_hi(0, 0, hb, sd, td, 1, l == 1)
                with act.Fori(1, g - 1) as i:
                    hi((sg_, i + (tg + 1)))
                    silu(i)
                    hi((su, i + (tu + 1)))
                    hidden_hi(0, i, hb, sd, td, 1, l == 1)
                    hi((sd, i + td))
                silu(g - 1)
                hidden_hi(0, g - 1, hb, sd, td, 1, l == 1)
                hi((sd, td + g - 1))

            def mlp(l):
                g, hb = groups(l), GRP0[l]
                (s0, t0), (s1, t1), (sd, td) = PLAN[l][2]
                us, ut = (s0, s1), (t0, t1)

                def relu(par, turn, i):
                    act.wait_ge(used[us[par]], turn + (ut[par] + 1))
                    if not isinstance(i, int) or i > 0:
                        act.wait_ge(h_mid, i + hb)
                    act.activation(sg[:], bank[par][:, :], ACT.Relu).then_inc(act_done, 1)

                relu(0, 0, 0)
                hi((s0, t0 + 1))
                hidden_hi(0, 0, hb, sd, td, 2)
                with act.Fori(0, 6) as j:
                    relu(1, j, j * 2 + 1)
                    hi((s1, j + (t1 + 1)))
                    hidden_hi(1, j * 2 + 1, hb, sd, td, 2)
                    hi((sd, j * 2 + (td + 1)))
                    relu(0, j + 1, j * 2 + 2)
                    hi((s0, j + (t0 + 2)))
                    hidden_hi(0, j * 2 + 2, hb, sd, td, 2)
                    hi((sd, j * 2 + (td + 2)))
                for i in range(g - 3, g):
                    relu(i % 2, i // 2, i)
                    if i == g - 3:
                        hi((s1, t1 + g // 2 - 1))
                    hidden_hi(i % 2, i, hb, sd, td, 2)
                    hi((sd, td + i))

            def setup():
                act.wait_ge(got["router"], 16)
                act.activation(router_hi[:], router_w[:], ACT.Copy).then_inc(router_hi_s, 1)
                act.wait_ge(lam_dot, 1)
                act.activation(lam[:, 4:8], lam[:, 0:4], ACT.Exp).then_inc(lam_exp, 1)
                act.wait_ge(rope_arg, 1)
                act.activation(cos_sin[:], rope_f[:, 4:6], ACT.Sin).then_inc(rope_sin, 1)

            for l in range(NL):
                proj, outp, first = PLAN[l]
                if l == 0:
                    for c in range(2):
                        hi(proj[c])
                to_t(3 * l)
                hi(proj[2])
                project(l)
                if l == 0:
                    setup()
                if KIND[l] == HYB:
                    for gp in range(2):
                        act.wait_ge(pool_done, 2 * l + gp + 1)
                        act.activation(pool_t[:, 2 * gp:2 * gp + 2, :],
                                       bank[4 + gp][0:HD, :].rearrange("p (g s) -> p g s", g=2),
                                       ACT.Copy).then_inc(pool_copied, 1)
                soft_heads(l)
                if KIND[l] == HYB:
                    stick_heads(l)
                to_t(3 * l + 1)
                hi(outp[3])
                for i in range(2):
                    hi(first[i])
                to_t(3 * l + 2)
                hi(first[2])
                if l == 1:
                    act.wait_ge(gap, 1)
                    act.activation(topf[:, :, 4:5], topf[:, :, 3:4], ACT.Exp).then_inc(gap_exp, 1)
                (swiglu if KIND[l] == HYB else mlp)(l)
                if l + 1 < NL:
                    for c in range(2):
                        hi(PLAN[l + 1][0][c])

        @block.vector
        def _(dve):
            chain = [0]
            asked = [0]
            gains_at = [0]

            def link(ins):
                chain[0] += 1
                ins.then_inc(dchain, 1)
                dve.wait_ge(dchain, chain[0])

            def lo(place):
                slot, turn = place
                for half in range(2):
                    h = slice(half * 1024, (half + 1) * 1024)
                    dve.wait_ge(hi_ready[slot], turn * 2 + half + 1)
                    dve.tensor_tensor(wlo[slot][:, h], raw[slot][:, h], whi[slot][:, h].bitcast(F32),
                                      ALU.subtract).then_inc(lo_ready[slot], 1)

            def to_t(q):
                for n in range(4):
                    dve.wait_ge(t_hi, 4 * q + n + 1)
                    t, kq = divmod(n, 2)
                    dve.tensor_tensor(xt_lo[:, 4 * kq:4 * kq + 4, t * P:(t + 1) * P],
                                      bank[n][:, :].rearrange("p (k s) -> p k s", k=4),
                                      xt_hi[:, 4 * kq:4 * kq + 4, t * P:(t + 1) * P].bitcast(F32),
                                      ALU.subtract).then_inc(t_lo, 1)

            def ask_root(src, scale, eps, w):
                r = asked[0]
                asked[0] += 1
                dve.tensor_scalar(var[:, r % 8, 0:w], src, scale, eps, ALU.mult, ALU.add).then_inc(var_ready, 1)
                return r

            def root(r):
                dve.wait_ge(root_ready, r + 1)
                return rstd[:, r % 8]

            def next_gain():
                u = gains_at[0]
                gains_at[0] += 1
                dve.wait_ge(gain_loaded[u % 3], 16 * (u // 3 + 1))
                return gain[u % 3]

            def acc_ready(acc, t):
                if t == 0:
                    dve.wait_ge(acc_done, acc + 1)
                else:
                    slot, turn = LAST_UNIT[acc]
                    dve.wait_ge(used[slot], turn + 1)

            def residual_norm(acc, to_turn=True):
                asks = []
                g, b = next_gain(), next_gain()
                for t in range(NT):
                    acc_ready(acc, t)
                    for half in range(2):
                        c = slice(half * 512, (half + 1) * 512)
                        ins = dve.scalar_tensor_tensor(out=x[:, t, c], in0=x[:, t, c], scalar=ALPHA,
                                                       in1=bank[4 + 2 * t + half][:, :], op0=ALU.mult, op1=ALU.add)
                    link(ins)
                    for half in range(2):
                        ins = dve.bn_stats(stats[:, t, half], x[:, t, half * 512:(half + 1) * 512])
                    link(ins)
                    link(dve.bn_aggr(mv[:, t], stats[:, t]))
                    asks.append(ask_root(mv[:, t, 1:2], 1.0, LN_EPS, 1))
                for t in range(NT):
                    r = root(asks[t])
                    link(dve.tensor_scalar(x[:, t], x[:, t], mv[:, t, 0:1], r[:, 0:1], ALU.subtract, ALU.mult))
                    link(dve.tensor_tensor(x[:, t], x[:, t], g[:], ALU.mult))
                    ins = dve.tensor_tensor(x[:, t], x[:, t], b[:], ALU.add)
                    if to_turn:
                        ins.then_inc(nat_ready, 1)
                if to_turn:
                    nat[0] += 2
                    dve.wait_ge(nat_ready, nat[0])
                else:
                    link(ins)
                gain_done(2)

            nat = [0]

            def gain_done(n):
                for _ in range(n):
                    dve.engine_nop().then_inc(gain_used, 1)

            def rms_norm(final=False):
                asks = []
                g = next_gain()
                for t in range(NT):
                    link(dve.tensor_tensor_reduce(y[:, t], x[:, t], x[:, t], 1.0, 0.0, ALU.mult, ALU.add,
                                                  sq[:, t, 0:1]))
                    asks.append(ask_root(sq[:, t, 0:1], 1.0 / D, NORM_EPS, 1))
                for t in range(NT):
                    r = root(asks[t])
                    ins = dve.scalar_tensor_tensor(out=y[:, t], in0=x[:, t], scalar=r[:, 0:1], in1=g[:],
                                                   op0=ALU.mult, op1=ALU.mult)
                    ins.then_inc(y_done if final else nat_ready, 1)
                if not final:
                    nat[0] += 2
                    dve.wait_ge(nat_ready, nat[0])
                    gain_done(1)

            def add_residual(acc):
                for t in range(NT):
                    acc_ready(acc, t)
                    for half in range(2):
                        c = slice(half * 512, (half + 1) * 512)
                        ins = dve.tensor_tensor(x[:, t, c], x[:, t, c], bank[4 + 2 * t + half][:, :], ALU.add)
                link(ins)

            def setup():
                dve.wait_ge(got["rel"], 16)
                dve.tensor_copy(rel_rev[:, 127:REVW], rel_in[:, REL - 1::-1]).then_inc(rel_done, 1)
                dve.tensor_copy(rel_rev[:, 0:127], rel_in[:, REL - 1:REL].broadcast_to([12, 127])).then_inc(rel_done, 1)
                dve.wait_ge(router_hi_s, 1)
                dve.tensor_tensor(router_lo[:], router_w[:], router_hi[:].bitcast(F32), ALU.subtract).then_inc(
                    router_lo_s, 1)
                dve.wait_ge(got["lam"], 64)
                for i in range(2):
                    for d in range(2):
                        ins = dve.tensor_tensor_reduce(lam_in[:, 2 * i, d], lam_in[:, 2 * i, d], lam_in[:, 2 * i + 1, d],
                                                       1.0, 0.0, ALU.mult, ALU.add, lam[:, 2 * i + d:2 * i + d + 1])
                ins.then_inc(lam_dot, 1)
                dve.wait_ge(got["pos"], 16)
                link(dve.tensor_copy(rope_f[:, 0, :, 0], pos_i[:]))
                for t in range(NT):
                    ins = dve.tensor_scalar(rope_f[:, 1, t], cst[:, C_INV:C_INV + 8], rope_f[:, 0, t, 0:1], None, ALU.mult)
                link(ins)
                link(dve.tensor_scalar(rope_k[:], rope_f[:, 1], 1.0 / (2 * math.pi), None, ALU.mult))
                link(dve.tensor_copy(rope_f[:, 2], rope_k[:]))
                link(dve.scalar_tensor_tensor(out=rope_f[:, 3], in0=rope_f[:, 2], scalar=-TWO_PI_1, in1=rope_f[:, 1],
                                              op0=ALU.mult, op1=ALU.add))
                link(dve.scalar_tensor_tensor(out=rope_f[:, 3], in0=rope_f[:, 2], scalar=-TWO_PI_2, in1=rope_f[:, 3],
                                              op0=ALU.mult, op1=ALU.add))
                link(dve.tensor_scalar(rope_f[:, 4], rope_f[:, 3], math.pi / 2, None, ALU.add))
                link(dve.tensor_scalar(rope_f[:, 1], rope_f[:, 4], math.pi, -2 * math.pi, ALU.is_gt, ALU.mult))
                link(dve.tensor_tensor(rope_f[:, 4], rope_f[:, 4], rope_f[:, 1], ALU.add))
                link(dve.tensor_scalar(rope_f[:, 4], rope_f[:, 4], PI_SAFE, -PI_SAFE, ALU.min, ALU.max))
                dve.tensor_scalar(rope_f[:, 5], rope_f[:, 3], PI_SAFE, -PI_SAFE, ALU.min, ALU.max).then_inc(rope_arg, 1)
                dve.wait_ge(lam_exp, 1)
                for l, d in DIFF_SLOT.items():
                    link(dve.tensor_tensor(lam[:, 8 + d:9 + d], lam[:, 6 + d:7 + d], lam[:, 4 + d:5 + d], ALU.subtract))
                    link(dve.tensor_scalar(lam[:, 10 + d:11 + d], lam[:, 8 + d:9 + d], -LAMBDA_INIT[l], None, ALU.add))
                dve.wait_ge(got["subg"], 16)
                for l, d in DIFF_SLOT.items():
                    link(dve.tensor_scalar(subg[:, d], subg[:, d], 1.0 - LAMBDA_INIT[l], None, ALU.mult))

            def rotate(l):
                n = 18 if KIND[l] == SWA else 32
                if l == 2:
                    dve.wait_ge(rope_sin, 1)
                dve.wait_ge(proj_ev, PROJ0[l + 1])
                heads = h_in[:, :, 0:n * HD].rearrange("p t (h c) -> p t h c", c=HD)
                x1, x2 = heads[:, :, :, 0:8], heads[:, :, :, 8:16]
                tmp = [r[:, 0:NT * n * 8].rearrange("p (t h c) -> p t h c", t=NT, c=8) for r in rt]

                def table(i):
                    return cos_sin[:, i].rearrange("p t c -> p t () c").broadcast_to([P, NT, n, 8])

                for i, (a, c) in enumerate(((x1, 0), (x2, 1), (x2, 0), (x1, 1))):
                    ins = dve.tensor_tensor(tmp[i], a, table(c), ALU.mult)
                link(ins)
                dve.tensor_tensor(x1, tmp[0], tmp[1], ALU.subtract)
                dve.tensor_tensor(x2, tmp[2], tmp[3], ALU.add).then_inc(rope_done, 1)

            def finish_group(l, order, soft):
                kind = KIND[l]
                og, dv = OGRP[kind], VW[kind]
                if order % og != og - 1:
                    return
                gi = order // og
                o = OG0[l] + gi
                b = bank[6 + o % 2]
                j0 = order - og + 1
                dve.wait_ge(pv_done, HEAD0[l] + order + 1)
                src = b[:, 0:NT * og * dv].rearrange("p (t h c) -> p t h c", t=NT, c=dv)
                if not soft:
                    at = D_POOL + D_CHUNK + (j0 - NSOFT[HYB]) * HD
                    link(dve.tensor_copy(y[:, :, at:at + og * HD].rearrange("p t (h c) -> p t h c", c=HD), src))
                else:
                    j = slice(j0, j0 + og)
                    if kind == SWA:
                        link(dve.tensor_tensor(sums[:, :, j], sums[:, :, j], esink[:, :, j], ALU.add))
                    link(dve.reciprocal(rinv[:, :, j], sums[:, :, j]))
                    if kind == DIFF:
                        d = DIFF_SLOT[l]
                        link(dve.tensor_scalar(rinv[:, :, j0 + 1:j0 + 2], rinv[:, :, j0 + 1:j0 + 2],
                                               lam[:, 10 + d:11 + d], None, ALU.mult))
                    r = rinv[:, :, j].rearrange("p t h -> p t h ()").broadcast_to([P, NT, og, dv])
                    if kind == DIFF:
                        link(dve.tensor_tensor(o_tmp[:], src, r, ALU.mult))
                        h = j0 // 2
                        link(dve.tensor_tensor(y[:, :, h * P:(h + 1) * P], o_tmp[:, :, 0], o_tmp[:, :, 1], ALU.add))
                        for t in range(NT):
                            ins = dve.tensor_tensor_reduce(o_tmp[:, t, 0], y[:, t, h * P:(h + 1) * P],
                                                           y[:, t, h * P:(h + 1) * P], 1.0, 0.0, ALU.mult, ALU.add,
                                                           sq[:, t, h:h + 1])
                        link(ins)
                    else:
                        at = (D_POOL if kind == HYB else 0) + j0 * HD
                        link(dve.tensor_tensor(y[:, :, at:at + og * dv].rearrange("p t (h c) -> p t h c", c=dv), src, r,
                                               ALU.mult))
                dve.engine_nop().then_inc(o_read, 1)

            def soft_heads(l):
                kind = KIND[l]
                n = NSOFT[kind]
                mask = cst[:, {HYB: C_CHUNK, SWA: C_WINDOW}.get(kind, C_CAUSAL):][:, 0:384]
                if kind == SWA:
                    dve.wait_ge(got["sinks"], 16)
                if kind != HYB:
                    dve.wait_ge(rope_done, l - 1)
                for i in range(n + 4):
                    j = i - 1
                    if 0 <= j < n:
                        g, s = HEAD0[l] + j, SOFT0[l] + j
                        dve.wait_ge(scored, g + 1)
                        if s >= 4:
                            dve.wait_ge(pt_done, s - 3)
                        for t, c in enumerate((slice(0, P), slice(P, 3 * P))):
                            ins = dve.tensor_tensor_reduce(z[:, s % 4, c], bank[g % 2][:, c], mask[:, c], SCALE, -3e38,
                                                           ALU.add, ALU.max, mx[:, t, j:j + 1])
                        ins.then_inc(z_read, 1)
                        dve.wait_ge(z_read, g + 1)
                        if kind == SWA:
                            dve.tensor_scalar(nmx[:, :, j], mx[:, :, j], sinks[:, j:j + 1], -1.0, ALU.max,
                                              ALU.mult).then_inc(nmx_ready, 1)
                        else:
                            dve.tensor_scalar(nmx[:, :, j], mx[:, :, j], -1.0, None, ALU.mult).then_inc(nmx_ready, 1)
                    if i in (1, 3, 5):
                        lo(PLAN[l][1][i // 2])
                    j = i - 3
                    if 0 <= j < n:
                        s = SOFT0[l] + j
                        dve.wait_ge(pt_done, s + 1)
                        dve.tensor_copy(pt[:, s % 4], bank[4 + s % 2][:, 0:384]).then_inc(pt_ready, 1)
                    j = i - 4
                    if 0 <= j < n:
                        finish_group(l, j, True)

            def stick_heads(l):
                n = NSTICK[HYB]
                for i in range(n + 6):
                    h = i - 1
                    if 0 <= h < n:
                        b = STICK0[l] + h
                        g = HEAD0[l] + NSOFT[HYB] + h
                        dve.wait_ge(scored, g + 1)
                        if h >= 2:
                            dve.wait_ge(zm_ready, b - 1)
                            dve.wait_ge(sp_ready, b - 1)
                        dve.tensor_scalar(zs[:, b % 2], bank[g % 2][:, 0:384], SCALE, None, ALU.mult).then_inc(z_read, 1)
                    h = i - 2
                    if 0 <= h < n:
                        b = STICK0[l] + h
                        dve.wait_ge(sp_log, b + 1)
                        if h >= 2:
                            dve.wait_ge(c_done, b - 1)
                        link(dve.scalar_tensor_tensor(out=sps[:, b % 2], in0=zs[:, b % 2], scalar=0.0, in1=es[:, b % 2],
                                                      op0=ALU.max, op1=ALU.add))
                        dve.tensor_tensor(sps[:, b % 2], sps[:, b % 2], cst[:, C_STRICT:C_STRICT + 384],
                                          ALU.mult).then_inc(sp_ready, 1)
                    h = i - 3
                    if 0 <= h < n:
                        b = STICK0[l] + h
                        dve.wait_ge(c_done, b + 1)
                        dve.wait_ge(zm_ready, b + 1)
                        dve.tensor_tensor(zm[:, b % 2], zm[:, b % 2], bank[4 + b % 2][:, 0:384],
                                          ALU.subtract).then_inc(arg_ready, 1)
                    h = i - 5
                    if 0 <= h < n:
                        finish_group(l, NSOFT[HYB] + h, False)

            def mixer_norm(l):
                g = next_gain()
                parts = ((0, D_POOL), (D_POOL, D_CHUNK), (D_POOL + D_CHUNK, D_SB))
                for t in range(NT):
                    for i, (at, w) in enumerate(parts):
                        ins = dve.tensor_tensor_reduce(h_in[:, t, at:at + w], y[:, t, at:at + w], y[:, t, at:at + w],
                                                       1.0 / w, 0.0, ALU.mult, ALU.add, sq[:, t, i:i + 1])
                link(ins)
                link(dve.tensor_copy(mv6[:], sq[:, :, 0:3]))
                r = root(ask_root(mv6[:].rearrange("p t c -> p (t c)"), 1.0, RMS_EPS, 6))
                for t in range(NT):
                    for i, (at, w) in enumerate(parts):
                        ins = dve.scalar_tensor_tensor(out=y[:, t, at:at + w], in0=y[:, t, at:at + w],
                                                       scalar=r[:, 3 * t + i:3 * t + i + 1], in1=g[:, at:at + w],
                                                       op0=ALU.mult, op1=ALU.mult)
                    ins.then_inc(nat_ready, 1)
                nat[0] += 2
                dve.wait_ge(nat_ready, nat[0])
                gain_done(1)

            def head_norm(l):
                r = root(ask_root(sq[:].rearrange("p t h -> p (t h)"), 1.0 / P, NORM_EPS, 16))
                for t in range(NT):
                    v = y[:, t].rearrange("p (h c) -> p h c", c=P)
                    link(dve.tensor_tensor(v, v, r[:, 8 * t:8 * t + 8].rearrange("p h -> p h ()").broadcast_to([P, 8, P]),
                                           ALU.mult))
                    dve.tensor_tensor(v, v, subg[:, DIFF_SLOT[l]].rearrange("p c -> p () c").broadcast_to([P, 8, P]),
                                      ALU.mult).then_inc(nat_ready, 1)
                nat[0] += 2

            def y_in_place():
                for _ in range(NT):
                    dve.engine_nop().then_inc(nat_ready, 1)
                nat[0] += 2

            def gates_of(l):
                dve.wait_ge(logits, 1)
                link(dve.tensor_copy(lg[:], bank[2][:, 0:16].rearrange("p (t e) -> p t e", t=NT)))
                for t in range(NT):
                    ins = dve.max(top[:, t], lg[:, t])
                link(ins)
                for t in range(NT):
                    ins = dve.max_index(topi[:, t], top[:, t], lg[:, t])
                link(ins)
                dve.tensor_copy(topf[:, :, 0:2], topi[:, :, 0:2])
                dve.tensor_tensor(topf[:, :, 3:4], top[:, :, 1:2], top[:, :, 0:1], ALU.subtract).then_inc(gap, 1)
                dve.wait_ge(gap_exp, 1)
                link(dve.tensor_scalar(topf[:, :, 5:6], topf[:, :, 4:5], 1.0, None, ALU.add))
                link(dve.reciprocal(topf[:, :, 6:7], topf[:, :, 5:6]))
                link(dve.tensor_tensor(topf[:, :, 7:8], topf[:, :, 6:7], topf[:, :, 4:5], ALU.mult))
                for t in range(NT):
                    for i, dst in ((0, gw), (1, lg)):
                        ins = dve.tensor_scalar(dst[:, t], cst[:, C_IOTA:C_IOTA + 8], topf[:, t, i:i + 1],
                                                topf[:, t, 6 + i:7 + i], ALU.is_equal, ALU.mult)
                link(ins)
                dve.tensor_tensor(gw[:], gw[:], lg[:], ALU.add).then_inc(gates, 1)
                dve.wait_ge(g_turned, 1)
                dve.tensor_copy(gt[:], bank[2][0:8, 256:512]).then_inc(g_copied, 1)
                for j in range(4):
                    dve.wait_ge(g_spread, j + 1)
                    dve.tensor_copy(gate[:, 2 * j:2 * j + 2, :],
                                    bank[2 + j % 2][:, :].rearrange("p (e s) -> p e s", e=2)).then_inc(g_stored, 1)
                dve.wait_ge(g_stored, 4)

            def hidden_lo(par, i, hb):
                dve.wait_ge(hh_ready, i + (hb + 1))
                dve.tensor_tensor(h_lo[:, par], h_f[:, par, :].rearrange("p (f s) -> p f s", f=2),
                                  h_hi[:, par].bitcast(F32), ALU.subtract).then_inc(hl_ready, 1)

            def swiglu(l):
                g, hb = groups(l), GRP0[l]
                (sg_, tg), (su, tu), (sd, td) = PLAN[l][2]

                def hidden(i):
                    dve.wait_ge(act_done, i + (hb + 1))
                    if not isinstance(i, int) or i > 0:
                        dve.wait_ge(hl_ready, i + hb)
                    dve.tensor_tensor(h_f[:, 0], sg[:], bank[1][:, :], ALU.mult).then_inc(h_mid, 1)
                    if l == 1:
                        dve.wait_ge(h_mid, i + (hb + 1))
                        e = i // GE
                        one = gate[:, e:e + 1, :] if isinstance(i, int) else gate[:, bass.ds(e, 1), :]
                        hv = h_f[:, 0, :].rearrange("p (f s) -> p f s", f=2)
                        dve.tensor_tensor(hv, hv, one.broadcast_to([P, 2, S]), ALU.mult).then_inc(h_ready, 1)

                lo((sg_, tg + 1))
                hidden(0)
                lo((su, tu + 1))
                hidden_lo(0, 0, hb)
                with dve.Fori(1, g - 1) as i:
                    lo((sg_, i + (tg + 1)))
                    hidden(i)
                    lo((su, i + (tu + 1)))
                    hidden_lo(0, i, hb)
                    lo((sd, i + td))
                hidden(g - 1)
                hidden_lo(0, g - 1, hb)
                lo((sd, td + g - 1))

            def mlp(l):
                g, hb = groups(l), GRP0[l]
                (s0, t0), (s1, t1), (sd, td) = PLAN[l][2]

                def square(par, i):
                    dve.wait_ge(act_done, i + (hb + 1))
                    if not isinstance(i, int) or i >= 2:
                        dve.wait_ge(hl_ready, i + (hb - 1))
                    dve.tensor_tensor(h_f[:, par], sg[:], sg[:], ALU.mult).then_inc(h_mid, 1)

                square(0, 0)
                lo((s0, t0 + 1))
                hidden_lo(0, 0, hb)
                with dve.Fori(0, 6) as j:
                    square(1, j * 2 + 1)
                    lo((s1, j + (t1 + 1)))
                    hidden_lo(1, j * 2 + 1, hb)
                    lo((sd, j * 2 + (td + 1)))
                    square(0, j * 2 + 2)
                    lo((s0, j + (t0 + 2)))
                    hidden_lo(0, j * 2 + 2, hb)
                    lo((sd, j * 2 + (td + 2)))
                for i in range(g - 3, g):
                    square(i % 2, i)
                    if i == g - 3:
                        lo((s1, t1 + g // 2 - 1))
                    hidden_lo(i % 2, i, hb)
                    lo((sd, td + i))

            for l in range(NL):
                proj, outp, first = PLAN[l]
                if l == 0:
                    for c in range(2):
                        lo(proj[c])
                to_t(3 * l)
                lo(proj[2])
                for c in range(len(proj)):
                    if KIND[l] == SWA:
                        dve.wait_ge(got["swa_bias"], 16)
                        dve.wait_ge(used[proj[c][0]], proj[c][1] + 1)
                        dve.tensor_tensor(h_in[:, :, c * UC:(c + 1) * UC],
                                          bank[4 + c % 4][:, :].rearrange("p (t c) -> p t c", t=NT),
                                          swa_bias[:, c * UC:(c + 1) * UC].rearrange("p c -> p () c").broadcast_to(
                                              [P, NT, UC]), ALU.add).then_inc(proj_ev, 1)
                    if c + 3 < len(proj):
                        lo(proj[c + 3])
                if l == 0:
                    dve.wait_ge(cst_loaded, 16)
                    setup()
                if KIND[l] == HYB:
                    dve.wait_ge(got["pool_scale"], 16)
                    dve.wait_ge(pool_out, l + 1)
                    link(dve.tensor_tensor(y[:, :, 0:D_POOL], bank[6][:, :].rearrange("p (t c) -> p t c", t=NT),
                                           pool_scale[:, l].rearrange("p c -> p () c").broadcast_to([P, NT, D_POOL]),
                                           ALU.mult))
                else:
                    rotate(l)
                soft_heads(l)
                if KIND[l] == HYB:
                    stick_heads(l)
                    mixer_norm(l)
                elif KIND[l] == DIFF:
                    head_norm(l)
                else:
                    y_in_place()
                to_t(3 * l + 1)
                lo(outp[3])
                for i in range(2):
                    lo(first[i])
                if KIND[l] == HYB:
                    if l == 0:
                        dve.wait_ge(x_loaded, 16)
                    residual_norm(2 * l)
                else:
                    add_residual(2 * l)
                    rms_norm()
                to_t(3 * l + 2)
                lo(first[2])
                if l == 1:
                    gates_of(l)
                (swiglu if KIND[l] == HYB else mlp)(l)
                if l + 1 < NL:
                    for c in range(2):
                        lo(PLAN[l + 1][0][c])
                if KIND[l] == HYB:
                    residual_norm(2 * l + 1, to_turn=(l == 0))
                else:
                    add_residual(2 * l + 1)
                if l >= 1:
                    rms_norm(final=(l == NL - 1))


def constants():
    import numpy as np
    f = np.float32
    c = np.zeros((P, C_N), f)
    i = np.arange(P)[:, None]
    j = np.arange(P)[None, :]
    c[:, C_ID:C_ID + P] = i == j
    c[:, C_TRI:C_TRI + P] = i >= j
    c[:, C_ONE:C_ONE + P] = 1
    c[:, C_FLIP:C_FLIP + P] = 8.0 * (i + j == P - 1)
    kt = np.arange(S)[None, :]

    def two_tiles(ok):
        return np.where(np.concatenate([ok(i, kt[:, :P]), ok(i + P, kt)], axis=1), 0.0, NEG).astype(f)

    c[:, C_CAUSAL:C_CAUSAL + 384] = two_tiles(lambda q, k: k <= q)
    c[:, C_CHUNK:C_CHUNK + 384] = two_tiles(lambda q, k: k // 64 <= q // 64)
    c[:, C_WINDOW:C_WINDOW + 384] = two_tiles(lambda q, k: (k <= q) & (q - k < 128))
    strict = np.concatenate([i < kt, (i + P) < kt[:, P:]], axis=1)
    c[:, C_STRICT:C_STRICT + 384] = strict
    c[:, C_STRICTNEG:C_STRICTNEG + 384] = np.where(strict, 0.0, NEG)
    c[:, C_IOTA:C_IOTA + 8] = np.arange(8)
    c[:, C_INV:C_INV + 8] = (f(500000.0) ** (-np.arange(0, 16, 2, dtype=f) / f(16))).astype(f)
    c[:, C_HALF:C_HALF + 16] = -0.5
    c[:, C_ONECOL] = 1
    tq, ts = np.arange(S)[None, :], np.arange(S)[:, None]
    pm = np.zeros((P, NT, 4, S), f)
    for g, w in enumerate((2, 4, 8, 16)):
        m = ((tq >= ts) & (tq - ts < w)) / np.minimum(tq + 1.0, w) - (tq == ts)
        pm[:, :, g, :] = m.astype(f).reshape(NT, P, S).transpose(1, 0, 2)
    sel = np.zeros((8, 8, P), f)
    for e in range(8):
        sel[e, e] = 1
    return {"cst": c, "pool_m": pm, "sel": sel}


_INS = ["x", "w_in", "pool_w", "pool_scale", "rel_bias", "g_mix", "w_out", "ln1_g", "ln1_b", "ln2_g", "ln2_b",
        "ffn_wg", "ffn_wu", "ffn_wd", "moe_router", "moe_wg", "moe_wu", "moe_wd", "positions_2", "attn_norm_g_2",
        "mlp_norm_g_2", "diff_w_in_2", "diff_w_out_2", "diff_lam_q1_2", "diff_lam_k1_2", "diff_lam_q2_2",
        "diff_lam_k2_2", "diff_subln_g_2", "moba_w_in_2", "moba_w_out_2", "swa_w_in_2", "swa_b_in_2", "swa_sinks_2",
        "swa_w_out_2", "mlp_w_up_2", "mlp_w_down_2", "final_norm_g_2"]


def kernel(**inputs):
    import numpy as np
    import concourse.bacc as bacc
    from concourse.bass_utils import run_bass_kernel_spmd as run

    nc = bacc.Bacc("TRN2", target_bir_lowering=False, num_devices=1)
    arrays = {name: np.ascontiguousarray(inputs[name]) for name in _INS}
    arrays.update(constants())
    aps = {name: nc.dram_tensor("in_" + name, a.shape, mybir.dt.from_np(a.dtype), kind="ExternalInput").ap()
           for name, a in arrays.items()}
    out = nc.dram_tensor("out", (1, S, D), F32, kind="ExternalOutput").ap()
    scratch = nc.dram_tensor("bias_scratch", (12, REVW), F32, kind="Internal").ap()
    build(nc, aps, out, scratch)
    r = run(nc, [{"in_" + n: a for n, a in arrays.items()}], core_ids=[0])
    return r.results[0]["out"]
```

```python
import math
from contextlib import ExitStack

import concourse.bass as bass
from concourse import mybir

F32 = mybir.dt.float32
F32R = mybir.dt.float32r
I32 = mybir.dt.int32
U32 = mybir.dt.uint32
ALU = mybir.AluOpType
ACT = mybir.ActivationFunctionType
AX = mybir.AxisListType

P = 128
S, D = 256, 1024
NT = S // P
KT = D // P
UC = 256
HD = 64
D_POOL, D_CHUNK, D_SB = 256, 384, 384
F_MOE = 2816
F_MLP = 4096
N_EXP = 8
GE = F_MOE // UC
ALPHA = 4.0 ** 0.25
LN_EPS, RMS_EPS, NORM_EPS = 1e-5, 1e-6, 1e-6
SCALE = HD ** -0.5
REL = 257
REVW = 384

HYB, DIFF, MOBA, SWA = range(4)
KIND = [HYB, HYB, DIFF, MOBA, SWA, DIFF]
NL = len(KIND)
NPROJ = {HYB: 10, DIFF: 12, MOBA: 12, SWA: 5}
NSOFT = {HYB: 6, DIFF: 16, MOBA: 16, SWA: 16}
NSTICK = {HYB: 6, DIFF: 0, MOBA: 0, SWA: 0}
VW = {HYB: 64, DIFF: 128, MOBA: 64, SWA: 64}
OGRP = {HYB: 3, DIFF: 2, MOBA: 4, SWA: 4}
DIFF_INDEX = {2: 0, 5: 3}
LAMBDA_INIT = {l: 0.8 - 0.6 * math.exp(-0.3 * i) for l, i in DIFF_INDEX.items()}
DIFF_SLOT = {2: 0, 5: 1}


def groups(l):
    return {0: GE, 1: N_EXP * GE}.get(l, F_MLP // UC)


def before(per_layer):
    return [sum(per_layer[:l]) for l in range(len(per_layer) + 1)]


PROJ0 = before([NPROJ[k] for k in KIND])
SOFT0 = before([NSOFT[k] for k in KIND])
STICK0 = before([NSTICK[k] for k in KIND])
HEAD0 = before([NSOFT[k] + NSTICK[k] for k in KIND])
OG0 = before([(NSOFT[k] + NSTICK[k]) // OGRP[k] for k in KIND])
GRP0 = before([groups(l) for l in range(NL)])
ROOTS = [w for l in range(NL) for w in (
    [6, 1, 1, 1, 1] if KIND[l] == HYB else [1, 1] + [16] * (KIND[l] == DIFF) + [1, 1])] + [1, 1]


def plan_slots():
    turns, at, plan = [0, 0, 0], [0], []

    def take(n=1):
        out = []
        for _ in range(n):
            s = at[0] % 3
            out.append((s, turns[s]))
            turns[s] += 1
            at[0] += 1
        return out

    for l in range(NL):
        proj = take(NPROJ[KIND[l]])
        out = take(4)
        first = take(3)
        g = groups(l)
        if KIND[l] == HYB:
            for s, _ in first:
                turns[s] += g - 1
        else:
            for (s, _), n in zip(first, (g // 2 - 1, g // 2 - 1, g - 1)):
                turns[s] += n
        plan.append((proj, out, first))
    return plan


PLAN = plan_slots()
LAST_UNIT = [u for l in range(NL) for u in (PLAN[l][1][3], (PLAN[l][2][2][0], PLAN[l][2][2][1] + groups(l) - 1))]

C_ID, C_TRI, C_ONE, C_FLIP = 0, 128, 256, 384
C_CAUSAL, C_CHUNK, C_WINDOW, C_STRICT, C_STRICTNEG = (512 + 384 * i for i in range(5))
C_IOTA = 512 + 384 * 5
C_INV = C_IOTA + 8
C_HALF = C_INV + 8
C_ONECOL = C_HALF + 16
C_N = C_ONECOL + 1
NEG = -1e30
TWO_PI_1, TWO_PI_2 = 6.28125, 2 * math.pi - 6.28125
PI_SAFE = 3.1415925


def build(nc, A, out, bias_scratch):
    with ExitStack() as ctx:
        def sb(name, shape, dt=F32, scope=ctx):
            return scope.enter_context(nc.sbuf_tensor(name, shape, dt))

        def sem(name):
            return ctx.enter_context(nc.semaphore(name))

        raw = [sb(f"raw{s}", [P, 2048]) for s in range(3)]
        whi = [sb(f"whi{s}", [P, 2048], F32R) for s in range(3)]
        wlo = [sb(f"wlo{s}", [P, 2048], F32R) for s in range(3)]
        xt_hi = sb("xt_hi", [P, KT, S], F32R)
        xt_lo = sb("xt_lo", [P, KT, S], F32R)
        x = sb("x", [P, NT, D])
        y = sb("y", [P, NT, D])
        gain = [sb(f"gain{i}", [P, D]) for i in range(3)]
        cst = sb("cst", [P, C_N])
        sinks = sb("sinks", [P, 16])
        pool_scale = sb("pool_scale", [P, 2, D_POOL])
        pool_w = sb("pool_w", [HD, 2, 4, HD])
        lam_in = sb("lam_in", [P, 4, 2, HD])
        lam = sb("lam", [P, 16])
        subg = sb("subg", [P, 2, 2 * HD])
        rel_in = sb("rel_in", [12, REL])
        rel_rev = sb("rel_rev", [12, REVW])
        pos_i = sb("pos_i", [P, NT], I32)
        rope_f = sb("rope_f", [P, 6, NT, 8])
        rope_k = sb("rope_k", [P, NT, 8], I32)
        cos_sin = sb("cos_sin", [P, 2, NT, 8])
        router_w = sb("router_w", [P, KT, N_EXP])
        router_hi = sb("router_hi", [P, KT, N_EXP], F32R)
        router_lo = sb("router_lo", [P, KT, N_EXP], F32R)
        stats = sb("stats", [P, NT, 2, 6])
        mv = sb("mv", [P, NT, 2])
        mv6 = sb("mv6", [P, NT, 3])
        var = sb("var", [P, 8, 16])
        rstd = sb("rstd", [P, 8, 16])
        mx = sb("mx", [P, NT, 16])
        nmx = sb("nmx", [P, NT, 16])
        sums = sb("sums", [P, NT, 16])
        esink = sb("esink", [P, NT, 16])
        rinv = sb("rinv", [P, NT, 16])
        sq = sb("sq", [P, NT, 8])
        lg = sb("lg", [P, NT, 8])
        top = sb("top", [P, NT, 8])
        topi = sb("topi", [P, NT, 8], U32)
        topf = sb("topf", [P, NT, 8])
        gw = sb("gw", [P, NT, 8])
        chosen = sb("chosen", [P, NT, 8])
        slot_of = sb("slot_of", [P, NT, 8])
        count = sb("count", [P, 8], I32)
        silu_warm = sb("silu_warm", [P, 1])
        with ExitStack() as mix:
            h_in = sb("h_in", [P, NT, 3072], scope=mix)
            qk = sb("qk", [HD, 4, 512], scope=mix)
            z = sb("z", [P, 4, 384], scope=mix)
            pt = sb("pt", [P, 4, 384], scope=mix)
            with ExitStack() as hyb_only:
                toep = sb("toep", [P, 6, S], scope=hyb_only)
            swa_bias = sb("swa_bias", [P, 6 * S], scope=mix)[:, 0:1280]
            o_tmp = sb("o_tmp", [P, NT, 2, P], scope=mix)
            with ExitStack() as early:
                pool_m = sb("pool_m", [P, NT, 4, S], scope=early)
                pool_t = sb("pool_t", [HD, 4, S], scope=early)
            zs = sb("zs", [P, 2, 384], scope=mix)
            es = sb("es", [P, 2, 384], scope=mix)
            sps = sb("sps", [P, 2, 384], scope=mix)
            zm = sb("zm", [P, 2, 384], scope=mix)
        with ExitStack() as ffn:
            sg = sb("sg", [P, 2 * S], scope=ffn)
            h_f = sb("h_f", [P, 2, 2 * S], scope=ffn)
            h_hi = sb("h_hi", [P, 2, 2, S], F32R, scope=ffn)
            h_lo = sb("h_lo", [P, 2, 2, S], F32R, scope=ffn)
            xn_hi = sb("xn_hi", [P, NT, D], F32R, scope=ffn)
            xn_lo = sb("xn_lo", [P, NT, D], F32R, scope=ffn)
            iota = sb("iota", [P, S], scope=ffn)
            perm = sb("perm", [P, NT, S], F32R, scope=ffn)
            perm_t = sb("perm_t", [P, NT, S], F32R, scope=ffn)
            ye_hi = sb("ye_hi", [P, NT, D], F32R, scope=ffn)
            ye_lo = sb("ye_lo", [P, NT, D], F32R, scope=ffn)
            odd_hi = sb("odd_hi", [P, KT, S], F32R, scope=ffn)
            odd_lo = sb("odd_lo", [P, KT, S], F32R, scope=ffn)
        rt = [z[:, 0:4, :].rearrange("p a b -> p (a b)")[:, 0:512], z[:, 0:4, :].rearrange("p a b -> p (a b)")[:, 512:1024],
              pt[:, 0:4, :].rearrange("p a b -> p (a b)")[:, 0:512], pt[:, 0:4, :].rearrange("p a b -> p (a b)")[:, 512:1024]]
        bank = [ctx.enter_context(nc.psum_tensor(f"bank{i}", [P, 512], F32)) for i in range(8)]

        ident = cst[:, C_ID:C_ID + P]
        tri = cst[:, C_TRI:C_TRI + P]
        ones = cst[:, C_ONE:C_ONE + P]
        flip8 = cst[:, C_FLIP:C_FLIP + P]

        loaded = [sem(f"raw_loaded{s}") for s in range(3)]
        hi_ready = [sem(f"hi_ready{s}") for s in range(3)]
        lo_ready = [sem(f"lo_ready{s}") for s in range(3)]
        used = [sem(f"unit_used{s}") for s in range(3)]
        gain_loaded = [sem(f"gain_loaded{i}") for i in range(3)]
        gain_used = sem("gain_used")
        cst_loaded = sem("cst_loaded")
        x_loaded = sem("x_loaded")
        names = ["swa_bias", "sinks", "pool_scale", "pool_w", "lam", "subg", "rel", "pos", "router", "pool_m",
                 "toep", "iota"]
        got = {n: sem(f"{n}_loaded") for n in names}
        rel_done, rel_stored = sem("rel_reversed"), sem("rel_stored")
        dchain, achain, pchain = sem("vector_chain"), sem("scalar_chain"), sem("gpsimd_chain")
        nat_ready = sem("natural_ready")
        turned = sem("turned")
        t_hi, t_lo = sem("t_hi"), sem("t_lo")
        proj_done, proj_ev = sem("proj_done"), sem("proj_evacuated")
        acc_done = sem("acc_done")
        var_ready, root_ready = sem("var_ready"), sem("root_ready")
        rope_done = sem("rope_done")
        qk_turned, qk_ready = sem("qk_turned"), sem("qk_ready")
        scored, z_read = sem("scored"), sem("z_read")
        nmx_ready, p_ready = sem("nmx_ready"), sem("p_ready")
        pt_done, pt_ready = sem("pt_done"), sem("pt_ready")
        pv_done, o_read = sem("pv_done"), sem("o_read")
        sp_log, sp_ready, zm_ready = sem("stick_log"), sem("stick_sp"), sem("stick_zm")
        c_done, arg_ready, w_ready = sem("stick_sums"), sem("stick_arg"), sem("stick_w")
        pool_done, pool_copied, pool_out = sem("pool_done"), sem("pool_copied"), sem("pool_out")
        act_done, h_mid, h_ready = sem("act_done"), sem("h_mid"), sem("h_ready")
        hh_ready, hl_ready = sem("hh_ready"), sem("hl_ready")
        lam_dot, lam_exp = sem("lam_dot"), sem("lam_exp")
        rope_arg, rope_sin = sem("rope_arg"), sem("rope_sin")
        router_hi_s, router_lo_s = sem("router_hi_ready"), sem("router_lo_ready")
        logits, gap, gap_exp, gates = sem("logits"), sem("gap"), sem("gap_exp"), sem("gates")
        ranked, counted = sem("ranked"), sem("counted")
        xn_hi_ready, xn_lo_ready = sem("xn_hi_ready"), sem("xn_lo_ready")
        perm_ready, perm_turned, perm_t_ready = sem("perm_ready"), sem("perm_turned"), sem("perm_t_ready")
        gathered, gather_copied = sem("gathered"), sem("gather_copied")
        ye_hi_ready, ye_lo_ready = sem("ye_hi_ready"), sem("ye_lo_ready")
        scattered, added = sem("scattered"), sem("added")
        h_turned = sem("h_turned")
        y_done, stored = sem("y_done"), sem("stored")

        w_in = [A["w_in"][0], A["w_in"][1], A["diff_w_in_2"][0], A["moba_w_in_2"][0], A["swa_w_in_2"][0],
                A["diff_w_in_2"][1]]
        w_out = [A["w_out"][0], A["w_out"][1], A["diff_w_out_2"][0], A["moba_w_out_2"][0], A["swa_w_out_2"][0],
                 A["diff_w_out_2"][1]]

        def as_k(t):
            return t[:, :].rearrange("p (k f) -> p k f", k=KT)

        def as_rows(t):
            return t[:, :].rearrange("p (k d) -> p k d", k=2)

        def head_cols(l, j):
            k = KIND[l]
            if k == HYB:
                return D_POOL + j * HD, D_POOL + D_CHUNK + j * HD, D_POOL + 2 * D_CHUNK + j * HD
            if k == DIFF:
                return j * HD, D + j * HD, 2 * D + (j // 2) * 2 * HD
            if k == MOBA:
                return j * HD, D + j * HD, 2 * D + j * HD
            return j * HD, D + (j // 8) * HD, D + 2 * HD + (j // 8) * HD

        def stick_cols(j):
            base = D_POOL + 3 * D_CHUNK
            return base + j * HD, base + D_SB + j * HD, base + 2 * D_SB + j * HD

        block = ctx.enter_context(nc.Block())

        @block.sync
        def _(sp):
            sp.dma_start(x[:], A["x"][0].rearrange("(t p) d -> p t d", p=P)).then_inc(x_loaded, 16)
            sp.dma_start(cst[:], A["cst"]).then_inc(cst_loaded, 16)

            def load(place, src, k):
                slot, turn = place
                if not isinstance(turn, int) or turn > 0:
                    sp.wait_ge(lo_ready[slot], turn * 2)
                sp.dma_start(raw[slot][:, :].rearrange("p (k f) -> p k f", k=k), src).then_inc(loaded[slot], 16)

            def cols(w, c):
                return w.rearrange("(k p) f -> p k f", p=P)[:, :, c]

            def rows(w, r):
                return w[r, :].rearrange("(k p) d -> p k d", p=P)

            gains = [A["g_mix"][0], A["ln1_g"][0], A["ln1_b"][0], A["ln2_g"][0], A["ln2_b"][0],
                     A["g_mix"][1], A["ln1_g"][1], A["ln1_b"][1], A["ln2_g"][1], A["ln2_b"][1]]
            for l in range(4):
                gains += [A["attn_norm_g_2"][l], A["mlp_norm_g_2"][l]]
            gains.append(A["final_norm_g_2"])
            next_gain = [0]

            def load_gains(n):
                for _ in range(n):
                    u = next_gain[0]
                    if u >= 3:
                        sp.wait_ge(gain_used, u - 2)
                    sp.dma_start(gain[u % 3][:], gains[u].partition_broadcast(P)).then_inc(gain_loaded[u % 3], 16)
                    next_gain[0] += 1

            def load_swiglu(l, wg, wu, wd, expert):
                g = groups(l)
                (sg_, tg), (su, tu), (sd, td) = PLAN[l][2]

                def up(w, i):
                    if expert:
                        return w[bass.ds(i // GE, 1), :, bass.ds((i % GE) * UC, UC)].rearrange(
                            "a (k p) f -> p (a k) f", p=P)
                    return w[:, bass.ds(i * UC, UC)].rearrange("(k p) f -> p k f", p=P)

                def down(i):
                    return wd[bass.ds(i * UC, UC), :].rearrange("(k p) d -> p k d", p=P)

                load((sg_, tg), up(wg, 0), KT)
                load((su, tu), up(wu, 0), KT)
                load((sd, td), down(0), 2)
                load((sg_, tg + 1), up(wg, 1), KT)
                load((su, tu + 1), up(wu, 1), KT)
                load_gains(3 if l == 1 else 2)
                with sp.Fori(1, g - 1) as i:
                    load((sg_, i + (tg + 1)), up(wg, i + 1), KT)
                    load((su, i + (tu + 1)), up(wu, i + 1), KT)
                    load((sd, i + td), down(i), 2)
                load((sd, td + g - 1), down(g - 1), 2)

            def load_mlp(l):
                g = groups(l)
                wu, wd = A["mlp_w_up_2"][l - 2], A["mlp_w_down_2"][l - 2]
                (s0, t0), (s1, t1), (sd, td) = PLAN[l][2]
                us, ut = (s0, s1), (t0, t1)

                def up(i, par, turn):
                    load((us[par], ut[par] + turn), wu[:, bass.ds(i * UC, UC)].rearrange("(k p) f -> p k f", p=P), KT)

                def down(i, ):
                    load((sd, i + td), wd[bass.ds(i * UC, UC), :].rearrange("(k p) d -> p k d", p=P), 2)

                up(0, 0, 0)
                up(1, 1, 0)
                down(0)
                up(2, 0, 1)
                load_gains(1)
                with sp.Fori(0, 6) as j:
                    up(j * 2 + 3, 1, j + 1)
                    down(j * 2 + 1)
                    up(j * 2 + 4, 0, j + 2)
                    down(j * 2 + 2)
                up(g - 1, 1, g // 2 - 1)
                down(g - 3)
                down(g - 2)
                down(g - 1)

            def small():
                sp.dma_start(rel_in[:], A["rel_bias"].rearrange("l h n -> (l h) n")).then_inc(got["rel"], 16)
                sp.dma_start(pool_m[:], A["pool_m"]).then_inc(got["pool_m"], 16)
                sp.dma_start(pool_w[:], A["pool_w"].rearrange("l g c d -> c l g d")).then_inc(got["pool_w"], 16)
                sp.dma_start(pool_scale[:], A["pool_scale"].partition_broadcast(P)).then_inc(got["pool_scale"], 16)
                sp.dma_start(pos_i[:], A["positions_2"][0].rearrange("(t p) -> p t", p=P),
                             allow_slow_non_contiguous=True).then_inc(got["pos"], 16)
                for i, n in enumerate(("diff_lam_q1_2", "diff_lam_k1_2", "diff_lam_q2_2", "diff_lam_k2_2")):
                    if i:
                        sp.wait_ge(got["lam"], 16 * i)
                    sp.dma_start(lam_in[:, i], A[n].partition_broadcast(P)).then_inc(got["lam"], 16)
                sp.dma_start(subg[:], A["diff_subln_g_2"].partition_broadcast(P)).then_inc(got["subg"], 16)
                sp.dma_start(router_w[:], A["moe_router"][0].rearrange("(k p) e -> p k e", p=P)).then_inc(
                    got["router"], 16)
                sp.dma_start(sinks[:], A["swa_sinks_2"][0].partition_broadcast(P)).then_inc(got["sinks"], 16)

            def load_toeplitz(l):
                sp.dma_start(toep[:], bass.AP(bias_scratch.tensor, l * 6 * REVW,
                                              [[1, P], [REVW, 6], [1, S]])).then_inc(got["toep"], 16)

            for l in range(NL):
                proj, outp, _ = PLAN[l]
                for c in range(NPROJ[KIND[l]]):
                    load(proj[c], cols(w_in[l], slice(c * UC, (c + 1) * UC)), KT)
                    if c == 2 and l == 0:
                        small()
                    if c == 4:
                        load_gains(3 if KIND[l] == HYB else 1)
                        if l == 2:
                            sp.wait_ge(nat_ready, 8)
                            sp.dma_start(swa_bias, A["swa_b_in_2"][0].partition_broadcast(P)).then_inc(
                                got["swa_bias"], 16)
                        if l == 1:
                            sp.dma_start(pool_m[:], A["pool_m"]).then_inc(got["pool_m"], 16)
                            load_toeplitz(1)
                if l == 0:
                    sp.wait_ge(rel_done, 2)
                    sp.dma_start(bias_scratch, rel_rev[:]).then_inc(rel_stored, 16)
                    sp.wait_ge(rel_stored, 16)
                    load_toeplitz(0)
                for o in range(4):
                    load(outp[o], rows(w_out[l], slice(o * UC, (o + 1) * UC)), 2)
                if l == 0:
                    load_swiglu(0, A["ffn_wg"][0], A["ffn_wu"][0], A["ffn_wd"][0], False)
                elif l == 1:
                    sp.wait_ge(nat_ready, 2 * 3 * l + 2)
                    sp.dma_start(iota[:], A["iota"]).then_inc(got["iota"], 16)
                    load_swiglu(1, A["moe_wg"][0], A["moe_wu"][0],
                                A["moe_wd"][0].rearrange("e f d -> (e f) d"), True)
                else:
                    load_mlp(l)
            for t in range(NT):
                sp.wait_ge(y_done, t + 1)
                sp.dma_start(out[0, t * P:(t + 1) * P, :], y[:, t]).then_inc(stored, 16)
            sp.wait_ge(stored, 16 * NT)

        @block.gpsimd
        def _(pool):
            pool.wait_ge(cst_loaded, 16)
            done = [0]

            def roots(n):
                for _ in range(n):
                    r = done[0]
                    w = ROOTS[r]
                    pool.wait_ge(var_ready, r + 1)
                    pool.tensor_tensor(rstd[:, r % 8, 0:w], var[:, r % 8, 0:w], cst[:, C_HALF:C_HALF + w],
                                       ALU.pow).then_inc(root_ready, 1)
                    done[0] += 1

            def stick_masks(l):
                for h in range(NSTICK[KIND[l]]):
                    b = STICK0[l] + h
                    pool.wait_ge(z_read, HEAD0[l] + NSOFT[KIND[l]] + h + 1)
                    if b >= 2:
                        pool.wait_ge(pv_done, SOFT0[l] + NSOFT[KIND[l]] + b - 1)
                    pool.tensor_tensor(zm[:, b % 2], zs[:, b % 2], cst[:, C_STRICTNEG:C_STRICTNEG + 384],
                                       ALU.add).then_inc(zm_ready, 1)

            for l in range(NL):
                stick_masks(l)
                roots(5 if KIND[l] == HYB else 5 if KIND[l] == DIFF else 4)
            roots(2)

        @block.tensor
        def _(pe):
            pe.wait_ge(cst_loaded, 16)

            def to_t(q, src):
                for t in range(NT):
                    if q == 0:
                        pe.wait_ge(x_loaded, 16)
                    else:
                        pe.wait_ge(nat_ready, 2 * (q - 1) + t + 1)
                    for kq in range(2):
                        for k in range(4):
                            mm = pe.transpose(bank[2 * t + kq][:, k * P:(k + 1) * P],
                                              src[:, t, (4 * kq + k) * P:(4 * kq + k + 1) * P], ident)
                        mm.then_inc(turned, 1)

            def t_ready(q):
                pe.wait_ge(t_lo, 4 * (q + 1))

            def unit_ready(place):
                slot, turn = place
                pe.wait_ge(lo_ready[slot], turn * 2 + 2)

            def project(l):
                for c in range(NPROJ[KIND[l]]):
                    slot, turn = PLAN[l][0][c]
                    unit_ready(PLAN[l][0][c])
                    n = PROJ0[l] + c
                    if c >= 4:
                        pe.wait_ge(proj_ev, n - 3)
                    hi, lo = as_k(whi[slot]), as_k(wlo[slot])
                    for t in range(NT):
                        for k in range(KT):
                            for i, (a, b) in enumerate(((xt_hi, hi), (xt_lo, hi), (xt_hi, lo))):
                                mm = pe.matmul(bank[4 + c % 4][:, t * UC:(t + 1) * UC],
                                               a[:, k, t * P:(t + 1) * P], b[:, k, :],
                                               start=(k == 0 and i == 0), stop=(k == KT - 1 and i == 2))
                    mm.then_inc(used[slot], 1)

            def down(place, at, a_hi, a_lo, first, last):
                slot, _ = place
                hi, lo = as_rows(whi[slot]), as_rows(wlo[slot])
                for t in range(NT):
                    for kk in range(2):
                        for i, (a, b) in enumerate(((a_hi, hi), (a_lo, hi), (a_hi, lo))):
                            for half in range(2):
                                mm = pe.matmul(bank[4 + 2 * t + half][:, :], a[:, at + kk, t * P:(t + 1) * P],
                                               b[:, kk, half * 512:(half + 1) * 512],
                                               start=first and kk == 0 and i == 0, stop=last and kk == 1 and i == 2)
                    if last and t == 0:
                        mm.then_inc(acc_done, 1)
                return mm

            def out_project(l):
                for o in range(4):
                    unit_ready(PLAN[l][1][o])
                    mm = down(PLAN[l][1][o], 2 * o, xt_hi, xt_lo, o == 0, o == 3)
                    mm.then_inc(used[PLAN[l][1][o][0]], 1)

            def up(place, b):
                slot, _ = place
                hi, lo = as_k(whi[slot]), as_k(wlo[slot])
                for f in range(2):
                    for k in range(KT):
                        for i, (a, w) in enumerate(((xt_hi, hi), (xt_lo, hi), (xt_hi, lo))):
                            mm = pe.matmul(bank[b][:, f * S:(f + 1) * S], w[:, k, f * P:(f + 1) * P], a[:, k, :],
                                           start=(k == 0 and i == 0), stop=(k == KT - 1 and i == 2))
                mm.then_inc(used[slot], 1)

            def router():
                pe.wait_ge(router_lo_s, 1)
                for t in range(NT):
                    for k in range(KT):
                        for i, (a, w) in enumerate(((xt_hi, router_hi), (xt_lo, router_hi), (xt_hi, router_lo),
                                                    (xt_lo, router_lo))):
                            mm = pe.matmul(bank[2][:, t * 8:(t + 1) * 8], a[:, k, t * P:(t + 1) * P], w[:, k, :],
                                           start=(k == 0 and i == 0), stop=(k == KT - 1 and i == 3))
                mm.then_inc(logits, 1)

            def rank():
                before = cst[:, C_STRICT:C_STRICT + P]
                pe.wait_ge(gates, 1)
                o = bank[3]
                pe.matmul(o[:, 0:8], before, chosen[:, 0, :], start=True, stop=True)
                pe.matmul(o[:, 8:16], ones, chosen[:, 0, :], start=True, stop=False)
                pe.matmul(o[:, 8:16], before, chosen[:, 1, :], start=False, stop=True)
                pe.matmul(o[:, 16:24], ones, chosen[:, 0, :], start=True, stop=False)
                pe.matmul(o[:, 16:24], ones, chosen[:, 1, :], start=False, stop=True).then_inc(ranked, 1)

            def gather(e, g):
                pe.wait_ge(perm_ready, e + 1)
                if g:
                    pe.wait_ge(gather_copied, e * 8 + g)
                src = (xn_hi, xn_lo)[g // 4]
                for k in range(2):
                    at = (2 * (g % 4) + k) * P
                    for t in range(NT):
                        mm = pe.matmul(bank[3][:, k * S:(k + 1) * S], src[:, t, at:at + P], perm[:, t, :],
                                       start=(t == 0), stop=(t == 1))
                mm.then_inc(gathered, 1)

            def turn_perm(e):
                pe.wait_ge(added, e * 4 + 4)
                for st in range(NT):
                    for t in range(NT):
                        mm = pe.transpose(bank[3][:, st * S + t * P:st * S + (t + 1) * P],
                                          perm[:, t, st * P:(st + 1) * P].bitcast(F32), ident)
                mm.then_inc(perm_turned, 1)

            def scatter(e, wide):
                pe.wait_ge(ye_lo_ready, e * 4 + 4)
                pe.wait_ge(gather_copied, e * 8 + 16)
                for t in range(NT):
                    for half in range(2):
                        if t:
                            pe.wait_ge(added, e * 4 + (5 + half))
                        for st in range(2 if wide else 1):
                            for i, part in enumerate((ye_hi, ye_lo)):
                                mm = pe.matmul(bank[2 + half][:, :], perm_t[:, st, t * P:(t + 1) * P],
                                               part[:, st, half * 512:(half + 1) * 512],
                                               start=(st == 0 and i == 0), stop=(st == wide and i == 1))
                        mm.then_inc(scattered, 1)

            def rise(e_odd, wide, place, b):
                x_hi, x_lo = (odd_hi, odd_lo) if e_odd else (xt_hi, xt_lo)
                unit_ready(place)
                slot = place[0]
                hi, lo = as_k(whi[slot]), as_k(wlo[slot])
                for t in range(2 if wide else 1):
                    for k in range(KT):
                        for i, (a, w) in enumerate(((x_hi, hi), (x_lo, hi), (x_hi, lo))):
                            mm = pe.matmul(bank[b][:, t * UC:(t + 1) * UC], a[:, k, t * P:(t + 1) * P],
                                           w[:, k, :], start=(k == 0 and i == 0), stop=(k == KT - 1 and i == 2))
                mm.then_inc(used[slot], 1)

            def rise_by(n_tokens, odd, place, b):
                with pe.If(n_tokens < P + 1):
                    rise(odd, False, place, b)
                with pe.Else():
                    rise(odd, True, place, b)

            def expert(e, odd, wide, n_next):
                hb = GRP0[1]
                (sg_, tg), (su, tu), (sd, td) = PLAN[1][2]
                tiles = 2 if wide else 1

                def turn_hidden(n):
                    pe.wait_ge(h_mid, n + (hb + 1))
                    for f in range(2):
                        for t in range(tiles):
                            mm = pe.transpose(bank[2][:, f * S + t * P:f * S + (t + 1) * P],
                                              h_f[:, 0, t * UC + f * P:t * UC + (f + 1) * P], ident)
                    mm.then_inc(h_turned, 1)

                def fold(n, first=False, stop=False):
                    unit_ready((sd, n + td))
                    pe.wait_ge(hl_ready, n + (hb + 1))
                    hi, lo = as_rows(whi[sd]), as_rows(wlo[sd])
                    for t in range(tiles):
                        for kk in range(2):
                            for i, (a, w) in enumerate(((h_hi, hi), (h_lo, hi), (h_hi, lo))):
                                for half in range(2):
                                    mm = pe.matmul(bank[4 + 2 * t + half][:, :], a[:, 0, kk, t * P:(t + 1) * P],
                                                   w[:, kk, half * 512:(half + 1) * 512],
                                                   start=first and kk == 0 and i == 0,
                                                   stop=stop and kk == 1 and i == 2)
                    mm.then_inc(used[sd], 1)

                def gate(n):
                    pe.wait_ge(act_done, n + hb)
                    rise(odd, wide, (sg_, n + tg), 0)

                n0 = e * GE
                pe.wait_ge(added, e * 4 + 3)
                turn_hidden(n0)
                rise(odd, wide, (su, n0 + (tu + 1)), 1)
                fold(n0, first=True)
                for i in range(2, 7):
                    gate(n0 + i)
                    turn_hidden(n0 + (i - 1))
                    if i == 2:
                        turn_perm(e)
                    else:
                        if i == 3:
                            pe.wait_ge(perm_t_ready, e + 1)
                        gather(e + 1, 2 * (i - 3))
                    rise(odd, wide, (su, n0 + (tu + i)), 1)
                    fold(n0 + (i - 1))
                    if i > 2:
                        gather(e + 1, 2 * (i - 3) + 1)
                with pe.Fori(7, GE) as i:
                    gate(n0 + i)
                    turn_hidden(n0 + i - 1)
                    rise(odd, wide, (su, n0 + i + tu), 1)
                    fold(n0 + i - 1)
                n1 = n0 + GE
                if n_next is None:
                    turn_hidden(n1 - 1)
                    fold(n1 - 1, stop=True)
                else:
                    pe.wait_ge(gather_copied, e * 8 + 16)
                    pe.wait_ge(act_done, n1 + hb)
                    rise_by(n_next, not odd, (sg_, n1 + tg), 0)
                    turn_hidden(n1 - 1)
                    rise_by(n_next, not odd, (su, n1 + tu), 1)
                    fold(n1 - 1, stop=True)
                    pe.wait_ge(act_done, n1 + (hb + 1))
                    rise_by(n_next, not odd, (sg_, n1 + (tg + 1)), 0)
                scatter(e, wide)

            def moe():
                router()
                rank()
                pe.wait_ge(xn_lo_ready, 1)
                pe.wait_ge(counted, 1)
                for g in range(8):
                    gather(0, g)
                hb = GRP0[1]
                (sg_, tg), (su, tu), _ = PLAN[1][2]

                def tokens_of(e):
                    return pe.value_load(count[0:1, bass.ds(e, 1)], min_val=0, max_val=S)

                def either(e, odd, last=False):
                    n = tokens_of(e)
                    n_next = None if last else tokens_of(e + 1)
                    with pe.If(n < P + 1):
                        expert(e, odd, False, n_next)
                    with pe.Else():
                        expert(e, odd, True, n_next)

                n = tokens_of(0)
                pe.wait_ge(gather_copied, 8)
                rise_by(n, False, (sg_, tg), 0)
                rise_by(n, False, (su, tu), 1)
                pe.wait_ge(act_done, hb + 1)
                rise_by(n, False, (sg_, tg + 1), 0)
                with pe.Fori(0, N_EXP // 2 - 1) as pair:
                    for odd in range(2):
                        either(pair * 2 + odd, odd)
                either(N_EXP - 2, 0)
                either(N_EXP - 1, 1, last=True)

            def swiglu(l):
                g, hb = groups(l), GRP0[l]
                (sg_, tg), (su, tu), (sd, td) = PLAN[l][2]

                def pair(i):
                    unit_ready((sg_, i + tg))
                    if not isinstance(i, int) or i > 0:
                        pe.wait_ge(h_mid, i + hb)
                    up((sg_, None), 0)
                    unit_ready((su, i + tu))
                    up((su, None), 1)

                def fold(i, first=False, last=False):
                    unit_ready((sd, i + td))
                    pe.wait_ge(hl_ready, i + (hb + 1))
                    down((sd, None), 0, h_hi[:, 0], h_lo[:, 0], first, last).then_inc(used[sd], 1)

                pair(0)
                pair(1)
                fold(0, first=True)
                with pe.Fori(2, g) as i:
                    pair(i)
                    fold(i - 1)
                fold(g - 1, last=True)

            def mlp(l):
                g, hb = groups(l), GRP0[l]
                (s0, t0), (s1, t1), (sd, td) = PLAN[l][2]
                us, ut = (s0, s1), (t0, t1)

                def rise(par, turn, i):
                    unit_ready((us[par], turn + ut[par]))
                    if not isinstance(i, int) or i >= 2:
                        pe.wait_ge(act_done, i + (hb - 1))
                    up((us[par], None), par)

                def fold(par, i, first=False, last=False):
                    unit_ready((sd, i + td))
                    pe.wait_ge(hl_ready, i + (hb + 1))
                    down((sd, None), 0, h_hi[:, par], h_lo[:, par], first, last).then_inc(used[sd], 1)

                rise(0, 0, 0)
                rise(1, 0, 1)
                fold(0, 0, first=True)
                with pe.Fori(1, g // 2) as j:
                    rise(0, j, j * 2)
                    fold(1, j * 2 - 1)
                    rise(1, j, j * 2 + 1)
                    fold(0, j * 2)
                fold(1, g - 1, last=True)

            def turn_heads(l, j, qcol, kcol, g):
                if g >= 2:
                    pe.wait_ge(qk_ready, g - 1)
                for i, col in enumerate((qcol, kcol)):
                    for t in range(NT):
                        mm = pe.transpose(bank[2 + g % 2][0:HD, (2 * i + t) * P:(2 * i + t + 1) * P],
                                          h_in[:, t, col:col + HD], ident)
                mm.then_inc(qk_turned, 1)

            def soft_heads(l):
                kind = KIND[l]
                n, dv, og = NSOFT[kind], VW[kind], OGRP[kind]
                for i in range(n + 4):
                    if i < n:
                        turn_heads(l, i, *head_cols(l, i)[0:2], HEAD0[l] + i)
                    j = i - 1
                    if 0 <= j < n:
                        g = HEAD0[l] + j
                        pe.wait_ge(qk_ready, g + 1)
                        if g >= 2:
                            pe.wait_ge(z_read, g - 1)
                        b = bank[g % 2]
                        q = qk[:, g % 4]
                        plain = kind != HYB
                        pe.matmul(b[:, 0:P], q[:, 0:P], q[:, 2 * P:3 * P], start=True, stop=plain)
                        if not plain:
                            pe.wait_ge(got["toep"], 16 * (l + 1))
                            pe.matmul(b[:, 0:P], flip8, toep[:, j, P:2 * P], start=False, stop=True)
                        mm = pe.matmul(b[:, P:3 * P], q[:, P:2 * P], q[:, 2 * P:4 * P], start=True, stop=plain)
                        if not plain:
                            mm = pe.matmul(b[:, P:3 * P], flip8, toep[:, j, :], start=False, stop=True)
                        mm.then_inc(scored, 1)
                    j = i - 3
                    if 0 <= j < n:
                        s = SOFT0[l] + j
                        pe.wait_ge(p_ready, s + 1)
                        if s >= 2:
                            pe.wait_ge(pt_ready, s - 1)
                        for m in range(3):
                            mm = pe.transpose(bank[4 + s % 2][:, m * P:(m + 1) * P],
                                              z[:, s % 4, m * P:(m + 1) * P], ident)
                        mm.then_inc(pt_done, 1)
                    j = i - 4
                    if 0 <= j < n:
                        s = SOFT0[l] + j
                        pe.wait_ge(pt_ready, s + 1)
                        values(l, j, pt[:, s % 4], dv, og, j, head_cols(l, j)[2])

            def values(l, j, w, dv, og, order, vcol):
                o = OG0[l] + order // og
                if order % og == 0 and o >= 2:
                    pe.wait_ge(o_read, o - 1)
                b = bank[6 + o % 2]
                at = (order % og) * dv
                half = og * dv
                pe.matmul(b[:, at:at + dv], w[:, 0:P], h_in[:, 0, vcol:vcol + dv], start=True, stop=True)
                pe.matmul(b[:, half + at:half + at + dv], w[:, P:2 * P], h_in[:, 0, vcol:vcol + dv],
                          start=True, stop=False)
                pe.matmul(b[:, half + at:half + at + dv], w[:, 2 * P:3 * P], h_in[:, 1, vcol:vcol + dv],
                          start=False, stop=True).then_inc(pv_done, 1)

            def pool_mix(l):
                pe.wait_ge(got["pool_m"], 16 * (l + 1))
                pe.wait_ge(got["pool_w"], 16)
                for gp in range(2):
                    for g in range(2):
                        c = (2 * gp + g) * HD
                        for t in range(NT):
                            mm = pe.matmul(bank[4 + gp][0:HD, g * S:(g + 1) * S], h_in[:, t, c:c + HD],
                                           pool_m[:, t, 2 * gp + g, :], start=(t == 0), stop=(t == NT - 1))
                    mm.then_inc(pool_done, 1)
                pe.wait_ge(pool_copied, 2 * l + 2)
                for t in range(NT):
                    for g in range(4):
                        mm = pe.matmul(bank[6][:, t * D_POOL + g * HD:t * D_POOL + (g + 1) * HD],
                                       pool_t[:, g, t * P:(t + 1) * P], pool_w[:, l, g, :], start=True, stop=True)
                mm.then_inc(pool_out, 1)

            def stick_heads(l):
                n = NSTICK[HYB]
                for i in range(n + 5):
                    if i < n:
                        turn_heads(l, i, *stick_cols(i)[0:2], HEAD0[l] + NSOFT[HYB] + i)
                    h = i - 1
                    if 0 <= h < n:
                        g = HEAD0[l] + NSOFT[HYB] + h
                        pe.wait_ge(qk_ready, g + 1)
                        pe.wait_ge(z_read, g - 1)
                        q = qk[:, g % 4]
                        pe.matmul(bank[g % 2][:, 0:2 * P], q[:, 2 * P:3 * P], q[:, 0:2 * P], start=True, stop=True)
                        pe.matmul(bank[g % 2][:, 2 * P:3 * P], q[:, 3 * P:4 * P], q[:, P:2 * P],
                                  start=True, stop=True).then_inc(scored, 1)
                    h = i - 3
                    if 0 <= h < n:
                        b = STICK0[l] + h
                        pe.wait_ge(sp_ready, b + 1)
                        if h >= 2:
                            pe.wait_ge(arg_ready, b - 1)
                        o = bank[4 + b % 2]
                        pe.matmul(o[:, 0:2 * P], tri, sps[:, b % 2, 0:2 * P], start=True, stop=False,
                                  skip_group_check=True)
                        pe.matmul(o[:, P:2 * P], ones, sps[:, b % 2, 2 * P:3 * P], start=False, stop=True,
                                  skip_group_check=True)
                        pe.matmul(o[:, 2 * P:3 * P], tri, sps[:, b % 2, 2 * P:3 * P], start=True,
                                  stop=True).then_inc(c_done, 1)
                    h = i - 5
                    if 0 <= h < n:
                        b = STICK0[l] + h
                        pe.wait_ge(w_ready, b + 1)
                        values(l, h, zm[:, b % 2], HD, OGRP[HYB], NSOFT[HYB] + h, stick_cols(h)[2])

            for l in range(NL):
                to_t(3 * l, x if KIND[l] == HYB else y)
                t_ready(3 * l)
                project(l)
                pe.wait_ge(proj_ev, PROJ0[l + 1])
                if KIND[l] == HYB:
                    pool_mix(l)
                else:
                    pe.wait_ge(rope_done, l - 1)
                soft_heads(l)
                if KIND[l] == HYB:
                    stick_heads(l)
                to_t(3 * l + 1, y)
                t_ready(3 * l + 1)
                out_project(l)
                to_t(3 * l + 2, x if KIND[l] == HYB else y)
                t_ready(3 * l + 2)
                if l == 1:
                    moe()
                else:
                    (swiglu if KIND[l] == HYB else mlp)(l)

        @block.scalar
        def _(act):
            chain = [0]

            def link(ins):
                chain[0] += 1
                ins.then_inc(achain, 1)
                act.wait_ge(achain, chain[0])

            def hi(place):
                slot, turn = place
                if not isinstance(turn, int) or turn > 0:
                    act.wait_ge(used[slot], turn)
                act.wait_ge(loaded[slot], turn * 16 + 16)
                for half in range(2):
                    act.activation(whi[slot][:, half * 1024:(half + 1) * 1024], raw[slot][:, half * 1024:(half + 1) * 1024],
                                   ACT.Copy).then_inc(hi_ready[slot], 1)

            def to_t(q):
                for n in range(4):
                    act.wait_ge(turned, 4 * q + n + 1)
                    t, kq = divmod(n, 2)
                    act.activation(xt_hi[:, 4 * kq:4 * kq + 4, t * P:(t + 1) * P],
                                   bank[n][:, :].rearrange("p (k s) -> p k s", k=4), ACT.Copy).then_inc(t_hi, 1)

            def project(l):
                proj = PLAN[l][0]
                for c in range(len(proj)):
                    if KIND[l] != SWA:
                        act.wait_ge(used[proj[c][0]], proj[c][1] + 1)
                        act.activation(h_in[:, :, c * UC:(c + 1) * UC],
                                       bank[4 + c % 4][:, :].rearrange("p (t c) -> p t c", t=NT),
                                       ACT.Copy).then_inc(proj_ev, 1)
                    if c + 3 < len(proj):
                        hi(proj[c + 3])

            def copy_qk(g):
                act.wait_ge(qk_turned, g + 1)
                if g >= 4:
                    act.wait_ge(scored, g - 3)
                act.activation(qk[:, g % 4], bank[2 + g % 2][0:HD, :], ACT.Copy).then_inc(qk_ready, 1)

            def soft_heads(l):
                kind = KIND[l]
                n = NSOFT[kind]
                for i in range(n + 2):
                    if i < n:
                        copy_qk(HEAD0[l] + i)
                    j = i - 2
                    if 0 <= j < n:
                        s = SOFT0[l] + j
                        act.wait_ge(nmx_ready, s + 1)
                        ins = act.activation(z[:, s % 4, 0:P], z[:, s % 4, 0:P], ACT.Exp, bias=nmx[:, 0, j:j + 1],
                                             accum_out=sums[:, 0, j:j + 1])
                        ins = act.activation(z[:, s % 4, P:3 * P], z[:, s % 4, P:3 * P], ACT.Exp,
                                             bias=nmx[:, 1, j:j + 1], accum_out=sums[:, 1, j:j + 1])
                        if kind == SWA:
                            ins = act.activation(esink[:, :, j], nmx[:, :, j], ACT.Exp, bias=sinks[:, j:j + 1])
                        ins.then_inc(p_ready, 1)
                    if i in (1, 3, 5):
                        hi(PLAN[l][1][i // 2])

            def stick_heads(l):
                n = NSTICK[HYB]
                for i in range(n + 4):
                    if i < n:
                        copy_qk(HEAD0[l] + NSOFT[HYB] + i)
                    h = i - 2
                    if 0 <= h < n:
                        b = STICK0[l] + h
                        e = es[:, b % 2]
                        act.wait_ge(z_read, HEAD0[l] + NSOFT[HYB] + h + 1)
                        if h >= 2:
                            act.wait_ge(sp_ready, b - 1)
                        link(act.activation(e, zs[:, b % 2], ACT.Abs))
                        link(act.activation(e, e, ACT.Exp, scale=-1.0))
                        act.activation(e, e, ACT.Ln, bias=cst[:, C_ONECOL:C_ONECOL + 1]).then_inc(sp_log, 1)
                    h = i - 4
                    if 0 <= h < n:
                        b = STICK0[l] + h
                        act.wait_ge(arg_ready, b + 1)
                        act.activation(zm[:, b % 2], zm[:, b % 2], ACT.Exp).then_inc(w_ready, 1)

            def hidden_hi(par, i, hb, sd, td, back):
                act.wait_ge(h_mid, i + (hb + 1))
                if not isinstance(i, int) or i >= back:
                    act.wait_ge(used[sd], i + (td + 1 - back))
                act.activation(h_hi[:, par], h_f[:, par, :].rearrange("p (f s) -> p f s", f=2), ACT.Copy).then_inc(hh_ready, 1)

            def swiglu(l):
                g, hb = groups(l), GRP0[l]
                (sg_, tg), (su, tu), (sd, td) = PLAN[l][2]

                def silu(i):
                    act.wait_ge(used[su], i + (tu + 1))
                    if not isinstance(i, int) or i > 0:
                        act.wait_ge(h_mid, i + hb)
                    act.activation(sg[:], bank[0][:, :], ACT.Silu).then_inc(act_done, 1)

                hi((sg_, tg + 1))
                silu(0)
                hi((su, tu + 1))
                hidden_hi(0, 0, hb, sd, td, 1)
                with act.Fori(1, g - 1) as i:
                    hi((sg_, i + (tg + 1)))
                    silu(i)
                    hi((su, i + (tu + 1)))
                    hidden_hi(0, i, hb, sd, td, 1)
                    hi((sd, i + td))
                silu(g - 1)
                hidden_hi(0, g - 1, hb, sd, td, 1)
                hi((sd, td + g - 1))

            def moe():
                hb = GRP0[1]
                (sg_, tg), (su, tu), (sd, td) = PLAN[1][2]

                def take_tokens(e, odd, g):
                    xt = (odd_hi, odd_lo)[g // 4] if odd else (xt_hi, xt_lo)[g // 4]
                    act.wait_ge(gathered, e * 8 + (g + 1))
                    act.activation(xt[:, 2 * (g % 4):2 * (g % 4) + 2, :],
                                   bank[3][:, :].rearrange("p (k s) -> p k s", k=2), ACT.Copy).then_inc(
                        gather_copied, 1)

                def take_perm(e):
                    act.wait_ge(perm_turned, e + 1)
                    act.activation(perm_t[:], bank[3][:, :].rearrange("p (a s) -> p a s", a=2), ACT.Copy).then_inc(
                        perm_t_ready, 1)

                def group(n, between=None, before_down=None, after=None, last=False):
                    if not last:
                        hi((sg_, n + (tg + 1)))
                    act.wait_ge(used[sg_], n + (tg + 1))
                    act.wait_ge(h_mid, n + hb)
                    act.activation(sg[:], bank[0][:, :], ACT.Silu).then_inc(act_done, 1)
                    if between is not None:
                        between()
                    if not last:
                        hi((su, n + (tu + 1)))
                    if before_down is not None:
                        before_down()
                    hi((sd, n + td))
                    if after is not None:
                        after()
                    act.wait_ge(h_turned, n + 1)
                    act.activation(h_hi[:, 0], bank[2][:, :].rearrange("p (f s) -> p f s", f=2), ACT.Copy).then_inc(
                        hh_ready, 1)

                def give_result(e):
                    act.wait_ge(used[sd], e * GE + (td + GE))
                    for b in range(4):
                        act.activation(ye_hi[:, b // 2, (b % 2) * 512:(b % 2 + 1) * 512], bank[4 + b][:, :],
                                       ACT.Copy).then_inc(ye_hi_ready, 1)

                def expert(e, odd, last=False):
                    n0 = e * GE
                    group(n0 + 1)
                    group(n0 + 2, between=lambda: take_perm(e))
                    for i in range(3, 7):
                        group(n0 + i, between=lambda: take_tokens(e + 1, not odd, 2 * (i - 3)),
                              after=lambda: take_tokens(e + 1, not odd, 2 * (i - 3) + 1))
                    with act.Fori(7, GE - last) as i:
                        group(n0 + i)
                    if last:
                        group(n0 + GE - 1, last=True)
                        give_result(e)
                    else:
                        group(n0 + GE, before_down=lambda: give_result(e))

                act.wait_ge(gates, 1)
                act.activation(silu_warm[:], topf[:, 0, 3:4], ACT.Silu)
                for g in range(8):
                    take_tokens(0, False, g)
                group(0)
                with act.Fori(0, N_EXP // 2 - 1) as pair:
                    expert(pair * 2, False)
                    expert(pair * 2 + 1, True)
                expert(N_EXP - 2, False)
                expert(N_EXP - 1, True, last=True)

            def mlp(l):
                g, hb = groups(l), GRP0[l]
                (s0, t0), (s1, t1), (sd, td) = PLAN[l][2]
                us, ut = (s0, s1), (t0, t1)

                def relu(par, turn, i):
                    act.wait_ge(used[us[par]], turn + (ut[par] + 1))
                    if not isinstance(i, int) or i > 0:
                        act.wait_ge(h_mid, i + hb)
                    act.activation(sg[:], bank[par][:, :], ACT.Relu).then_inc(act_done, 1)

                relu(0, 0, 0)
                hi((s0, t0 + 1))
                hidden_hi(0, 0, hb, sd, td, 2)
                with act.Fori(0, 6) as j:
                    relu(1, j, j * 2 + 1)
                    hi((s1, j + (t1 + 1)))
                    hidden_hi(1, j * 2 + 1, hb, sd, td, 2)
                    hi((sd, j * 2 + (td + 1)))
                    relu(0, j + 1, j * 2 + 2)
                    hi((s0, j + (t0 + 2)))
                    hidden_hi(0, j * 2 + 2, hb, sd, td, 2)
                    hi((sd, j * 2 + (td + 2)))
                for i in range(g - 3, g):
                    relu(i % 2, i // 2, i)
                    if i == g - 3:
                        hi((s1, t1 + g // 2 - 1))
                    hidden_hi(i % 2, i, hb, sd, td, 2)
                    hi((sd, td + i))

            def setup():
                act.wait_ge(got["router"], 16)
                act.activation(router_hi[:], router_w[:], ACT.Copy).then_inc(router_hi_s, 1)
                act.wait_ge(lam_dot, 1)
                act.activation(lam[:, 4:8], lam[:, 0:4], ACT.Exp).then_inc(lam_exp, 1)
                act.wait_ge(rope_arg, 1)
                act.activation(cos_sin[:], rope_f[:, 4:6], ACT.Sin).then_inc(rope_sin, 1)

            for l in range(NL):
                proj, outp, first = PLAN[l]
                if l == 0:
                    for c in range(2):
                        hi(proj[c])
                to_t(3 * l)
                hi(proj[2])
                project(l)
                if l == 0:
                    setup()
                if KIND[l] == HYB:
                    for gp in range(2):
                        act.wait_ge(pool_done, 2 * l + gp + 1)
                        act.activation(pool_t[:, 2 * gp:2 * gp + 2, :],
                                       bank[4 + gp][0:HD, :].rearrange("p (g s) -> p g s", g=2),
                                       ACT.Copy).then_inc(pool_copied, 1)
                soft_heads(l)
                if KIND[l] == HYB:
                    stick_heads(l)
                to_t(3 * l + 1)
                hi(outp[3])
                for i in range(2):
                    hi(first[i])
                if l == 1:
                    act.wait_ge(nat_ready, 2 * (3 * l + 1) + 2)
                    for t in range(NT):
                        ins = act.activation(xn_hi[:, t], x[:, t], ACT.Copy)
                    ins.then_inc(xn_hi_ready, 1)
                to_t(3 * l + 2)
                if l != 1:
                    hi(first[2])
                    (swiglu if KIND[l] == HYB else mlp)(l)
                else:
                    act.wait_ge(gap, 1)
                    act.activation(topf[:, :, 4:5], topf[:, :, 3:4], ACT.Exp).then_inc(gap_exp, 1)
                    moe()
                if l + 1 < NL:
                    for c in range(2):
                        hi(PLAN[l + 1][0][c])

        @block.vector
        def _(dve):
            chain = [0]
            asked = [0]
            gains_at = [0]

            def link(ins):
                chain[0] += 1
                ins.then_inc(dchain, 1)
                dve.wait_ge(dchain, chain[0])

            def lo(place):
                slot, turn = place
                for half in range(2):
                    h = slice(half * 1024, (half + 1) * 1024)
                    dve.wait_ge(hi_ready[slot], turn * 2 + half + 1)
                    dve.tensor_tensor(wlo[slot][:, h], raw[slot][:, h], whi[slot][:, h].bitcast(F32),
                                      ALU.subtract).then_inc(lo_ready[slot], 1)

            def to_t(q):
                for n in range(4):
                    dve.wait_ge(t_hi, 4 * q + n + 1)
                    t, kq = divmod(n, 2)
                    dve.tensor_tensor(xt_lo[:, 4 * kq:4 * kq + 4, t * P:(t + 1) * P],
                                      bank[n][:, :].rearrange("p (k s) -> p k s", k=4),
                                      xt_hi[:, 4 * kq:4 * kq + 4, t * P:(t + 1) * P].bitcast(F32),
                                      ALU.subtract).then_inc(t_lo, 1)

            def ask_root(src, scale, eps, w):
                r = asked[0]
                asked[0] += 1
                dve.tensor_scalar(var[:, r % 8, 0:w], src, scale, eps, ALU.mult, ALU.add).then_inc(var_ready, 1)
                return r

            def root(r):
                dve.wait_ge(root_ready, r + 1)
                return rstd[:, r % 8]

            def next_gain():
                u = gains_at[0]
                gains_at[0] += 1
                dve.wait_ge(gain_loaded[u % 3], 16 * (u // 3 + 1))
                return gain[u % 3]

            def acc_ready(acc, t):
                if t == 0:
                    dve.wait_ge(acc_done, acc + 1 - (acc > 3))
                else:
                    slot, turn = LAST_UNIT[acc]
                    dve.wait_ge(used[slot], turn + 1)

            def residual_norm(acc, to_turn=True):
                asks = []
                g, b = next_gain(), next_gain()
                for t in range(NT):
                    if acc != 3:
                        acc_ready(acc, t)
                    for half in range(2):
                        c = slice(half * 512, (half + 1) * 512)
                        ins = dve.scalar_tensor_tensor(out=x[:, t, c], in0=x[:, t, c], scalar=ALPHA,
                                                       in1=y[:, t, c] if acc == 3 else bank[4 + 2 * t + half][:, :],
                                                       op0=ALU.mult, op1=ALU.add)
                    link(ins)
                    for half in range(2):
                        ins = dve.bn_stats(stats[:, t, half], x[:, t, half * 512:(half + 1) * 512])
                    link(ins)
                    link(dve.bn_aggr(mv[:, t], stats[:, t]))
                    asks.append(ask_root(mv[:, t, 1:2], 1.0, LN_EPS, 1))
                for t in range(NT):
                    r = root(asks[t])
                    link(dve.tensor_scalar(x[:, t], x[:, t], mv[:, t, 0:1], r[:, 0:1], ALU.subtract, ALU.mult))
                    link(dve.tensor_tensor(x[:, t], x[:, t], g[:], ALU.mult))
                    ins = dve.tensor_tensor(x[:, t], x[:, t], b[:], ALU.add)
                    if to_turn:
                        ins.then_inc(nat_ready, 1)
                if to_turn:
                    nat[0] += 2
                    dve.wait_ge(nat_ready, nat[0])
                else:
                    link(ins)
                gain_done(2)

            nat = [0]

            def gain_done(n):
                for _ in range(n):
                    dve.engine_nop().then_inc(gain_used, 1)

            def rms_norm(final=False):
                asks = []
                g = next_gain()
                for t in range(NT):
                    link(dve.tensor_tensor_reduce(y[:, t], x[:, t], x[:, t], 1.0, 0.0, ALU.mult, ALU.add,
                                                  sq[:, t, 0:1]))
                    asks.append(ask_root(sq[:, t, 0:1], 1.0 / D, NORM_EPS, 1))
                for t in range(NT):
                    r = root(asks[t])
                    ins = dve.scalar_tensor_tensor(out=y[:, t], in0=x[:, t], scalar=r[:, 0:1], in1=g[:],
                                                   op0=ALU.mult, op1=ALU.mult)
                    ins.then_inc(y_done if final else nat_ready, 1)
                if not final:
                    nat[0] += 2
                    dve.wait_ge(nat_ready, nat[0])
                    gain_done(1)

            def add_residual(acc):
                for t in range(NT):
                    acc_ready(acc, t)
                    for half in range(2):
                        c = slice(half * 512, (half + 1) * 512)
                        ins = dve.tensor_tensor(x[:, t, c], x[:, t, c], bank[4 + 2 * t + half][:, :], ALU.add)
                link(ins)

            def setup():
                dve.wait_ge(got["rel"], 16)
                dve.tensor_copy(rel_rev[:, 127:REVW], rel_in[:, REL - 1::-1]).then_inc(rel_done, 1)
                dve.tensor_copy(rel_rev[:, 0:127], rel_in[:, REL - 1:REL].broadcast_to([12, 127])).then_inc(rel_done, 1)
                dve.wait_ge(router_hi_s, 1)
                dve.tensor_tensor(router_lo[:], router_w[:], router_hi[:].bitcast(F32), ALU.subtract).then_inc(
                    router_lo_s, 1)
                dve.wait_ge(got["lam"], 64)
                for i in range(2):
                    for d in range(2):
                        ins = dve.tensor_tensor_reduce(lam_in[:, 2 * i, d], lam_in[:, 2 * i, d], lam_in[:, 2 * i + 1, d],
                                                       1.0, 0.0, ALU.mult, ALU.add, lam[:, 2 * i + d:2 * i + d + 1])
                ins.then_inc(lam_dot, 1)
                dve.wait_ge(got["pos"], 16)
                link(dve.tensor_copy(rope_f[:, 0, :, 0], pos_i[:]))
                for t in range(NT):
                    ins = dve.tensor_scalar(rope_f[:, 1, t], cst[:, C_INV:C_INV + 8], rope_f[:, 0, t, 0:1], None, ALU.mult)
                link(ins)
                link(dve.tensor_scalar(rope_k[:], rope_f[:, 1], 1.0 / (2 * math.pi), None, ALU.mult))
                link(dve.tensor_copy(rope_f[:, 2], rope_k[:]))
                link(dve.scalar_tensor_tensor(out=rope_f[:, 3], in0=rope_f[:, 2], scalar=-TWO_PI_1, in1=rope_f[:, 1],
                                              op0=ALU.mult, op1=ALU.add))
                link(dve.scalar_tensor_tensor(out=rope_f[:, 3], in0=rope_f[:, 2], scalar=-TWO_PI_2, in1=rope_f[:, 3],
                                              op0=ALU.mult, op1=ALU.add))
                link(dve.tensor_scalar(rope_f[:, 4], rope_f[:, 3], math.pi / 2, None, ALU.add))
                link(dve.tensor_scalar(rope_f[:, 1], rope_f[:, 4], math.pi, -2 * math.pi, ALU.is_gt, ALU.mult))
                link(dve.tensor_tensor(rope_f[:, 4], rope_f[:, 4], rope_f[:, 1], ALU.add))
                link(dve.tensor_scalar(rope_f[:, 4], rope_f[:, 4], PI_SAFE, -PI_SAFE, ALU.min, ALU.max))
                dve.tensor_scalar(rope_f[:, 5], rope_f[:, 3], PI_SAFE, -PI_SAFE, ALU.min, ALU.max).then_inc(rope_arg, 1)
                dve.wait_ge(lam_exp, 1)
                for l, d in DIFF_SLOT.items():
                    link(dve.tensor_tensor(lam[:, 8 + d:9 + d], lam[:, 6 + d:7 + d], lam[:, 4 + d:5 + d], ALU.subtract))
                    link(dve.tensor_scalar(lam[:, 10 + d:11 + d], lam[:, 8 + d:9 + d], -LAMBDA_INIT[l], None, ALU.add))
                dve.wait_ge(got["subg"], 16)
                for l, d in DIFF_SLOT.items():
                    link(dve.tensor_scalar(subg[:, d], subg[:, d], 1.0 - LAMBDA_INIT[l], None, ALU.mult))

            def rotate(l):
                n = 18 if KIND[l] == SWA else 32
                if l == 2:
                    dve.wait_ge(rope_sin, 1)
                dve.wait_ge(proj_ev, PROJ0[l + 1])
                heads = h_in[:, :, 0:n * HD].rearrange("p t (h c) -> p t h c", c=HD)
                x1, x2 = heads[:, :, :, 0:8], heads[:, :, :, 8:16]
                tmp = [r[:, 0:NT * n * 8].rearrange("p (t h c) -> p t h c", t=NT, c=8) for r in rt]

                def table(i):
                    return cos_sin[:, i].rearrange("p t c -> p t () c").broadcast_to([P, NT, n, 8])

                for i, (a, c) in enumerate(((x1, 0), (x2, 1), (x2, 0), (x1, 1))):
                    ins = dve.tensor_tensor(tmp[i], a, table(c), ALU.mult)
                link(ins)
                dve.tensor_tensor(x1, tmp[0], tmp[1], ALU.subtract)
                dve.tensor_tensor(x2, tmp[2], tmp[3], ALU.add).then_inc(rope_done, 1)

            def finish_group(l, order, soft):
                kind = KIND[l]
                og, dv = OGRP[kind], VW[kind]
                if order % og != og - 1:
                    return
                gi = order // og
                o = OG0[l] + gi
                b = bank[6 + o % 2]
                j0 = order - og + 1
                dve.wait_ge(pv_done, HEAD0[l] + order + 1)
                src = b[:, 0:NT * og * dv].rearrange("p (t h c) -> p t h c", t=NT, c=dv)
                if not soft:
                    at = D_POOL + D_CHUNK + (j0 - NSOFT[HYB]) * HD
                    link(dve.tensor_copy(y[:, :, at:at + og * HD].rearrange("p t (h c) -> p t h c", c=HD), src))
                else:
                    j = slice(j0, j0 + og)
                    if kind == SWA:
                        link(dve.tensor_tensor(sums[:, :, j], sums[:, :, j], esink[:, :, j], ALU.add))
                    link(dve.reciprocal(rinv[:, :, j], sums[:, :, j]))
                    if kind == DIFF:
                        d = DIFF_SLOT[l]
                        link(dve.tensor_scalar(rinv[:, :, j0 + 1:j0 + 2], rinv[:, :, j0 + 1:j0 + 2],
                                               lam[:, 10 + d:11 + d], None, ALU.mult))
                    r = rinv[:, :, j].rearrange("p t h -> p t h ()").broadcast_to([P, NT, og, dv])
                    if kind == DIFF:
                        link(dve.tensor_tensor(o_tmp[:], src, r, ALU.mult))
                        h = j0 // 2
                        link(dve.tensor_tensor(y[:, :, h * P:(h + 1) * P], o_tmp[:, :, 0], o_tmp[:, :, 1], ALU.add))
                        for t in range(NT):
                            ins = dve.tensor_tensor_reduce(o_tmp[:, t, 0], y[:, t, h * P:(h + 1) * P],
                                                           y[:, t, h * P:(h + 1) * P], 1.0, 0.0, ALU.mult, ALU.add,
                                                           sq[:, t, h:h + 1])
                        link(ins)
                    else:
                        at = (D_POOL if kind == HYB else 0) + j0 * HD
                        link(dve.tensor_tensor(y[:, :, at:at + og * dv].rearrange("p t (h c) -> p t h c", c=dv), src, r,
                                               ALU.mult))
                dve.engine_nop().then_inc(o_read, 1)

            def soft_heads(l):
                kind = KIND[l]
                n = NSOFT[kind]
                mask = cst[:, {HYB: C_CHUNK, SWA: C_WINDOW}.get(kind, C_CAUSAL):][:, 0:384]
                if kind == SWA:
                    dve.wait_ge(got["sinks"], 16)
                if kind != HYB:
                    dve.wait_ge(rope_done, l - 1)
                for i in range(n + 4):
                    j = i - 1
                    if 0 <= j < n:
                        g, s = HEAD0[l] + j, SOFT0[l] + j
                        dve.wait_ge(scored, g + 1)
                        if s >= 4:
                            dve.wait_ge(pt_done, s - 3)
                        for t, c in enumerate((slice(0, P), slice(P, 3 * P))):
                            ins = dve.tensor_tensor_reduce(z[:, s % 4, c], bank[g % 2][:, c], mask[:, c], SCALE, -3e38,
                                                           ALU.add, ALU.max, mx[:, t, j:j + 1])
                        ins.then_inc(z_read, 1)
                        dve.wait_ge(z_read, g + 1)
                        if kind == SWA:
                            dve.tensor_scalar(nmx[:, :, j], mx[:, :, j], sinks[:, j:j + 1], -1.0, ALU.max,
                                              ALU.mult).then_inc(nmx_ready, 1)
                        else:
                            dve.tensor_scalar(nmx[:, :, j], mx[:, :, j], -1.0, None, ALU.mult).then_inc(nmx_ready, 1)
                    if i in (1, 3, 5):
                        lo(PLAN[l][1][i // 2])
                    j = i - 3
                    if 0 <= j < n:
                        s = SOFT0[l] + j
                        dve.wait_ge(pt_done, s + 1)
                        dve.tensor_copy(pt[:, s % 4], bank[4 + s % 2][:, 0:384]).then_inc(pt_ready, 1)
                    j = i - 4
                    if 0 <= j < n:
                        finish_group(l, j, True)

            def stick_heads(l):
                n = NSTICK[HYB]
                for i in range(n + 6):
                    h = i - 1
                    if 0 <= h < n:
                        b = STICK0[l] + h
                        g = HEAD0[l] + NSOFT[HYB] + h
                        dve.wait_ge(scored, g + 1)
                        if h >= 2:
                            dve.wait_ge(zm_ready, b - 1)
                            dve.wait_ge(sp_ready, b - 1)
                        dve.tensor_scalar(zs[:, b % 2], bank[g % 2][:, 0:384], SCALE, None, ALU.mult).then_inc(z_read, 1)
                    h = i - 2
                    if 0 <= h < n:
                        b = STICK0[l] + h
                        dve.wait_ge(sp_log, b + 1)
                        if h >= 2:
                            dve.wait_ge(c_done, b - 1)
                        link(dve.scalar_tensor_tensor(out=sps[:, b % 2], in0=zs[:, b % 2], scalar=0.0, in1=es[:, b % 2],
                                                      op0=ALU.max, op1=ALU.add))
                        dve.tensor_tensor(sps[:, b % 2], sps[:, b % 2], cst[:, C_STRICT:C_STRICT + 384],
                                          ALU.mult).then_inc(sp_ready, 1)
                    h = i - 3
                    if 0 <= h < n:
                        b = STICK0[l] + h
                        dve.wait_ge(c_done, b + 1)
                        dve.wait_ge(zm_ready, b + 1)
                        dve.tensor_tensor(zm[:, b % 2], zm[:, b % 2], bank[4 + b % 2][:, 0:384],
                                          ALU.subtract).then_inc(arg_ready, 1)
                    h = i - 5
                    if 0 <= h < n:
                        finish_group(l, NSOFT[HYB] + h, False)

            def mixer_norm(l):
                g = next_gain()
                parts = ((0, D_POOL), (D_POOL, D_CHUNK), (D_POOL + D_CHUNK, D_SB))
                for t in range(NT):
                    for i, (at, w) in enumerate(parts):
                        ins = dve.tensor_tensor_reduce(h_in[:, t, at:at + w], y[:, t, at:at + w], y[:, t, at:at + w],
                                                       1.0 / w, 0.0, ALU.mult, ALU.add, sq[:, t, i:i + 1])
                link(ins)
                link(dve.tensor_copy(mv6[:], sq[:, :, 0:3]))
                r = root(ask_root(mv6[:].rearrange("p t c -> p (t c)"), 1.0, RMS_EPS, 6))
                for t in range(NT):
                    for i, (at, w) in enumerate(parts):
                        ins = dve.scalar_tensor_tensor(out=y[:, t, at:at + w], in0=y[:, t, at:at + w],
                                                       scalar=r[:, 3 * t + i:3 * t + i + 1], in1=g[:, at:at + w],
                                                       op0=ALU.mult, op1=ALU.mult)
                    ins.then_inc(nat_ready, 1)
                nat[0] += 2
                dve.wait_ge(nat_ready, nat[0])
                gain_done(1)

            def head_norm(l):
                r = root(ask_root(sq[:].rearrange("p t h -> p (t h)"), 1.0 / P, NORM_EPS, 16))
                for t in range(NT):
                    v = y[:, t].rearrange("p (h c) -> p h c", c=P)
                    link(dve.tensor_tensor(v, v, r[:, 8 * t:8 * t + 8].rearrange("p h -> p h ()").broadcast_to([P, 8, P]),
                                           ALU.mult))
                    dve.tensor_tensor(v, v, subg[:, DIFF_SLOT[l]].rearrange("p c -> p () c").broadcast_to([P, 8, P]),
                                      ALU.mult).then_inc(nat_ready, 1)
                nat[0] += 2

            def y_in_place():
                for _ in range(NT):
                    dve.engine_nop().then_inc(nat_ready, 1)
                nat[0] += 2

            def gates_of(l):
                dve.wait_ge(logits, 1)
                dve.wait_ge(xn_hi_ready, 1)
                dve.tensor_tensor(xn_lo[:], x[:], xn_hi[:].bitcast(F32), ALU.subtract).then_inc(xn_lo_ready, 1)
                link(dve.tensor_copy(lg[:], bank[2][:, 0:16].rearrange("p (t e) -> p t e", t=NT)))
                for t in range(NT):
                    ins = dve.max(top[:, t], lg[:, t])
                link(ins)
                for t in range(NT):
                    ins = dve.max_index(topi[:, t], top[:, t], lg[:, t])
                link(ins)
                dve.tensor_copy(topf[:, :, 0:2], topi[:, :, 0:2])
                dve.tensor_tensor(topf[:, :, 3:4], top[:, :, 1:2], top[:, :, 0:1], ALU.subtract).then_inc(gap, 1)
                dve.wait_ge(gap_exp, 1)
                link(dve.tensor_scalar(topf[:, :, 5:6], topf[:, :, 4:5], 1.0, None, ALU.add))
                link(dve.reciprocal(topf[:, :, 6:7], topf[:, :, 5:6]))
                link(dve.tensor_tensor(topf[:, :, 7:8], topf[:, :, 6:7], topf[:, :, 4:5], ALU.mult))
                for t in range(NT):
                    for i, dst in ((0, gw), (1, lg)):
                        ins = dve.tensor_scalar(dst[:, t], cst[:, C_IOTA:C_IOTA + 8], topf[:, t, i:i + 1],
                                                topf[:, t, 6 + i:7 + i], ALU.is_equal, ALU.mult)
                    for i, dst in ((0, chosen), (1, top)):
                        ins = dve.tensor_scalar(dst[:, t], cst[:, C_IOTA:C_IOTA + 8], topf[:, t, i:i + 1], None,
                                                ALU.is_equal)
                link(ins)
                dve.tensor_tensor(gw[:], gw[:], lg[:], ALU.add)
                dve.tensor_tensor(chosen[:], chosen[:], top[:], ALU.add).then_inc(gates, 1)
                dve.wait_ge(ranked, 1)
                dve.tensor_copy(count[:], bank[3][:, 16:24])
                dve.tensor_copy(slot_of[:], bank[3][:, 0:16].rearrange("p (t e) -> p t e", t=NT)).then_inc(counted, 1)
                dve.wait_ge(counted, 1)

            def moe():
                hb = GRP0[1]
                (sg_, tg), (su, tu), (sd, td) = PLAN[1][2]

                def column(tile, t, e):
                    return tile[:, t, e:e + 1] if isinstance(e, int) else tile[:, t, bass.ds(e, 1)]

                def place_tokens(e):
                    for t in range(NT):
                        ins = dve.tensor_scalar(perm[:, t], iota[:], column(slot_of, t, e), column(chosen, t, e),
                                                ALU.is_equal, ALU.mult)
                    ins.then_inc(perm_ready, 1)

                def group(n, after_gate=None, before_down=None, after=None, last=False):
                    if not last:
                        lo((sg_, n + (tg + 1)))
                    if after_gate is not None:
                        after_gate()
                    dve.wait_ge(act_done, n + (hb + 1))
                    dve.wait_ge(used[su], n + (tu + 1))
                    dve.wait_ge(hl_ready, n + hb)
                    dve.tensor_tensor(h_f[:, 0], sg[:], bank[1][:, :], ALU.mult).then_inc(h_mid, 1)
                    if not last:
                        lo((su, n + (tu + 1)))
                    if before_down is not None:
                        before_down()
                    lo((sd, n + td))
                    if after is not None:
                        after()
                    dve.wait_ge(hh_ready, n + (hb + 1))
                    dve.tensor_tensor(h_lo[:, 0], bank[2][:, :].rearrange("p (f s) -> p f s", f=2),
                                      h_hi[:, 0].bitcast(F32), ALU.subtract).then_inc(hl_ready, 1)

                def split_result(e):
                    for b in range(4):
                        dve.wait_ge(ye_hi_ready, e * 4 + (b + 1))
                        c = slice((b % 2) * 512, (b % 2 + 1) * 512)
                        dve.tensor_tensor(ye_lo[:, b // 2, c], bank[4 + b][:, :], ye_hi[:, b // 2, c].bitcast(F32),
                                          ALU.subtract).then_inc(ye_lo_ready, 1)

                def add_result(e):
                    for t in range(NT):
                        for half in range(2):
                            c = slice(half * 512, (half + 1) * 512)
                            dve.wait_ge(scattered, e * 4 + (2 * t + half + 1))
                            dve.wait_ge(added, e * 4 + (2 * t + half + 1))
                            dve.scalar_tensor_tensor(out=y[:, t, c], in0=bank[2 + half][:, :],
                                                     scalar=column(gw, t, e), in1=y[:, t, c], op0=ALU.mult,
                                                     op1=ALU.add).then_inc(added, 1)

                def next_perm(e):
                    dve.wait_ge(perm_turned, e + 1)
                    place_tokens((e + 1) % N_EXP)

                def expert(e, last=False):
                    n0 = e * GE
                    group(n0 + 1)
                    group(n0 + 2, after_gate=lambda: next_perm(e))
                    with dve.Fori(3, GE - last) as i:
                        group(n0 + i)
                    if last:
                        group(n0 + GE - 1, last=True)
                        split_result(e)
                        add_result(e)
                    else:
                        group(n0 + GE, before_down=lambda: split_result(e), after=lambda: add_result(e))

                for t in range(NT):
                    for half in range(2):
                        dve.memset(y[:, t, half * 512:(half + 1) * 512], 0.0).then_inc(added, 1)
                dve.wait_ge(got["iota"], 16)
                place_tokens(0)
                group(0)
                with dve.Fori(0, N_EXP - 1) as e:
                    expert(e)
                expert(N_EXP - 1, last=True)
                dve.wait_ge(added, 4 * N_EXP + 4)

            def hidden_lo(par, i, hb):
                dve.wait_ge(hh_ready, i + (hb + 1))
                dve.tensor_tensor(h_lo[:, par], h_f[:, par, :].rearrange("p (f s) -> p f s", f=2),
                                  h_hi[:, par].bitcast(F32), ALU.subtract).then_inc(hl_ready, 1)

            def swiglu(l):
                g, hb = groups(l), GRP0[l]
                (sg_, tg), (su, tu), (sd, td) = PLAN[l][2]

                def hidden(i):
                    dve.wait_ge(act_done, i + (hb + 1))
                    if not isinstance(i, int) or i > 0:
                        dve.wait_ge(hl_ready, i + hb)
                    dve.tensor_tensor(h_f[:, 0], sg[:], bank[1][:, :], ALU.mult).then_inc(h_mid, 1)

                lo((sg_, tg + 1))
                hidden(0)
                lo((su, tu + 1))
                hidden_lo(0, 0, hb)
                with dve.Fori(1, g - 1) as i:
                    lo((sg_, i + (tg + 1)))
                    hidden(i)
                    lo((su, i + (tu + 1)))
                    hidden_lo(0, i, hb)
                    lo((sd, i + td))
                hidden(g - 1)
                hidden_lo(0, g - 1, hb)
                lo((sd, td + g - 1))

            def mlp(l):
                g, hb = groups(l), GRP0[l]
                (s0, t0), (s1, t1), (sd, td) = PLAN[l][2]

                def square(par, i):
                    dve.wait_ge(act_done, i + (hb + 1))
                    if not isinstance(i, int) or i >= 2:
                        dve.wait_ge(hl_ready, i + (hb - 1))
                    dve.tensor_tensor(h_f[:, par], sg[:], sg[:], ALU.mult).then_inc(h_mid, 1)

                square(0, 0)
                lo((s0, t0 + 1))
                hidden_lo(0, 0, hb)
                with dve.Fori(0, 6) as j:
                    square(1, j * 2 + 1)
                    lo((s1, j + (t1 + 1)))
                    hidden_lo(1, j * 2 + 1, hb)
                    lo((sd, j * 2 + (td + 1)))
                    square(0, j * 2 + 2)
                    lo((s0, j + (t0 + 2)))
                    hidden_lo(0, j * 2 + 2, hb)
                    lo((sd, j * 2 + (td + 2)))
                for i in range(g - 3, g):
                    square(i % 2, i)
                    if i == g - 3:
                        lo((s1, t1 + g // 2 - 1))
                    hidden_lo(i % 2, i, hb)
                    lo((sd, td + i))

            for l in range(NL):
                proj, outp, first = PLAN[l]
                if l == 0:
                    for c in range(2):
                        lo(proj[c])
                to_t(3 * l)
                lo(proj[2])
                for c in range(len(proj)):
                    if KIND[l] == SWA:
                        dve.wait_ge(got["swa_bias"], 16)
                        dve.wait_ge(used[proj[c][0]], proj[c][1] + 1)
                        dve.tensor_tensor(h_in[:, :, c * UC:(c + 1) * UC],
                                          bank[4 + c % 4][:, :].rearrange("p (t c) -> p t c", t=NT),
                                          swa_bias[:, c * UC:(c + 1) * UC].rearrange("p c -> p () c").broadcast_to(
                                              [P, NT, UC]), ALU.add).then_inc(proj_ev, 1)
                    if c + 3 < len(proj):
                        lo(proj[c + 3])
                if l == 0:
                    dve.wait_ge(cst_loaded, 16)
                    setup()
                if KIND[l] == HYB:
                    dve.wait_ge(got["pool_scale"], 16)
                    dve.wait_ge(pool_out, l + 1)
                    link(dve.tensor_tensor(y[:, :, 0:D_POOL], bank[6][:, :].rearrange("p (t c) -> p t c", t=NT),
                                           pool_scale[:, l].rearrange("p c -> p () c").broadcast_to([P, NT, D_POOL]),
                                           ALU.mult))
                else:
                    rotate(l)
                soft_heads(l)
                if KIND[l] == HYB:
                    stick_heads(l)
                    mixer_norm(l)
                elif KIND[l] == DIFF:
                    head_norm(l)
                else:
                    y_in_place()
                to_t(3 * l + 1)
                lo(outp[3])
                for i in range(2):
                    lo(first[i])
                if KIND[l] == HYB:
                    if l == 0:
                        dve.wait_ge(x_loaded, 16)
                    residual_norm(2 * l)
                else:
                    add_residual(2 * l)
                    rms_norm()
                to_t(3 * l + 2)
                if l != 1:
                    lo(first[2])
                    (swiglu if KIND[l] == HYB else mlp)(l)
                else:
                    gates_of(l)
                    moe()
                if l + 1 < NL:
                    for c in range(2):
                        lo(PLAN[l + 1][0][c])
                if KIND[l] == HYB:
                    residual_norm(2 * l + 1, to_turn=(l == 0))
                else:
                    add_residual(2 * l + 1)
                if l >= 1:
                    rms_norm(final=(l == NL - 1))


def constants():
    import numpy as np
    f = np.float32
    c = np.zeros((P, C_N), f)
    i = np.arange(P)[:, None]
    j = np.arange(P)[None, :]
    c[:, C_ID:C_ID + P] = i == j
    c[:, C_TRI:C_TRI + P] = i >= j
    c[:, C_ONE:C_ONE + P] = 1
    c[:, C_FLIP:C_FLIP + P] = 8.0 * (i + j == P - 1)
    kt = np.arange(S)[None, :]

    def two_tiles(ok):
        return np.where(np.concatenate([ok(i, kt[:, :P]), ok(i + P, kt)], axis=1), 0.0, NEG).astype(f)

    c[:, C_CAUSAL:C_CAUSAL + 384] = two_tiles(lambda q, k: k <= q)
    c[:, C_CHUNK:C_CHUNK + 384] = two_tiles(lambda q, k: k // 64 <= q // 64)
    c[:, C_WINDOW:C_WINDOW + 384] = two_tiles(lambda q, k: (k <= q) & (q - k < 128))
    strict = np.concatenate([i < kt, (i + P) < kt[:, P:]], axis=1)
    c[:, C_STRICT:C_STRICT + 384] = strict
    c[:, C_STRICTNEG:C_STRICTNEG + 384] = np.where(strict, 0.0, NEG)
    c[:, C_IOTA:C_IOTA + 8] = np.arange(8)
    c[:, C_INV:C_INV + 8] = (f(500000.0) ** (-np.arange(0, 16, 2, dtype=f) / f(16))).astype(f)
    c[:, C_HALF:C_HALF + 16] = -0.5
    c[:, C_ONECOL] = 1
    tq, ts = np.arange(S)[None, :], np.arange(S)[:, None]
    pm = np.zeros((P, NT, 4, S), f)
    for g, w in enumerate((2, 4, 8, 16)):
        m = ((tq >= ts) & (tq - ts < w)) / np.minimum(tq + 1.0, w) - (tq == ts)
        pm[:, :, g, :] = m.astype(f).reshape(NT, P, S).transpose(1, 0, 2)
    iota = np.broadcast_to(np.arange(S, dtype=f), (P, S)).copy()
    return {"cst": c, "pool_m": pm, "iota": iota}


_INS = ["x", "w_in", "pool_w", "pool_scale", "rel_bias", "g_mix", "w_out", "ln1_g", "ln1_b", "ln2_g", "ln2_b",
        "ffn_wg", "ffn_wu", "ffn_wd", "moe_router", "moe_wg", "moe_wu", "moe_wd", "positions_2", "attn_norm_g_2",
        "mlp_norm_g_2", "diff_w_in_2", "diff_w_out_2", "diff_lam_q1_2", "diff_lam_k1_2", "diff_lam_q2_2",
        "diff_lam_k2_2", "diff_subln_g_2", "moba_w_in_2", "moba_w_out_2", "swa_w_in_2", "swa_b_in_2", "swa_sinks_2",
        "swa_w_out_2", "mlp_w_up_2", "mlp_w_down_2", "final_norm_g_2"]


def kernel(**inputs):
    import numpy as np
    import concourse.bacc as bacc
    from concourse.bass_utils import run_bass_kernel_spmd as run

    nc = bacc.Bacc("TRN2", target_bir_lowering=False, num_devices=1)
    arrays = {name: np.ascontiguousarray(inputs[name]) for name in _INS}
    arrays.update(constants())
    aps = {name: nc.dram_tensor("in_" + name, a.shape, mybir.dt.from_np(a.dtype), kind="ExternalInput").ap()
           for name, a in arrays.items()}
    out = nc.dram_tensor("out", (1, S, D), F32, kind="ExternalOutput").ap()
    scratch = nc.dram_tensor("bias_scratch", (12, REVW), F32, kind="Internal").ap()
    build(nc, aps, out, scratch)
    r = run(nc, [{"in_" + n: a for n, a in arrays.items()}], core_ids=[0])
    return r.results[0]["out"]
```

```python
import math
from contextlib import ExitStack

import concourse.bass as bass
from concourse import mybir

F32 = mybir.dt.float32
F32R = mybir.dt.float32r
I32 = mybir.dt.int32
U32 = mybir.dt.uint32
ALU = mybir.AluOpType
ACT = mybir.ActivationFunctionType
AX = mybir.AxisListType

P = 128
S, D = 256, 1024
NT = S // P
KT = D // P
UC = 256
HD = 64
D_POOL, D_CHUNK, D_SB = 256, 384, 384
F_MOE = 2816
F_MLP = 4096
N_EXP = 8
GE = F_MOE // UC
ALPHA = 4.0 ** 0.25
LN_EPS, RMS_EPS, NORM_EPS = 1e-5, 1e-6, 1e-6
SCALE = HD ** -0.5
REL = 257
REVW = 384

HYB, DIFF, MOBA, SWA = range(4)
KIND = [HYB, HYB, DIFF, MOBA, SWA, DIFF]
NL = len(KIND)
NPROJ = {HYB: 10, DIFF: 12, MOBA: 12, SWA: 5}
NSOFT = {HYB: 6, DIFF: 16, MOBA: 16, SWA: 16}
NSTICK = {HYB: 6, DIFF: 0, MOBA: 0, SWA: 0}
ORDER = {HYB: list(range(10)), DIFF: [0, 4, 8, 1, 5, 9, 2, 6, 10, 3, 7, 11], MOBA: [0, 4, 8, 1, 5, 9, 2, 6, 10, 3, 7, 11],
         SWA: [4, 0, 1, 2, 3]}
LATE_HEAD = {DIFF: 12, MOBA: 12, SWA: 8}
VW = {HYB: 64, DIFF: 128, MOBA: 64, SWA: 64}
OGRP = {HYB: 3, DIFF: 2, MOBA: 4, SWA: 4}
DIFF_INDEX = {2: 0, 5: 3}
LAMBDA_INIT = {l: 0.8 - 0.6 * math.exp(-0.3 * i) for l, i in DIFF_INDEX.items()}
DIFF_SLOT = {2: 0, 5: 1}


def groups(l):
    return {0: GE, 1: N_EXP * GE}.get(l, F_MLP // UC)


def before(per_layer):
    return [sum(per_layer[:l]) for l in range(len(per_layer) + 1)]


PROJ0 = before([NPROJ[k] for k in KIND])
SOFT0 = before([NSOFT[k] for k in KIND])
STICK0 = before([NSTICK[k] for k in KIND])
HEAD0 = before([NSOFT[k] + NSTICK[k] for k in KIND])
OG0 = before([(NSOFT[k] + NSTICK[k]) // OGRP[k] for k in KIND])
GRP0 = before([groups(l) for l in range(NL)])
ROOTS = [w for l in range(NL) for w in (
    [6, 1, 1, 1, 1] if KIND[l] == HYB else [1, 1] + [2] * (8 * (KIND[l] == DIFF)) + [1, 1])] + [1, 1]


def plan_slots():
    turns, at, plan = [0, 0, 0], [0], []

    def take(n=1):
        out = []
        for _ in range(n):
            s = at[0] % 3
            out.append((s, turns[s]))
            turns[s] += 1
            at[0] += 1
        return out

    for l in range(NL):
        proj = take(NPROJ[KIND[l]])
        out = take(4)
        first = take(3)
        g = groups(l)
        if KIND[l] == HYB:
            for s, _ in first:
                turns[s] += g - 1
        else:
            for (s, _), n in zip(first, (g // 2 - 1, g // 2 - 1, g - 1)):
                turns[s] += n
        plan.append((proj, out, first))
    return plan


PLAN = plan_slots()
LAST_UNIT = [u for l in range(NL) for u in (PLAN[l][1][3], (PLAN[l][2][2][0], PLAN[l][2][2][1] + groups(l) - 1))]

C_ID, C_TRI, C_ONE, C_FLIP = 0, 128, 256, 384
C_CAUSAL, C_CHUNK, C_WINDOW, C_STRICT, C_STRICTNEG = (512 + 384 * i for i in range(5))
C_IOTA = 512 + 384 * 5
C_INV = C_IOTA + 8
C_HALF = C_INV + 8
C_ONECOL = C_HALF + 16
C_N = C_ONECOL + 1
NEG = -1e30
TWO_PI_1, TWO_PI_2 = 6.28125, 2 * math.pi - 6.28125
PI_SAFE = 3.1415925


def build(nc, A, out, bias_scratch):
    with ExitStack() as ctx:
        def sb(name, shape, dt=F32, scope=ctx):
            return scope.enter_context(nc.sbuf_tensor(name, shape, dt))

        def sem(name):
            return ctx.enter_context(nc.semaphore(name))

        raw = [sb(f"raw{s}", [P, 2048]) for s in range(3)]
        whi = [sb(f"whi{s}", [P, 2048], F32R) for s in range(3)]
        wlo = [sb(f"wlo{s}", [P, 2048], F32R) for s in range(3)]
        xt_hi = sb("xt_hi", [P, KT, S], F32R)
        xt_lo = sb("xt_lo", [P, KT, S], F32R)
        x = sb("x", [P, NT, D])
        y = sb("y", [P, NT, D])
        gain = [sb(f"gain{i}", [P, D]) for i in range(3)]
        cst = sb("cst", [P, C_N])
        sinks = sb("sinks", [P, 16])
        pool_scale = sb("pool_scale", [P, 2, D_POOL])
        pool_w = sb("pool_w", [HD, 2, 4, HD])
        lam_in = sb("lam_in", [P, 4, 2, HD])
        lam = sb("lam", [P, 16])
        subg = sb("subg", [P, 2, 2 * HD])
        rel_in = sb("rel_in", [12, REL])
        rel_rev = sb("rel_rev", [12, REVW])
        pos_i = sb("pos_i", [P, NT], I32)
        rope_f = sb("rope_f", [P, 6, NT, 8])
        rope_k = sb("rope_k", [P, NT, 8], I32)
        cos_sin = sb("cos_sin", [P, 2, NT, 8])
        router_w = sb("router_w", [P, KT, N_EXP])
        router_hi = sb("router_hi", [P, KT, N_EXP], F32R)
        router_lo = sb("router_lo", [P, KT, N_EXP], F32R)
        stats = sb("stats", [P, NT, 2, 6])
        mv = sb("mv", [P, NT, 2])
        mv6 = sb("mv6", [P, NT, 3])
        var = sb("var", [P, 8, 16])
        rstd = sb("rstd", [P, 8, 16])
        mx = sb("mx", [P, NT, 16])
        nmx = sb("nmx", [P, NT, 16])
        sums = sb("sums", [P, NT, 16])
        esink = sb("esink", [P, NT, 16])
        rinv = sb("rinv", [P, NT, 16])
        sq = sb("sq", [P, NT, 8])
        lg = sb("lg", [P, NT, 8])
        top = sb("top", [P, NT, 8])
        topi = sb("topi", [P, NT, 8], U32)
        topf = sb("topf", [P, NT, 8])
        gw = sb("gw", [P, NT, 8])
        chosen = sb("chosen", [P, NT, 8])
        slot_of = sb("slot_of", [P, NT, 8])
        count = sb("count", [P, 8], I32)
        silu_warm = sb("silu_warm", [P, 1])
        with ExitStack() as mix:
            h_in = sb("h_in", [P, NT, 3072], scope=mix)
            qk = sb("qk", [HD, 4, 512], scope=mix)
            z = sb("z", [P, 4, 384], scope=mix)
            pt = sb("pt", [P, 4, 384], scope=mix)
            with ExitStack() as hyb_only:
                toep = sb("toep", [P, 6, S], scope=hyb_only)
            swa_bias = sb("swa_bias", [P, 6 * S], scope=mix)[:, 0:1280]
            o_tmp = sb("o_tmp", [P, NT, 2, P], scope=mix)
            with ExitStack() as early:
                pool_m = sb("pool_m", [P, NT, 4, S], scope=early)
                pool_t = sb("pool_t", [HD, 4, S], scope=early)
            zs = sb("zs", [P, 2, 384], scope=mix)
            es = sb("es", [P, 2, 384], scope=mix)
            sps = sb("sps", [P, 2, 384], scope=mix)
            zm = sb("zm", [P, 2, 384], scope=mix)
        with ExitStack() as ffn:
            sg = sb("sg", [P, 2 * S], scope=ffn)
            h_f = sb("h_f", [P, 2, 2 * S], scope=ffn)
            h_hi = sb("h_hi", [P, 2, 2, S], F32R, scope=ffn)
            h_lo = sb("h_lo", [P, 2, 2, S], F32R, scope=ffn)
            xn_hi = sb("xn_hi", [P, NT, D], F32R, scope=ffn)
            xn_lo = sb("xn_lo", [P, NT, D], F32R, scope=ffn)
            iota = sb("iota", [P, S], scope=ffn)
            perm = sb("perm", [P, NT, S], F32R, scope=ffn)
            perm_t = sb("perm_t", [P, NT, S], F32R, scope=ffn)
            ye_hi = sb("ye_hi", [P, NT, D], F32R, scope=ffn)
            ye_lo = sb("ye_lo", [P, NT, D], F32R, scope=ffn)
            odd_hi = sb("odd_hi", [P, KT, S], F32R, scope=ffn)
            odd_lo = sb("odd_lo", [P, KT, S], F32R, scope=ffn)
        late_tmp = zs[:, :, :].rearrange("p a b -> p (a b)")
        rt = [z[:, 0:4, :].rearrange("p a b -> p (a b)")[:, 0:512], z[:, 0:4, :].rearrange("p a b -> p (a b)")[:, 512:1024],
              pt[:, 0:4, :].rearrange("p a b -> p (a b)")[:, 0:512], pt[:, 0:4, :].rearrange("p a b -> p (a b)")[:, 512:1024]]
        bank = [ctx.enter_context(nc.psum_tensor(f"bank{i}", [P, 512], F32)) for i in range(8)]

        ident = cst[:, C_ID:C_ID + P]
        tri = cst[:, C_TRI:C_TRI + P]
        ones = cst[:, C_ONE:C_ONE + P]
        flip8 = cst[:, C_FLIP:C_FLIP + P]

        loaded = [sem(f"raw_loaded{s}") for s in range(3)]
        hi_ready = [sem(f"hi_ready{s}") for s in range(3)]
        lo_ready = [sem(f"lo_ready{s}") for s in range(3)]
        used = [sem(f"unit_used{s}") for s in range(3)]
        gain_loaded = [sem(f"gain_loaded{i}") for i in range(3)]
        gain_used = sem("gain_used")
        cst_loaded = sem("cst_loaded")
        ident_loaded = sem("identity_loaded")
        x_loaded = [sem(f"x_loaded{t}") for t in range(NT)]
        names = ["swa_bias", "sinks", "pool_scale", "pool_w", "lam", "subg", "rel", "pos", "router", "pool_m",
                 "toep", "iota"]
        got = {n: sem(f"{n}_loaded") for n in names}
        rel_done, rel_stored = sem("rel_reversed"), sem("rel_stored")
        dchain, achain, pchain = sem("vector_chain"), sem("scalar_chain"), sem("gpsimd_chain")
        nat_ready = sem("natural_ready")
        turned = sem("turned")
        t_hi, t_lo = sem("t_hi"), sem("t_lo")
        proj_done, proj_ev = sem("proj_done"), sem("proj_evacuated")
        acc_done = sem("acc_done")
        var_ready, root_ready = sem("var_ready"), sem("root_ready")
        x_summed, squared = sem("x_summed"), sem("squared")
        rope_done, late_rope_done = sem("rope_done"), sem("late_rope_done")
        qk_turned, qk_ready = sem("qk_turned"), sem("qk_ready")
        scored, z_read = sem("scored"), sem("z_read")
        nmx_ready, p_ready = sem("nmx_ready"), sem("p_ready")
        pt_done, pt_ready = sem("pt_done"), sem("pt_ready")
        pv_done, o_read = sem("pv_done"), sem("o_read")
        sp_log, sp_ready, zm_ready = sem("stick_log"), sem("stick_sp"), sem("stick_zm")
        c_done, arg_ready, w_ready = sem("stick_sums"), sem("stick_arg"), sem("stick_w")
        pool_done, pool_copied, pool_out = sem("pool_done"), sem("pool_copied"), sem("pool_out")
        pool_read = sem("pool_read")
        act_done, h_mid, h_ready = sem("act_done"), sem("h_mid"), sem("h_ready")
        hh_ready, hl_ready = sem("hh_ready"), sem("hl_ready")
        lam_dot, lam_exp = sem("lam_dot"), sem("lam_exp")
        rope_arg, rope_sin = sem("rope_arg"), sem("rope_sin")
        router_hi_s, router_lo_s = sem("router_hi_ready"), sem("router_lo_ready")
        logits, gap, gap_exp, gates = sem("logits"), sem("gap"), sem("gap_exp"), sem("gates")
        ranked, counted = sem("ranked"), sem("counted")
        xn_hi_ready, xn_lo_ready = sem("xn_hi_ready"), sem("xn_lo_ready")
        perm_ready, perm_turned, perm_t_ready = sem("perm_ready"), sem("perm_turned"), sem("perm_t_ready")
        gathered, gather_copied = sem("gathered"), sem("gather_copied")
        ye_hi_ready, ye_lo_ready = sem("ye_hi_ready"), sem("ye_lo_ready")
        scattered, added = sem("scattered"), sem("added")
        h_turned = sem("h_turned")
        y_done, stored = sem("y_done"), sem("stored")

        w_in = [A["w_in"][0], A["w_in"][1], A["diff_w_in_2"][0], A["moba_w_in_2"][0], A["swa_w_in_2"][0],
                A["diff_w_in_2"][1]]
        w_out = [A["w_out"][0], A["w_out"][1], A["diff_w_out_2"][0], A["moba_w_out_2"][0], A["swa_w_out_2"][0],
                 A["diff_w_out_2"][1]]

        def as_k(t):
            return t[:, :].rearrange("p (k f) -> p k f", k=KT)

        def as_rows(t):
            return t[:, :].rearrange("p (k d) -> p k d", k=2)

        def proj_bank(l, c):
            return bank[4 + (c - NPROJ[KIND[l]]) % 4]

        def head_cols(l, j):
            k = KIND[l]
            if k == HYB:
                return D_POOL + j * HD, D_POOL + D_CHUNK + j * HD, D_POOL + 2 * D_CHUNK + j * HD
            if k == DIFF:
                return j * HD, D + j * HD, 2 * D + (j // 2) * 2 * HD
            if k == MOBA:
                return j * HD, D + j * HD, 2 * D + j * HD
            return j * HD, D + (j // 8) * HD, D + 2 * HD + (j // 8) * HD

        def stick_cols(j):
            base = D_POOL + 3 * D_CHUNK
            return base + j * HD, base + D_SB + j * HD, base + 2 * D_SB + j * HD

        def out_halves(l, i):
            third = (8, 12) if KIND[l] == SWA else (4, 6)
            steps = {0: [(0, 0), (0, 1)], 2: [(1, 0), (1, 1)], third[0]: [(2, 0)], third[1]: [(2, 1)]}
            return [(PLAN[l][1][u], half) for u, half in steps.get(i, [])]

        def rotate(engine, link, l, late):
            if KIND[l] == SWA:
                parts = [(8, 8)] if late else [(0, 8), (16, 2)]
            else:
                parts = [(12, 4), (28, 4)] if late else [(0, 12), (16, 12)]
            at, todo = 0, []
            for h0, n in parts:
                heads = h_in[:, :, h0 * HD:(h0 + n) * HD].rearrange("p t (h c) -> p t h c", c=HD)
                x1, x2 = heads[:, :, :, 0:8], heads[:, :, :, 8:16]
                w = NT * n * 8
                if late:
                    tmp = [late_tmp[:, at + i * w:at + (i + 1) * w] for i in range(4)]
                    at += 4 * w
                else:
                    tmp = [r[:, at:at + w] for r in rt]
                    at += w
                tmp = [m.rearrange("p (t h c) -> p t h c", t=NT, c=8) for m in tmp]
                for i, (a, c) in enumerate(((x1, 0), (x2, 1), (x2, 0), (x1, 1))):
                    table = cos_sin[:, c].rearrange("p t c -> p t () c").broadcast_to([P, NT, n, 8])
                    ins = engine.tensor_tensor(tmp[i], a, table, ALU.mult)
                todo.append((x1, x2, tmp))
            link(ins)
            for x1, x2, tmp in todo:
                engine.tensor_tensor(x1, tmp[0], tmp[1], ALU.subtract)
                ins = engine.tensor_tensor(x2, tmp[2], tmp[3], ALU.add)
            return ins

        block = ctx.enter_context(nc.Block())

        @block.sync
        def _(sp):
            sp.dma_start(cst[:, 0:P], A["cst"][:, 0:P]).then_inc(ident_loaded, 16)
            for t in range(NT):
                sp.dma_start(x[:, t], A["x"][0, t * P:(t + 1) * P, :]).then_inc(x_loaded[t], 16)

            def load(place, src, k):
                slot, turn = place
                if not isinstance(turn, int) or turn > 0:
                    sp.wait_ge(lo_ready[slot], turn * 2)
                sp.dma_start(raw[slot][:, :].rearrange("p (k f) -> p k f", k=k), src).then_inc(loaded[slot], 16)

            def cols(w, c):
                return w.rearrange("(k p) f -> p k f", p=P)[:, :, c]

            def rows(w, r):
                return w[r, :].rearrange("(k p) d -> p k d", p=P)

            gains = [A["g_mix"][0], A["ln1_g"][0], A["ln1_b"][0], A["ln2_g"][0], A["ln2_b"][0],
                     A["g_mix"][1], A["ln1_g"][1], A["ln1_b"][1], A["ln2_g"][1], A["ln2_b"][1]]
            for l in range(4):
                gains += [A["attn_norm_g_2"][l], A["mlp_norm_g_2"][l]]
            gains.append(A["final_norm_g_2"])
            next_gain = [0]

            def load_gains(n):
                for _ in range(n):
                    u = next_gain[0]
                    if u >= 3:
                        sp.wait_ge(gain_used, u - 2)
                    sp.dma_start(gain[u % 3][:], gains[u].partition_broadcast(P)).then_inc(gain_loaded[u % 3], 16)
                    next_gain[0] += 1

            def load_swiglu(l, wg, wu, wd, expert):
                g = groups(l)
                (sg_, tg), (su, tu), (sd, td) = PLAN[l][2]

                def up(w, i):
                    if expert:
                        return w[bass.ds(i // GE, 1), :, bass.ds((i % GE) * UC, UC)].rearrange(
                            "a (k p) f -> p (a k) f", p=P)
                    return w[:, bass.ds(i * UC, UC)].rearrange("(k p) f -> p k f", p=P)

                def down(i):
                    return wd[bass.ds(i * UC, UC), :].rearrange("(k p) d -> p k d", p=P)

                load((sg_, tg), up(wg, 0), KT)
                load((su, tu), up(wu, 0), KT)
                load((sd, td), down(0), 2)
                load((sg_, tg + 1), up(wg, 1), KT)
                load((su, tu + 1), up(wu, 1), KT)
                load_gains(3 if l == 1 else 2)
                with sp.Fori(1, g - 1) as i:
                    load((sg_, i + (tg + 1)), up(wg, i + 1), KT)
                    load((su, i + (tu + 1)), up(wu, i + 1), KT)
                    load((sd, i + td), down(i), 2)
                load((sd, td + g - 1), down(g - 1), 2)

            def load_mlp(l):
                g = groups(l)
                wu, wd = A["mlp_w_up_2"][l - 2], A["mlp_w_down_2"][l - 2]
                (s0, t0), (s1, t1), (sd, td) = PLAN[l][2]
                us, ut = (s0, s1), (t0, t1)

                def up(i, par, turn):
                    load((us[par], ut[par] + turn), wu[:, bass.ds(i * UC, UC)].rearrange("(k p) f -> p k f", p=P), KT)

                def down(i, ):
                    load((sd, i + td), wd[bass.ds(i * UC, UC), :].rearrange("(k p) d -> p k d", p=P), 2)

                up(0, 0, 0)
                up(1, 1, 0)
                down(0)
                up(2, 0, 1)
                load_gains(1)
                with sp.Fori(0, 6) as j:
                    up(j * 2 + 3, 1, j + 1)
                    down(j * 2 + 1)
                    up(j * 2 + 4, 0, j + 2)
                    down(j * 2 + 2)
                up(g - 1, 1, g // 2 - 1)
                down(g - 3)
                down(g - 2)
                down(g - 1)

            def small():
                sp.dma_start(rel_in[:], A["rel_bias"].rearrange("l h n -> (l h) n")).then_inc(got["rel"], 16)
                sp.dma_start(pool_scale[:], A["pool_scale"].partition_broadcast(P)).then_inc(got["pool_scale"], 16)
                sp.dma_start(pos_i[:], A["positions_2"][0].rearrange("(t p) -> p t", p=P),
                             allow_slow_non_contiguous=True).then_inc(got["pos"], 16)
                for i, n in enumerate(("diff_lam_q1_2", "diff_lam_k1_2", "diff_lam_q2_2", "diff_lam_k2_2")):
                    if i:
                        sp.wait_ge(got["lam"], 16 * i)
                    sp.dma_start(lam_in[:, i], A[n].partition_broadcast(P)).then_inc(got["lam"], 16)
                sp.dma_start(subg[:], A["diff_subln_g_2"].partition_broadcast(P)).then_inc(got["subg"], 16)
                sp.dma_start(router_w[:], A["moe_router"][0].rearrange("(k p) e -> p k e", p=P)).then_inc(
                    got["router"], 16)
                sp.dma_start(sinks[:], A["swa_sinks_2"][0].partition_broadcast(P)).then_inc(got["sinks"], 16)

            def load_toeplitz(l):
                sp.dma_start(toep[:], bass.AP(bias_scratch.tensor, l * 6 * REVW,
                                              [[1, P], [REVW, 6], [1, S]])).then_inc(got["toep"], 16)

            for l in range(NL):
                proj, outp, _ = PLAN[l]
                for c in range(NPROJ[KIND[l]]):
                    u = ORDER[KIND[l]][c]
                    load(proj[c], cols(w_in[l], slice(u * UC, (u + 1) * UC)), KT)
                    if l == 0 and c == 2:
                        sp.dma_start(pool_m[:], A["pool_m"]).then_inc(got["pool_m"], 16)
                        sp.dma_start(pool_w[:], A["pool_w"].rearrange("l g c d -> c l g d")).then_inc(
                            got["pool_w"], 16)
                    if l == 0 and c == 4:
                        sp.dma_start(cst[:, P:], A["cst"][:, P:]).then_inc(cst_loaded, 16)
                        small()
                    if c == (8 if l == 0 else 4):
                        load_gains(3 if KIND[l] == HYB else 1)
                        if l == 2:
                            sp.wait_ge(nat_ready, 8)
                            sp.dma_start(swa_bias, A["swa_b_in_2"][0].partition_broadcast(P)).then_inc(
                                got["swa_bias"], 16)
                        if l == 1:
                            sp.dma_start(pool_m[:], A["pool_m"]).then_inc(got["pool_m"], 16)
                            load_toeplitz(1)
                if l == 0:
                    sp.wait_ge(rel_done, 2)
                    sp.dma_start(bias_scratch, rel_rev[:]).then_inc(rel_stored, 16)
                    sp.wait_ge(rel_stored, 16)
                    load_toeplitz(0)
                for o in range(4):
                    load(outp[o], rows(w_out[l], slice(o * UC, (o + 1) * UC)), 2)
                if l == 0:
                    load_swiglu(0, A["ffn_wg"][0], A["ffn_wu"][0], A["ffn_wd"][0], False)
                elif l == 1:
                    sp.wait_ge(nat_ready, 2 * 3 * l + 2)
                    sp.dma_start(iota[:], A["iota"]).then_inc(got["iota"], 16)
                    load_swiglu(1, A["moe_wg"][0], A["moe_wu"][0],
                                A["moe_wd"][0].rearrange("e f d -> (e f) d"), True)
                else:
                    load_mlp(l)
            for t in range(NT):
                sp.wait_ge(y_done, t + 1)
                sp.dma_start(out[0, t * P:(t + 1) * P, :], y[:, t]).then_inc(stored, 16)
            sp.wait_ge(stored, 16 * NT)

        @block.gpsimd
        def _(pool):
            pool.wait_ge(cst_loaded, 16)
            done = [0]

            def roots(n):
                for _ in range(n):
                    r = done[0]
                    w = ROOTS[r]
                    pool.wait_ge(var_ready, r + 1)
                    pool.tensor_tensor(rstd[:, r % 8, 0:w], var[:, r % 8, 0:w], cst[:, C_HALF:C_HALF + w],
                                       ALU.pow).then_inc(root_ready, 1)
                    done[0] += 1

            def stick_masks(l):
                for h in range(NSTICK[KIND[l]]):
                    b = STICK0[l] + h
                    pool.wait_ge(z_read, HEAD0[l] + NSOFT[KIND[l]] + h + 1)
                    if b >= 2:
                        pool.wait_ge(pv_done, SOFT0[l] + NSOFT[KIND[l]] + b - 1)
                    pool.tensor_tensor(zm[:, b % 2], zs[:, b % 2], cst[:, C_STRICTNEG:C_STRICTNEG + 384],
                                       ALU.add).then_inc(zm_ready, 1)

            chain = [0]

            def link(ins):
                chain[0] += 1
                ins.then_inc(pchain, 1)
                pool.wait_ge(pchain, chain[0])

            for l in range(NL):
                if KIND[l] != HYB:
                    roots(2)
                    if l == 2:
                        pool.wait_ge(rope_sin, 1)
                    pool.wait_ge(proj_ev, PROJ0[l + 1])
                    rotate(pool, link, l, True).then_inc(late_rope_done, 1)
                stick_masks(l)
                roots({HYB: 5, DIFF: 10}.get(KIND[l], 2))
            roots(2)

        @block.tensor
        def _(pe):
            pe.wait_ge(ident_loaded, 16)

            def to_t(q, src):
                for t in range(NT):
                    if q == 0:
                        pe.wait_ge(x_loaded[t], 16)
                    else:
                        pe.wait_ge(nat_ready, 2 * (q - 1) + t + 1)
                    for kq in range(2):
                        for k in range(4):
                            mm = pe.transpose(bank[2 * t + kq][:, k * P:(k + 1) * P],
                                              src[:, t, (4 * kq + k) * P:(4 * kq + k + 1) * P], ident)
                        mm.then_inc(turned, 1)

            def t_ready(q):
                pe.wait_ge(t_lo, 4 * (q + 1))

            def unit_ready(place):
                slot, turn = place
                pe.wait_ge(lo_ready[slot], turn * 2 + 2)

            def pool_means(l):
                pe.wait_ge(got["pool_m"], 16 * (l + 1))
                pe.wait_ge(proj_ev, PROJ0[l] + 1)
                pe.wait_ge(t_lo, 4 * (3 * l + 1))
                for gp in range(2):
                    for g in range(2):
                        c = (2 * gp + g) * HD
                        for t in range(NT):
                            mm = pe.matmul(bank[gp][0:HD, g * S:(g + 1) * S], h_in[:, t, c:c + HD],
                                           pool_m[:, t, 2 * gp + g, :], start=(t == 0), stop=(t == NT - 1))
                    mm.then_inc(pool_done, 1)

            def pool_map(l):
                pe.wait_ge(got["pool_w"], 16)
                pe.wait_ge(pool_copied, 2 * l + 2)
                for t in range(NT):
                    for g in range(4):
                        mm = pe.matmul(bank[2][:, t * D_POOL + g * HD:t * D_POOL + (g + 1) * HD],
                                       pool_t[:, g, t * P:(t + 1) * P], pool_w[:, l, g, :], start=True, stop=True)
                mm.then_inc(pool_out, 1)

            def project_tile(l, c, t):
                place = PLAN[l][0][c]
                slot = place[0]
                if t == 0:
                    unit_ready(place)
                    if c >= 4:
                        pe.wait_ge(proj_ev, PROJ0[l] + c - 3)
                if c == 0:
                    pe.wait_ge(t_lo, 12 * l + 2 * t + 2)
                hi, lo = as_k(whi[slot]), as_k(wlo[slot])
                for k in range(KT):
                    for i, (a, b) in enumerate(((xt_hi, hi), (xt_lo, hi), (xt_hi, lo))):
                        mm = pe.matmul(proj_bank(l, c)[:, t * UC:(t + 1) * UC], a[:, k, t * P:(t + 1) * P], b[:, k, :],
                                       start=(k == 0 and i == 0), stop=(k == KT - 1 and i == 2))
                if t == NT - 1:
                    mm.then_inc(used[slot], 1)

            def project(l):
                n = NPROJ[KIND[l]]
                for c in range(n - 2):
                    for t in range(NT):
                        project_tile(l, c, t)
                    if KIND[l] == HYB and c == 5:
                        pool_means(l)
                    if KIND[l] == HYB and c == 7:
                        pool_map(l)

            def down(place, at, a_hi, a_lo, first, last, turned_by=None):
                slot, _ = place
                hi, lo = as_rows(whi[slot]), as_rows(wlo[slot])
                for t in range(NT):
                    if turned_by is not None:
                        pe.wait_ge(t_lo, turned_by + 2 * t + 2)
                    for kk in range(2):
                        for i, (a, b) in enumerate(((a_hi, hi), (a_lo, hi), (a_hi, lo))):
                            for half in range(2):
                                mm = pe.matmul(bank[4 + 2 * t + half][:, :], a[:, at + kk, t * P:(t + 1) * P],
                                               b[:, kk, half * 512:(half + 1) * 512],
                                               start=first and kk == 0 and i == 0, stop=last and kk == 1 and i == 2)
                    if last and t == 0:
                        mm.then_inc(acc_done, 1)
                return mm

            def out_project(l):
                for o in range(4):
                    unit_ready(PLAN[l][1][o])
                    mm = down(PLAN[l][1][o], 2 * o, xt_hi, xt_lo, o == 0, o == 3,
                              4 * (3 * l + 1) if o == 0 else None)
                    mm.then_inc(used[PLAN[l][1][o][0]], 1)

            def up(place, b):
                slot, _ = place
                hi, lo = as_k(whi[slot]), as_k(wlo[slot])
                for f in range(2):
                    for k in range(KT):
                        for i, (a, w) in enumerate(((xt_hi, hi), (xt_lo, hi), (xt_hi, lo))):
                            mm = pe.matmul(bank[b][:, f * S:(f + 1) * S], w[:, k, f * P:(f + 1) * P], a[:, k, :],
                                           start=(k == 0 and i == 0), stop=(k == KT - 1 and i == 2))
                mm.then_inc(used[slot], 1)

            def router():
                pe.wait_ge(router_lo_s, 1)
                for t in range(NT):
                    for k in range(KT):
                        for i, (a, w) in enumerate(((xt_hi, router_hi), (xt_lo, router_hi), (xt_hi, router_lo),
                                                    (xt_lo, router_lo))):
                            mm = pe.matmul(bank[2][:, t * 8:(t + 1) * 8], a[:, k, t * P:(t + 1) * P], w[:, k, :],
                                           start=(k == 0 and i == 0), stop=(k == KT - 1 and i == 3))
                mm.then_inc(logits, 1)

            def rank():
                before = cst[:, C_STRICT:C_STRICT + P]
                pe.wait_ge(gates, 1)
                o = bank[3]
                pe.matmul(o[:, 0:8], before, chosen[:, 0, :], start=True, stop=True)
                pe.matmul(o[:, 8:16], ones, chosen[:, 0, :], start=True, stop=False)
                pe.matmul(o[:, 8:16], before, chosen[:, 1, :], start=False, stop=True)
                pe.matmul(o[:, 16:24], ones, chosen[:, 0, :], start=True, stop=False)
                pe.matmul(o[:, 16:24], ones, chosen[:, 1, :], start=False, stop=True).then_inc(ranked, 1)

            def gather(e, g):
                pe.wait_ge(perm_ready, e + 1)
                if g:
                    pe.wait_ge(gather_copied, e * 8 + g)
                src = (xn_hi, xn_lo)[g // 4]
                for k in range(2):
                    at = (2 * (g % 4) + k) * P
                    for t in range(NT):
                        mm = pe.matmul(bank[3][:, k * S:(k + 1) * S], src[:, t, at:at + P], perm[:, t, :],
                                       start=(t == 0), stop=(t == 1))
                mm.then_inc(gathered, 1)

            def turn_perm(e):
                pe.wait_ge(added, e * 4 + 4)
                for st in range(NT):
                    for t in range(NT):
                        mm = pe.transpose(bank[3][:, st * S + t * P:st * S + (t + 1) * P],
                                          perm[:, t, st * P:(st + 1) * P].bitcast(F32), ident)
                mm.then_inc(perm_turned, 1)

            def scatter(e, wide):
                pe.wait_ge(ye_lo_ready, e * 4 + 4)
                pe.wait_ge(gather_copied, e * 8 + 16)
                for t in range(NT):
                    for half in range(2):
                        if t:
                            pe.wait_ge(added, e * 4 + (5 + half))
                        for st in range(2 if wide else 1):
                            for i, part in enumerate((ye_hi, ye_lo)):
                                mm = pe.matmul(bank[2 + half][:, :], perm_t[:, st, t * P:(t + 1) * P],
                                               part[:, st, half * 512:(half + 1) * 512],
                                               start=(st == 0 and i == 0), stop=(st == wide and i == 1))
                        mm.then_inc(scattered, 1)

            def rise(e_odd, wide, place, b):
                x_hi, x_lo = (odd_hi, odd_lo) if e_odd else (xt_hi, xt_lo)
                unit_ready(place)
                slot = place[0]
                hi, lo = as_k(whi[slot]), as_k(wlo[slot])
                for t in range(2 if wide else 1):
                    for k in range(KT):
                        for i, (a, w) in enumerate(((x_hi, hi), (x_lo, hi), (x_hi, lo))):
                            mm = pe.matmul(bank[b][:, t * UC:(t + 1) * UC], a[:, k, t * P:(t + 1) * P],
                                           w[:, k, :], start=(k == 0 and i == 0), stop=(k == KT - 1 and i == 2))
                mm.then_inc(used[slot], 1)

            def rise_by(n_tokens, odd, place, b):
                with pe.If(n_tokens < P + 1):
                    rise(odd, False, place, b)
                with pe.Else():
                    rise(odd, True, place, b)

            def expert(e, odd, wide, n_next):
                hb = GRP0[1]
                (sg_, tg), (su, tu), (sd, td) = PLAN[1][2]
                tiles = 2 if wide else 1

                def turn_hidden(n):
                    pe.wait_ge(h_mid, n + (hb + 1))
                    for f in range(2):
                        for t in range(tiles):
                            mm = pe.transpose(bank[2][:, f * S + t * P:f * S + (t + 1) * P],
                                              h_f[:, 0, t * UC + f * P:t * UC + (f + 1) * P], ident)
                    mm.then_inc(h_turned, 1)

                def fold(n, first=False, stop=False):
                    unit_ready((sd, n + td))
                    pe.wait_ge(hl_ready, n + (hb + 1))
                    hi, lo = as_rows(whi[sd]), as_rows(wlo[sd])
                    for t in range(tiles):
                        for kk in range(2):
                            for i, (a, w) in enumerate(((h_hi, hi), (h_lo, hi), (h_hi, lo))):
                                for half in range(2):
                                    mm = pe.matmul(bank[4 + 2 * t + half][:, :], a[:, 0, kk, t * P:(t + 1) * P],
                                                   w[:, kk, half * 512:(half + 1) * 512],
                                                   start=first and kk == 0 and i == 0,
                                                   stop=stop and kk == 1 and i == 2)
                    mm.then_inc(used[sd], 1)

                def gate(n):
                    pe.wait_ge(act_done, n + hb)
                    rise(odd, wide, (sg_, n + tg), 0)

                n0 = e * GE
                pe.wait_ge(added, e * 4 + 3)
                turn_hidden(n0)
                rise(odd, wide, (su, n0 + (tu + 1)), 1)
                fold(n0, first=True)
                for i in range(2, 7):
                    gate(n0 + i)
                    turn_hidden(n0 + (i - 1))
                    if i == 2:
                        turn_perm(e)
                    else:
                        if i == 3:
                            pe.wait_ge(perm_t_ready, e + 1)
                        gather(e + 1, 2 * (i - 3))
                    rise(odd, wide, (su, n0 + (tu + i)), 1)
                    fold(n0 + (i - 1))
                    if i > 2:
                        gather(e + 1, 2 * (i - 3) + 1)
                with pe.Fori(7, GE) as i:
                    gate(n0 + i)
                    turn_hidden(n0 + i - 1)
                    rise(odd, wide, (su, n0 + i + tu), 1)
                    fold(n0 + i - 1)
                n1 = n0 + GE
                if n_next is None:
                    turn_hidden(n1 - 1)
                    fold(n1 - 1, stop=True)
                else:
                    pe.wait_ge(gather_copied, e * 8 + 16)
                    pe.wait_ge(act_done, n1 + hb)
                    rise_by(n_next, not odd, (sg_, n1 + tg), 0)
                    turn_hidden(n1 - 1)
                    rise_by(n_next, not odd, (su, n1 + tu), 1)
                    fold(n1 - 1, stop=True)
                    pe.wait_ge(act_done, n1 + (hb + 1))
                    rise_by(n_next, not odd, (sg_, n1 + (tg + 1)), 0)
                scatter(e, wide)

            def moe():
                router()
                rank()
                pe.wait_ge(xn_lo_ready, 1)
                pe.wait_ge(counted, 1)
                for g in range(8):
                    gather(0, g)
                hb = GRP0[1]
                (sg_, tg), (su, tu), _ = PLAN[1][2]

                def tokens_of(e):
                    return pe.value_load(count[0:1, bass.ds(e, 1)], min_val=0, max_val=S)

                def either(e, odd, last=False):
                    n = tokens_of(e)
                    n_next = None if last else tokens_of(e + 1)
                    with pe.If(n < P + 1):
                        expert(e, odd, False, n_next)
                    with pe.Else():
                        expert(e, odd, True, n_next)

                n = tokens_of(0)
                pe.wait_ge(gather_copied, 8)
                rise_by(n, False, (sg_, tg), 0)
                rise_by(n, False, (su, tu), 1)
                pe.wait_ge(act_done, hb + 1)
                rise_by(n, False, (sg_, tg + 1), 0)
                with pe.Fori(0, N_EXP // 2 - 1) as pair:
                    for odd in range(2):
                        either(pair * 2 + odd, odd)
                either(N_EXP - 2, 0)
                either(N_EXP - 1, 1, last=True)

            def swiglu(l):
                g, hb = groups(l), GRP0[l]
                (sg_, tg), (su, tu), (sd, td) = PLAN[l][2]

                def pair(i):
                    unit_ready((sg_, i + tg))
                    if not isinstance(i, int) or i > 0:
                        pe.wait_ge(h_mid, i + hb)
                    up((sg_, None), 0)
                    unit_ready((su, i + tu))
                    up((su, None), 1)

                def fold(i, first=False, last=False):
                    unit_ready((sd, i + td))
                    pe.wait_ge(hl_ready, i + (hb + 1))
                    down((sd, None), 0, h_hi[:, 0], h_lo[:, 0], first, last).then_inc(used[sd], 1)

                pair(0)
                pair(1)
                fold(0, first=True)
                with pe.Fori(2, g) as i:
                    pair(i)
                    fold(i - 1)
                fold(g - 1, last=True)

            def mlp(l):
                g, hb = groups(l), GRP0[l]
                (s0, t0), (s1, t1), (sd, td) = PLAN[l][2]
                us, ut = (s0, s1), (t0, t1)

                def rise(par, turn, i):
                    unit_ready((us[par], turn + ut[par]))
                    if not isinstance(i, int) or i >= 2:
                        pe.wait_ge(act_done, i + (hb - 1))
                    up((us[par], None), par)

                def fold(par, i, first=False, last=False):
                    unit_ready((sd, i + td))
                    pe.wait_ge(hl_ready, i + (hb + 1))
                    down((sd, None), 0, h_hi[:, par], h_lo[:, par], first, last).then_inc(used[sd], 1)

                rise(0, 0, 0)
                rise(1, 0, 1)
                fold(0, 0, first=True)
                with pe.Fori(1, g // 2) as j:
                    rise(0, j, j * 2)
                    fold(1, j * 2 - 1)
                    rise(1, j, j * 2 + 1)
                    fold(0, j * 2)
                fold(1, g - 1, last=True)

            def turn_heads(l, j, qcol, kcol, g):
                if g >= 2:
                    pe.wait_ge(qk_ready, g - 1)
                for i, col in enumerate((qcol, kcol)):
                    for t in range(NT):
                        mm = pe.transpose(bank[2 + g % 2][0:HD, (2 * i + t) * P:(2 * i + t + 1) * P],
                                          h_in[:, t, col:col + HD], ident)
                mm.then_inc(qk_turned, 1)

            def soft_heads(l):
                kind = KIND[l]
                n, dv, og = NSOFT[kind], VW[kind], OGRP[kind]
                for i in range(n + 4):
                    if 1 <= i <= 3:
                        project_tile(l, NPROJ[kind] - 2 + i // 2, i % 2)
                    if i == 4:
                        pe.wait_ge(proj_ev, PROJ0[l + 1])
                    if kind != HYB and i == LATE_HEAD[kind]:
                        pe.wait_ge(late_rope_done, l - 1)
                    if i < n:
                        turn_heads(l, i, *head_cols(l, i)[0:2], HEAD0[l] + i)
                    j = i - 1
                    if 0 <= j < n:
                        g = HEAD0[l] + j
                        pe.wait_ge(qk_ready, g + 1)
                        if g >= 2:
                            pe.wait_ge(z_read, g - 1)
                        b = bank[g % 2]
                        q = qk[:, g % 4]
                        plain = kind != HYB
                        pe.matmul(b[:, 0:P], q[:, 0:P], q[:, 2 * P:3 * P], start=True, stop=plain)
                        if not plain:
                            pe.wait_ge(got["toep"], 16 * (l + 1))
                            pe.matmul(b[:, 0:P], flip8, toep[:, j, P:2 * P], start=False, stop=True)
                        mm = pe.matmul(b[:, P:3 * P], q[:, P:2 * P], q[:, 2 * P:4 * P], start=True, stop=plain)
                        if not plain:
                            mm = pe.matmul(b[:, P:3 * P], flip8, toep[:, j, :], start=False, stop=True)
                        mm.then_inc(scored, 1)
                    j = i - 3
                    if 0 <= j < n:
                        s = SOFT0[l] + j
                        pe.wait_ge(p_ready, s + 1)
                        if s >= 2:
                            pe.wait_ge(pt_ready, s - 1)
                        for m in range(3):
                            mm = pe.transpose(bank[4 + s % 2][:, m * P:(m + 1) * P],
                                              z[:, s % 4, m * P:(m + 1) * P], ident)
                        mm.then_inc(pt_done, 1)
                    j = i - 4
                    if 0 <= j < n:
                        s = SOFT0[l] + j
                        pe.wait_ge(pt_ready, s + 1)
                        values(l, j, pt[:, s % 4], dv, og, j, head_cols(l, j)[2])

            def values(l, j, w, dv, og, order, vcol):
                o = OG0[l] + order // og
                if order % og == 0 and o >= 2:
                    pe.wait_ge(o_read, o - 1)
                b = bank[6 + o % 2]
                at = (order % og) * dv
                half = og * dv
                pe.matmul(b[:, at:at + dv], w[:, 0:P], h_in[:, 0, vcol:vcol + dv], start=True, stop=True)
                pe.matmul(b[:, half + at:half + at + dv], w[:, P:2 * P], h_in[:, 0, vcol:vcol + dv],
                          start=True, stop=False)
                pe.matmul(b[:, half + at:half + at + dv], w[:, 2 * P:3 * P], h_in[:, 1, vcol:vcol + dv],
                          start=False, stop=True).then_inc(pv_done, 1)

            def stick_heads(l):
                n = NSTICK[HYB]

                def score(h):
                    g = HEAD0[l] + NSOFT[HYB] + h
                    pe.wait_ge(qk_ready, g + 1)
                    pe.wait_ge(z_read, g - 1)
                    q = qk[:, g % 4]
                    pe.matmul(bank[g % 2][:, 0:2 * P], q[:, 2 * P:3 * P], q[:, 0:2 * P], start=True, stop=True)
                    pe.matmul(bank[g % 2][:, 2 * P:3 * P], q[:, 3 * P:4 * P], q[:, P:2 * P],
                              start=True, stop=True).then_inc(scored, 1)

                def sum_up(h):
                    b = STICK0[l] + h
                    pe.wait_ge(sp_ready, b + 1)
                    if h >= 2:
                        pe.wait_ge(arg_ready, b - 1)
                    o = bank[4 + b % 2]
                    pe.matmul(o[:, 0:2 * P], tri, sps[:, b % 2, 0:2 * P], start=True, stop=False,
                              skip_group_check=True)
                    pe.matmul(o[:, P:2 * P], ones, sps[:, b % 2, 2 * P:3 * P], start=False, stop=True,
                              skip_group_check=True)
                    pe.matmul(o[:, 2 * P:3 * P], tri, sps[:, b % 2, 2 * P:3 * P], start=True,
                              stop=True).then_inc(c_done, 1)

                for p in range(0, n + 2, 2):
                    if p < n:
                        for h in (p, p + 1):
                            turn_heads(l, h, *stick_cols(h)[0:2], HEAD0[l] + NSOFT[HYB] + h)
                        for h in (p, p + 1):
                            score(h)
                    if p >= 2:
                        for h in (p - 2, p - 1):
                            sum_up(h)
                        for h in (p - 2, p - 1):
                            b = STICK0[l] + h
                            pe.wait_ge(w_ready, b + 1)
                            values(l, h, zm[:, b % 2], HD, OGRP[HYB], NSOFT[HYB] + h, stick_cols(h)[2])

            for l in range(NL):
                to_t(3 * l, x if KIND[l] == HYB else y)
                project(l)
                project_tile(l, NPROJ[KIND[l]] - 2, 0)
                pe.wait_ge(proj_ev, PROJ0[l + 1] - 2)
                if l == 0:
                    pe.wait_ge(cst_loaded, 16)
                if KIND[l] == HYB:
                    pe.wait_ge(pool_read, l + 1)
                else:
                    pe.wait_ge(rope_done, l - 1)
                soft_heads(l)
                if KIND[l] == HYB:
                    stick_heads(l)
                to_t(3 * l + 1, y)
                out_project(l)
                to_t(3 * l + 2, x if KIND[l] == HYB else y)
                t_ready(3 * l + 2)
                if l == 1:
                    moe()
                else:
                    (swiglu if KIND[l] == HYB else mlp)(l)

        @block.scalar
        def _(act):
            chain = [0]

            def link(ins):
                chain[0] += 1
                ins.then_inc(achain, 1)
                act.wait_ge(achain, chain[0])

            def hi(place, halves=(0, 1)):
                slot, turn = place
                if not isinstance(turn, int) or turn > 0:
                    act.wait_ge(used[slot], turn)
                act.wait_ge(loaded[slot], turn * 16 + 16)
                for half in halves:
                    act.activation(whi[slot][:, half * 1024:(half + 1) * 1024], raw[slot][:, half * 1024:(half + 1) * 1024],
                                   ACT.Copy).then_inc(hi_ready[slot], 1)

            def to_t(q):
                for n in range(4):
                    act.wait_ge(turned, 4 * q + n + 1)
                    t, kq = divmod(n, 2)
                    act.activation(xt_hi[:, 4 * kq:4 * kq + 4, t * P:(t + 1) * P],
                                   bank[n][:, :].rearrange("p (k s) -> p k s", k=4), ACT.Copy).then_inc(t_hi, 1)

            def evacuate(l, c):
                if KIND[l] != SWA:
                    u = ORDER[KIND[l]][c]
                    act.wait_ge(used[PLAN[l][0][c][0]], PLAN[l][0][c][1] + 1)
                    act.activation(h_in[:, :, u * UC:(u + 1) * UC],
                                   proj_bank(l, c)[:, :].rearrange("p (t c) -> p t c", t=NT),
                                   ACT.Copy).then_inc(proj_ev, 1)

            def project(l):
                proj = PLAN[l][0]
                for c in range(len(proj) - 2):
                    evacuate(l, c)
                    if c + 3 < len(proj):
                        hi(proj[c + 3])
                    if KIND[l] == HYB and c == 5:
                        for gp in range(2):
                            act.wait_ge(pool_done, 2 * l + gp + 1)
                            act.activation(pool_t[:, 2 * gp:2 * gp + 2, :],
                                           bank[gp][0:HD, :].rearrange("p (g s) -> p g s", g=2),
                                           ACT.Copy).then_inc(pool_copied, 1)
                if l == 0:
                    setup()

            def copy_qk(g):
                act.wait_ge(qk_turned, g + 1)
                if g >= 4:
                    act.wait_ge(scored, g - 3)
                act.activation(qk[:, g % 4], bank[2 + g % 2][0:HD, :], ACT.Copy).then_inc(qk_ready, 1)

            def soft_heads(l):
                kind = KIND[l]
                n = NSOFT[kind]
                for i in range(n + (3 if kind == DIFF else 2)):
                    if i in (1, 3):
                        evacuate(l, NPROJ[kind] - 2 + i // 2)
                    if i < n:
                        copy_qk(HEAD0[l] + i)
                    j = i - 2
                    if 0 <= j < n:
                        s = SOFT0[l] + j
                        act.wait_ge(nmx_ready, s + 1)
                        ins = act.activation(z[:, s % 4, 0:P], z[:, s % 4, 0:P], ACT.Exp, bias=nmx[:, 0, j:j + 1],
                                             accum_out=sums[:, 0, j:j + 1])
                        ins = act.activation(z[:, s % 4, P:3 * P], z[:, s % 4, P:3 * P], ACT.Exp,
                                             bias=nmx[:, 1, j:j + 1], accum_out=sums[:, 1, j:j + 1])
                        if kind == SWA:
                            ins = act.activation(esink[:, :, j], nmx[:, :, j], ACT.Exp, bias=sinks[:, j:j + 1])
                        ins.then_inc(p_ready, 1)
                    j = i - 3
                    if 0 <= j < n and kind == DIFF:
                        s = SOFT0[l] + j
                        act.wait_ge(pt_done, s + 1)
                        act.activation(pt[:, s % 4], bank[4 + s % 2][:, 0:384], ACT.Copy).then_inc(pt_ready, 1)
                    for place, half in out_halves(l, i):
                        hi(place, (half,))

            def stick_heads(l):
                n = NSTICK[HYB]

                def weights(h):
                    b = STICK0[l] + h
                    act.wait_ge(arg_ready, b + 1)
                    act.activation(zm[:, b % 2], zm[:, b % 2], ACT.Exp).then_inc(w_ready, 1)

                for h in range(2):
                    copy_qk(HEAD0[l] + NSOFT[HYB] + h)
                for p in range(0, n, 2):
                    for h in (p, p + 1):
                        b = STICK0[l] + h
                        act.wait_ge(z_read, HEAD0[l] + NSOFT[HYB] + h + 1)
                        if h >= 2:
                            act.wait_ge(sp_ready, b - 1)
                        ins = act.activation(es[:, b % 2], zs[:, b % 2], ACT.Abs)
                    link(ins)
                    chain[0] += 1
                    act.activation(es[:], es[:], ACT.Exp, scale=-1.0).then_inc(achain, 1)
                    if p:
                        for h in (p - 2, p - 1):
                            weights(h)
                    if p + 2 < n:
                        for h in (p + 2, p + 3):
                            copy_qk(HEAD0[l] + NSOFT[HYB] + h)
                    for h in (p, p + 1):
                        b = STICK0[l] + h
                        if h == p:
                            act.wait_ge(achain, chain[0])
                        act.activation(es[:, b % 2], es[:, b % 2], ACT.Ln, bias=cst[:, C_ONECOL:C_ONECOL + 1]).then_inc(
                            sp_log, 1)
                for h in (n - 2, n - 1):
                    weights(h)

            def hidden_hi(par, i, hb, sd, td, back):
                act.wait_ge(h_mid, i + (hb + 1))
                if not isinstance(i, int) or i >= back:
                    act.wait_ge(used[sd], i + (td + 1 - back))
                act.activation(h_hi[:, par], h_f[:, par, :].rearrange("p (f s) -> p f s", f=2), ACT.Copy).then_inc(hh_ready, 1)

            def swiglu(l):
                g, hb = groups(l), GRP0[l]
                (sg_, tg), (su, tu), (sd, td) = PLAN[l][2]

                def silu(i):
                    act.wait_ge(used[su], i + (tu + 1))
                    if not isinstance(i, int) or i > 0:
                        act.wait_ge(h_mid, i + hb)
                    act.activation(sg[:], bank[0][:, :], ACT.Silu).then_inc(act_done, 1)

                hi((sg_, tg + 1))
                silu(0)
                hi((su, tu + 1))
                hidden_hi(0, 0, hb, sd, td, 1)
                with act.Fori(1, g - 1) as i:
                    hi((sg_, i + (tg + 1)))
                    silu(i)
                    hi((su, i + (tu + 1)))
                    hidden_hi(0, i, hb, sd, td, 1)
                    hi((sd, i + td))
                silu(g - 1)
                hidden_hi(0, g - 1, hb, sd, td, 1)
                hi((sd, td + g - 1))

            def moe():
                hb = GRP0[1]
                (sg_, tg), (su, tu), (sd, td) = PLAN[1][2]

                def take_tokens(e, odd, g):
                    xt = (odd_hi, odd_lo)[g // 4] if odd else (xt_hi, xt_lo)[g // 4]
                    act.wait_ge(gathered, e * 8 + (g + 1))
                    act.activation(xt[:, 2 * (g % 4):2 * (g % 4) + 2, :],
                                   bank[3][:, :].rearrange("p (k s) -> p k s", k=2), ACT.Copy).then_inc(
                        gather_copied, 1)

                def take_perm(e):
                    act.wait_ge(perm_turned, e + 1)
                    act.activation(perm_t[:], bank[3][:, :].rearrange("p (a s) -> p a s", a=2), ACT.Copy).then_inc(
                        perm_t_ready, 1)

                def group(n, between=None, before_down=None, after=None, last=False):
                    if not last:
                        hi((sg_, n + (tg + 1)))
                    act.wait_ge(used[sg_], n + (tg + 1))
                    act.wait_ge(h_mid, n + hb)
                    act.activation(sg[:], bank[0][:, :], ACT.Silu).then_inc(act_done, 1)
                    if between is not None:
                        between()
                    if not last:
                        hi((su, n + (tu + 1)))
                    if before_down is not None:
                        before_down()
                    hi((sd, n + td))
                    if after is not None:
                        after()
                    act.wait_ge(h_turned, n + 1)
                    act.activation(h_hi[:, 0], bank[2][:, :].rearrange("p (f s) -> p f s", f=2), ACT.Copy).then_inc(
                        hh_ready, 1)

                def give_result(e):
                    act.wait_ge(used[sd], e * GE + (td + GE))
                    for b in range(4):
                        act.activation(ye_hi[:, b // 2, (b % 2) * 512:(b % 2 + 1) * 512], bank[4 + b][:, :],
                                       ACT.Copy).then_inc(ye_hi_ready, 1)

                def expert(e, odd, last=False):
                    n0 = e * GE
                    group(n0 + 1)
                    group(n0 + 2, between=lambda: take_perm(e))
                    for i in range(3, 7):
                        group(n0 + i, between=lambda: take_tokens(e + 1, not odd, 2 * (i - 3)),
                              after=lambda: take_tokens(e + 1, not odd, 2 * (i - 3) + 1))
                    with act.Fori(7, GE - last) as i:
                        group(n0 + i)
                    if last:
                        group(n0 + GE - 1, last=True)
                        give_result(e)
                    else:
                        group(n0 + GE, before_down=lambda: give_result(e))

                act.wait_ge(gates, 1)
                act.activation(silu_warm[:], topf[:, 0, 3:4], ACT.Silu)
                for g in range(8):
                    take_tokens(0, False, g)
                group(0)
                with act.Fori(0, N_EXP // 2 - 1) as pair:
                    expert(pair * 2, False)
                    expert(pair * 2 + 1, True)
                expert(N_EXP - 2, False)
                expert(N_EXP - 1, True, last=True)

            def mlp(l):
                g, hb = groups(l), GRP0[l]
                (s0, t0), (s1, t1), (sd, td) = PLAN[l][2]
                us, ut = (s0, s1), (t0, t1)

                def relu(par, turn, i):
                    act.wait_ge(used[us[par]], turn + (ut[par] + 1))
                    if not isinstance(i, int) or i > 0:
                        act.wait_ge(h_mid, i + hb)
                    act.activation(sg[:], bank[par][:, :], ACT.Relu).then_inc(act_done, 1)

                relu(0, 0, 0)
                hi((s0, t0 + 1))
                hidden_hi(0, 0, hb, sd, td, 2)
                with act.Fori(0, 6) as j:
                    relu(1, j, j * 2 + 1)
                    hi((s1, j + (t1 + 1)))
                    hidden_hi(1, j * 2 + 1, hb, sd, td, 2)
                    hi((sd, j * 2 + (td + 1)))
                    relu(0, j + 1, j * 2 + 2)
                    hi((s0, j + (t0 + 2)))
                    hidden_hi(0, j * 2 + 2, hb, sd, td, 2)
                    hi((sd, j * 2 + (td + 2)))
                for i in range(g - 3, g):
                    relu(i % 2, i // 2, i)
                    if i == g - 3:
                        hi((s1, t1 + g // 2 - 1))
                    hidden_hi(i % 2, i, hb, sd, td, 2)
                    hi((sd, td + i))

            def setup():
                act.wait_ge(got["router"], 16)
                act.activation(router_hi[:], router_w[:], ACT.Copy).then_inc(router_hi_s, 1)
                act.wait_ge(lam_dot, 1)
                act.activation(lam[:, 4:8], lam[:, 0:4], ACT.Exp).then_inc(lam_exp, 1)
                act.wait_ge(rope_arg, 1)
                act.activation(cos_sin[:], rope_f[:, 4:6], ACT.Sin).then_inc(rope_sin, 1)

            squares = [0]

            def square():
                squares[0] += 1
                act.wait_ge(x_summed, squares[0])
                act.activation(y[:, 1], x[:, 1], ACT.Square, accum_out=sq[:, 1, 0:1]).then_inc(squared, 1)

            for l in range(NL):
                proj, outp, first = PLAN[l]
                to_t(3 * l)
                if l == 0:
                    for c in range(2):
                        hi(proj[c])
                hi(proj[2])
                project(l)
                soft_heads(l)
                if KIND[l] == HYB:
                    stick_heads(l)
                to_t(3 * l + 1)
                hi(outp[3])
                for i in range(2):
                    hi(first[i])
                if l == 1:
                    act.wait_ge(nat_ready, 2 * (3 * l + 1) + 2)
                    for t in range(NT):
                        ins = act.activation(xn_hi[:, t], x[:, t], ACT.Copy)
                    ins.then_inc(xn_hi_ready, 1)
                if KIND[l] != HYB:
                    square()
                to_t(3 * l + 2)
                if l != 1:
                    hi(first[2])
                    (swiglu if KIND[l] == HYB else mlp)(l)
                else:
                    act.wait_ge(gap, 1)
                    act.activation(topf[:, :, 4:5], topf[:, :, 3:4], ACT.Exp).then_inc(gap_exp, 1)
                    moe()
                if l + 1 < NL:
                    for c in range(2):
                        hi(PLAN[l + 1][0][c])
                if l >= 1:
                    square()

        @block.vector
        def _(dve):
            chain = [0]
            asked = [0]
            gains_at = [0]

            def link(ins):
                chain[0] += 1
                ins.then_inc(dchain, 1)
                dve.wait_ge(dchain, chain[0])

            def lo(place, halves=(0, 1)):
                slot, turn = place
                for half in halves:
                    h = slice(half * 1024, (half + 1) * 1024)
                    dve.wait_ge(hi_ready[slot], turn * 2 + half + 1)
                    dve.tensor_tensor(wlo[slot][:, h], raw[slot][:, h], whi[slot][:, h].bitcast(F32),
                                      ALU.subtract).then_inc(lo_ready[slot], 1)

            def to_t(q):
                for n in range(4):
                    dve.wait_ge(t_hi, 4 * q + n + 1)
                    t, kq = divmod(n, 2)
                    dve.tensor_tensor(xt_lo[:, 4 * kq:4 * kq + 4, t * P:(t + 1) * P],
                                      bank[n][:, :].rearrange("p (k s) -> p k s", k=4),
                                      xt_hi[:, 4 * kq:4 * kq + 4, t * P:(t + 1) * P].bitcast(F32),
                                      ALU.subtract).then_inc(t_lo, 1)

            def ask_root(src, scale, eps, w):
                r = asked[0]
                asked[0] += 1
                dve.tensor_scalar(var[:, r % 8, 0:w], src, scale, eps, ALU.mult, ALU.add).then_inc(var_ready, 1)
                return r

            def root(r):
                dve.wait_ge(root_ready, r + 1)
                return rstd[:, r % 8]

            def next_gain():
                u = gains_at[0]
                gains_at[0] += 1
                dve.wait_ge(gain_loaded[u % 3], 16 * (u // 3 + 1))
                return gain[u % 3]

            def acc_ready(acc, t):
                if t == 0:
                    dve.wait_ge(acc_done, acc + 1 - (acc > 3))
                else:
                    slot, turn = LAST_UNIT[acc]
                    dve.wait_ge(used[slot], turn + 1)

            def residual_norm(acc, to_turn=True):
                asks = []
                g, b = next_gain(), next_gain()

                def centre(t):
                    link(dve.scalar_tensor_tensor(out=x[:, t], in0=x[:, t], scalar=mv[:, t, 0:1], in1=g[:],
                                                  op0=ALU.subtract, op1=ALU.mult))

                def finish(t):
                    r = root(asks[t])
                    ins = dve.scalar_tensor_tensor(out=x[:, t], in0=x[:, t], scalar=r[:, 0:1], in1=b[:],
                                                   op0=ALU.mult, op1=ALU.add)
                    if to_turn:
                        ins.then_inc(nat_ready, 1)
                    return ins

                for t in range(NT):
                    if acc != 3:
                        acc_ready(acc, t)
                    for half in range(2):
                        c = slice(half * 512, (half + 1) * 512)
                        ins = dve.scalar_tensor_tensor(out=x[:, t, c], in0=x[:, t, c], scalar=ALPHA,
                                                       in1=y[:, t, c] if acc == 3 else bank[4 + 2 * t + half][:, :],
                                                       op0=ALU.mult, op1=ALU.add)
                    link(ins)
                    for half in range(2):
                        ins = dve.bn_stats(stats[:, t, half], x[:, t, half * 512:(half + 1) * 512])
                    link(ins)
                    link(dve.bn_aggr(mv[:, t], stats[:, t]))
                    asks.append(ask_root(mv[:, t, 1:2], 1.0, LN_EPS, 1))
                    centre(t)
                    ins = finish(t)
                if to_turn:
                    nat[0] += 2
                    dve.wait_ge(nat_ready, nat[0])
                else:
                    link(ins)
                gain_done(2)

            nat = [0]

            def gain_done(n):
                for _ in range(n):
                    dve.engine_nop().then_inc(gain_used, 1)

            def rms_norm(acc=None, final=False):
                asks = []
                g = next_gain()

                def add(t):
                    acc_ready(acc, t)
                    for half in range(2):
                        c = slice(half * 512, (half + 1) * 512)
                        ins = dve.tensor_tensor(x[:, t, c], x[:, t, c], bank[4 + 2 * t + half][:, :], ALU.add)
                    return ins

                def scale(t):
                    r = root(asks[t])
                    dve.scalar_tensor_tensor(out=y[:, t], in0=x[:, t], scalar=r[:, 0:1], in1=g[:], op0=ALU.mult,
                                             op1=ALU.mult).then_inc(y_done if final else nat_ready, 1)

                if acc is not None:
                    link(add(0))
                link(dve.tensor_tensor_reduce(y[:, 0], x[:, 0], x[:, 0], 1.0, 0.0, ALU.mult, ALU.add, sq[:, 0, 0:1]))
                asks.append(ask_root(sq[:, 0, 0:1], 1.0 / D, NORM_EPS, 1))
                ins = dve.engine_nop() if acc is None else add(1)
                ins.then_inc(x_summed, 1)
                squares[0] += 1
                if acc is not None:
                    dve.wait_ge(x_summed, squares[0])
                scale(0)
                dve.wait_ge(squared, squares[0])
                asks.append(ask_root(sq[:, 1, 0:1], 1.0 / D, NORM_EPS, 1))
                scale(1)
                if not final:
                    nat[0] += 2
                    dve.wait_ge(nat_ready, nat[0])
                    gain_done(1)

            squares = [0]

            def setup():
                dve.wait_ge(got["rel"], 16)
                dve.tensor_copy(rel_rev[:, 127:REVW], rel_in[:, REL - 1::-1]).then_inc(rel_done, 1)
                dve.tensor_copy(rel_rev[:, 0:127], rel_in[:, REL - 1:REL].broadcast_to([12, 127])).then_inc(rel_done, 1)
                dve.wait_ge(router_hi_s, 1)
                dve.tensor_tensor(router_lo[:], router_w[:], router_hi[:].bitcast(F32), ALU.subtract).then_inc(
                    router_lo_s, 1)
                dve.wait_ge(got["lam"], 64)
                for i in range(2):
                    for d in range(2):
                        ins = dve.tensor_tensor_reduce(lam_in[:, 2 * i, d], lam_in[:, 2 * i, d], lam_in[:, 2 * i + 1, d],
                                                       1.0, 0.0, ALU.mult, ALU.add, lam[:, 2 * i + d:2 * i + d + 1])
                ins.then_inc(lam_dot, 1)
                dve.wait_ge(got["pos"], 16)
                link(dve.tensor_copy(rope_f[:, 0, :, 0], pos_i[:]))
                for t in range(NT):
                    ins = dve.tensor_scalar(rope_f[:, 1, t], cst[:, C_INV:C_INV + 8], rope_f[:, 0, t, 0:1], None, ALU.mult)
                link(ins)
                link(dve.tensor_scalar(rope_k[:], rope_f[:, 1], 1.0 / (2 * math.pi), None, ALU.mult))
                link(dve.tensor_copy(rope_f[:, 2], rope_k[:]))
                link(dve.scalar_tensor_tensor(out=rope_f[:, 3], in0=rope_f[:, 2], scalar=-TWO_PI_1, in1=rope_f[:, 1],
                                              op0=ALU.mult, op1=ALU.add))
                link(dve.scalar_tensor_tensor(out=rope_f[:, 3], in0=rope_f[:, 2], scalar=-TWO_PI_2, in1=rope_f[:, 3],
                                              op0=ALU.mult, op1=ALU.add))
                link(dve.tensor_scalar(rope_f[:, 4], rope_f[:, 3], math.pi / 2, None, ALU.add))
                link(dve.tensor_scalar(rope_f[:, 1], rope_f[:, 4], math.pi, -2 * math.pi, ALU.is_gt, ALU.mult))
                link(dve.tensor_tensor(rope_f[:, 4], rope_f[:, 4], rope_f[:, 1], ALU.add))
                link(dve.tensor_scalar(rope_f[:, 4], rope_f[:, 4], PI_SAFE, -PI_SAFE, ALU.min, ALU.max))
                dve.tensor_scalar(rope_f[:, 5], rope_f[:, 3], PI_SAFE, -PI_SAFE, ALU.min, ALU.max).then_inc(rope_arg, 1)
                dve.wait_ge(lam_exp, 1)
                for l, d in DIFF_SLOT.items():
                    link(dve.tensor_tensor(lam[:, 8 + d:9 + d], lam[:, 6 + d:7 + d], lam[:, 4 + d:5 + d], ALU.subtract))
                    link(dve.tensor_scalar(lam[:, 10 + d:11 + d], lam[:, 8 + d:9 + d], -LAMBDA_INIT[l], None, ALU.add))
                dve.wait_ge(got["subg"], 16)
                for l, d in DIFF_SLOT.items():
                    link(dve.tensor_scalar(subg[:, d], subg[:, d], 1.0 - LAMBDA_INIT[l], None, ALU.mult))

            def add_bias(l, c):
                u = ORDER[KIND[l]][c]
                slot, turn = PLAN[l][0][c]
                dve.wait_ge(used[slot], turn + 1)
                dve.tensor_tensor(h_in[:, :, u * UC:(u + 1) * UC],
                                  proj_bank(l, c)[:, :].rearrange("p (t c) -> p t c", t=NT),
                                  swa_bias[:, u * UC:(u + 1) * UC].rearrange("p c -> p () c").broadcast_to(
                                      [P, NT, UC]), ALU.add).then_inc(proj_ev, 1)

            def finish_group(l, order, soft):
                kind = KIND[l]
                og, dv = OGRP[kind], VW[kind]
                if order % og != og - 1:
                    return
                gi = order // og
                o = OG0[l] + gi
                b = bank[6 + o % 2]
                j0 = order - og + 1
                dve.wait_ge(pv_done, HEAD0[l] + order + 1)
                src = b[:, 0:NT * og * dv].rearrange("p (t h c) -> p t h c", t=NT, c=dv)
                if not soft:
                    at = D_POOL + D_CHUNK + (j0 - NSOFT[HYB]) * HD
                    link(dve.tensor_copy(y[:, :, at:at + og * HD].rearrange("p t (h c) -> p t h c", c=HD), src))
                else:
                    j = slice(j0, j0 + og)
                    if kind == SWA:
                        link(dve.tensor_tensor(sums[:, :, j], sums[:, :, j], esink[:, :, j], ALU.add))
                    link(dve.reciprocal(rinv[:, :, j], sums[:, :, j]))
                    if kind == DIFF:
                        d = DIFF_SLOT[l]
                        link(dve.tensor_scalar(rinv[:, :, j0 + 1:j0 + 2], rinv[:, :, j0 + 1:j0 + 2],
                                               lam[:, 10 + d:11 + d], None, ALU.mult))
                    r = rinv[:, :, j].rearrange("p t h -> p t h ()").broadcast_to([P, NT, og, dv])
                    if kind == DIFF:
                        link(dve.tensor_tensor(o_tmp[:], src, r, ALU.mult))
                        h = j0 // 2
                        link(dve.tensor_tensor(y[:, :, h * P:(h + 1) * P], o_tmp[:, :, 0], o_tmp[:, :, 1], ALU.add))
                        for t in range(NT):
                            ins = dve.tensor_tensor_reduce(o_tmp[:, t, 0], y[:, t, h * P:(h + 1) * P],
                                                           y[:, t, h * P:(h + 1) * P], 1.0, 0.0, ALU.mult, ALU.add,
                                                           sq[:, t, h:h + 1])
                        link(ins)
                        head_asks.append(ask_root(sq[:, :, h], 1.0 / P, NORM_EPS, 2))
                        if h:
                            norm_head(l, h - 1)
                    else:
                        at = (D_POOL if kind == HYB else 0) + j0 * HD
                        link(dve.tensor_tensor(y[:, :, at:at + og * dv].rearrange("p t (h c) -> p t h c", c=dv), src, r,
                                               ALU.mult))
                dve.engine_nop().then_inc(o_read, 1)

            def soft_heads(l):
                kind = KIND[l]
                n = NSOFT[kind]
                mask = cst[:, {HYB: C_CHUNK, SWA: C_WINDOW}.get(kind, C_CAUSAL):][:, 0:384]
                if kind == SWA:
                    dve.wait_ge(got["sinks"], 16)
                if kind != HYB:
                    dve.wait_ge(rope_done, l - 1)
                for i in range(n + 4):
                    if kind == SWA and i in (1, 3):
                        add_bias(l, NPROJ[kind] - 2 + i // 2)
                    j = i - 1
                    if 0 <= j < n:
                        g, s = HEAD0[l] + j, SOFT0[l] + j
                        dve.wait_ge(scored, g + 1)
                        if s >= 4:
                            dve.wait_ge(pt_done, s - 3)
                        for t, c in enumerate((slice(0, P), slice(P, 3 * P))):
                            ins = dve.tensor_tensor_reduce(z[:, s % 4, c], bank[g % 2][:, c], mask[:, c], SCALE, -3e38,
                                                           ALU.add, ALU.max, mx[:, t, j:j + 1])
                        ins.then_inc(z_read, 1)
                        dve.wait_ge(z_read, g + 1)
                        if kind == SWA:
                            dve.tensor_scalar(nmx[:, :, j], mx[:, :, j], sinks[:, j:j + 1], -1.0, ALU.max,
                                              ALU.mult).then_inc(nmx_ready, 1)
                        else:
                            dve.tensor_scalar(nmx[:, :, j], mx[:, :, j], -1.0, None, ALU.mult).then_inc(nmx_ready, 1)
                    for place, half in out_halves(l, i):
                        lo(place, (half,))
                    j = i - 3
                    if 0 <= j < n and kind != DIFF:
                        s = SOFT0[l] + j
                        dve.wait_ge(pt_done, s + 1)
                        dve.tensor_copy(pt[:, s % 4], bank[4 + s % 2][:, 0:384]).then_inc(pt_ready, 1)
                    j = i - 4
                    if 0 <= j < n:
                        finish_group(l, j, True)

            def stick_heads(l):
                n = NSTICK[HYB]

                def take_scores(h):
                    b = STICK0[l] + h
                    g = HEAD0[l] + NSOFT[HYB] + h
                    dve.wait_ge(scored, g + 1)
                    if h >= 2:
                        dve.wait_ge(zm_ready, b - 1)
                        dve.wait_ge(sp_ready, b - 1)
                    dve.tensor_scalar(zs[:, b % 2], bank[g % 2][:, 0:384], SCALE, None, ALU.mult).then_inc(z_read, 1)

                def softplus(p):
                    for h in (p, p + 1):
                        b = STICK0[l] + h
                        dve.wait_ge(sp_log, b + 1)
                        if h >= 2:
                            dve.wait_ge(c_done, b - 1)
                        ins = dve.scalar_tensor_tensor(out=sps[:, b % 2], in0=zs[:, b % 2], scalar=0.0,
                                                       in1=es[:, b % 2], op0=ALU.max, op1=ALU.add)
                    link(ins)
                    for h in (p, p + 1):
                        b = STICK0[l] + h
                        dve.tensor_tensor(sps[:, b % 2], sps[:, b % 2], cst[:, C_STRICT:C_STRICT + 384],
                                          ALU.mult).then_inc(sp_ready, 1)

                for h in range(2):
                    take_scores(h)
                for p in range(0, n, 2):
                    softplus(p)
                    if p + 2 < n:
                        for h in (p + 2, p + 3):
                            take_scores(h)
                    for h in (p, p + 1):
                        b = STICK0[l] + h
                        dve.wait_ge(c_done, b + 1)
                        dve.wait_ge(zm_ready, b + 1)
                        dve.tensor_tensor(zm[:, b % 2], zm[:, b % 2], bank[4 + b % 2][:, 0:384],
                                          ALU.subtract).then_inc(arg_ready, 1)
                    if p:
                        for h in (p - 2, p - 1):
                            finish_group(l, NSOFT[HYB] + h, False)
                for h in (n - 2, n - 1):
                    finish_group(l, NSOFT[HYB] + h, False)

            def mixer_norm(l):
                g = next_gain()
                parts = ((0, D_POOL), (D_POOL, D_CHUNK), (D_POOL + D_CHUNK, D_SB))
                for t in range(NT):
                    for i, (at, w) in enumerate(parts):
                        ins = dve.tensor_tensor_reduce(h_in[:, t, at:at + w], y[:, t, at:at + w], y[:, t, at:at + w],
                                                       1.0 / w, 0.0, ALU.mult, ALU.add, sq[:, t, i:i + 1])
                link(ins)
                link(dve.tensor_copy(mv6[:], sq[:, :, 0:3]))
                r = root(ask_root(mv6[:].rearrange("p t c -> p (t c)"), 1.0, RMS_EPS, 6))
                for t in range(NT):
                    for i, (at, w) in enumerate(parts):
                        ins = dve.scalar_tensor_tensor(out=y[:, t, at:at + w], in0=y[:, t, at:at + w],
                                                       scalar=r[:, 3 * t + i:3 * t + i + 1], in1=g[:, at:at + w],
                                                       op0=ALU.mult, op1=ALU.mult)
                    ins.then_inc(nat_ready, 1)
                nat[0] += 2
                dve.wait_ge(nat_ready, nat[0])
                gain_done(1)

            def norm_head(l, h, last=False):
                r = root(head_asks.pop(0))
                for t in range(NT):
                    v = y[:, t, h * P:(h + 1) * P]
                    ins = dve.scalar_tensor_tensor(out=v, in0=v, scalar=r[:, t:t + 1], in1=subg[:, DIFF_SLOT[l]],
                                                   op0=ALU.mult, op1=ALU.mult)
                    if last:
                        ins.then_inc(nat_ready, 1)
                if last:
                    nat[0] += 2

            head_asks = []

            def y_in_place():
                for _ in range(NT):
                    dve.engine_nop().then_inc(nat_ready, 1)
                nat[0] += 2

            def gates_of(l):
                dve.wait_ge(logits, 1)
                dve.wait_ge(xn_hi_ready, 1)
                dve.tensor_tensor(xn_lo[:], x[:], xn_hi[:].bitcast(F32), ALU.subtract).then_inc(xn_lo_ready, 1)
                link(dve.tensor_copy(lg[:], bank[2][:, 0:16].rearrange("p (t e) -> p t e", t=NT)))
                for t in range(NT):
                    ins = dve.max(top[:, t], lg[:, t])
                link(ins)
                for t in range(NT):
                    ins = dve.max_index(topi[:, t], top[:, t], lg[:, t])
                link(ins)
                dve.tensor_copy(topf[:, :, 0:2], topi[:, :, 0:2])
                dve.tensor_tensor(topf[:, :, 3:4], top[:, :, 1:2], top[:, :, 0:1], ALU.subtract).then_inc(gap, 1)
                dve.wait_ge(gap_exp, 1)
                link(dve.tensor_scalar(topf[:, :, 5:6], topf[:, :, 4:5], 1.0, None, ALU.add))
                link(dve.reciprocal(topf[:, :, 6:7], topf[:, :, 5:6]))
                link(dve.tensor_tensor(topf[:, :, 7:8], topf[:, :, 6:7], topf[:, :, 4:5], ALU.mult))
                for t in range(NT):
                    for i, dst in ((0, gw), (1, lg)):
                        ins = dve.tensor_scalar(dst[:, t], cst[:, C_IOTA:C_IOTA + 8], topf[:, t, i:i + 1],
                                                topf[:, t, 6 + i:7 + i], ALU.is_equal, ALU.mult)
                    for i, dst in ((0, chosen), (1, top)):
                        ins = dve.tensor_scalar(dst[:, t], cst[:, C_IOTA:C_IOTA + 8], topf[:, t, i:i + 1], None,
                                                ALU.is_equal)
                link(ins)
                dve.tensor_tensor(gw[:], gw[:], lg[:], ALU.add)
                dve.tensor_tensor(chosen[:], chosen[:], top[:], ALU.add).then_inc(gates, 1)
                dve.wait_ge(ranked, 1)
                dve.tensor_copy(count[:], bank[3][:, 16:24])
                dve.tensor_copy(slot_of[:], bank[3][:, 0:16].rearrange("p (t e) -> p t e", t=NT)).then_inc(counted, 1)
                dve.wait_ge(counted, 1)

            def moe():
                hb = GRP0[1]
                (sg_, tg), (su, tu), (sd, td) = PLAN[1][2]

                def column(tile, t, e):
                    return tile[:, t, e:e + 1] if isinstance(e, int) else tile[:, t, bass.ds(e, 1)]

                def place_tokens(e):
                    for t in range(NT):
                        ins = dve.tensor_scalar(perm[:, t], iota[:], column(slot_of, t, e), column(chosen, t, e),
                                                ALU.is_equal, ALU.mult)
                    ins.then_inc(perm_ready, 1)

                def group(n, after_gate=None, before_down=None, after=None, last=False):
                    if not last:
                        lo((sg_, n + (tg + 1)))
                    if after_gate is not None:
                        after_gate()
                    dve.wait_ge(act_done, n + (hb + 1))
                    dve.wait_ge(used[su], n + (tu + 1))
                    dve.wait_ge(hl_ready, n + hb)
                    dve.tensor_tensor(h_f[:, 0], sg[:], bank[1][:, :], ALU.mult).then_inc(h_mid, 1)
                    if not last:
                        lo((su, n + (tu + 1)))
                    if before_down is not None:
                        before_down()
                    lo((sd, n + td))
                    if after is not None:
                        after()
                    dve.wait_ge(hh_ready, n + (hb + 1))
                    dve.tensor_tensor(h_lo[:, 0], bank[2][:, :].rearrange("p (f s) -> p f s", f=2),
                                      h_hi[:, 0].bitcast(F32), ALU.subtract).then_inc(hl_ready, 1)

                def split_result(e):
                    for b in range(4):
                        dve.wait_ge(ye_hi_ready, e * 4 + (b + 1))
                        c = slice((b % 2) * 512, (b % 2 + 1) * 512)
                        dve.tensor_tensor(ye_lo[:, b // 2, c], bank[4 + b][:, :], ye_hi[:, b // 2, c].bitcast(F32),
                                          ALU.subtract).then_inc(ye_lo_ready, 1)

                def add_result(e):
                    for t in range(NT):
                        for half in range(2):
                            c = slice(half * 512, (half + 1) * 512)
                            dve.wait_ge(scattered, e * 4 + (2 * t + half + 1))
                            dve.wait_ge(added, e * 4 + (2 * t + half + 1))
                            dve.scalar_tensor_tensor(out=y[:, t, c], in0=bank[2 + half][:, :],
                                                     scalar=column(gw, t, e), in1=y[:, t, c], op0=ALU.mult,
                                                     op1=ALU.add).then_inc(added, 1)

                def next_perm(e):
                    dve.wait_ge(perm_turned, e + 1)
                    place_tokens((e + 1) % N_EXP)

                def expert(e, last=False):
                    n0 = e * GE
                    group(n0 + 1)
                    group(n0 + 2, after_gate=lambda: next_perm(e))
                    with dve.Fori(3, GE - last) as i:
                        group(n0 + i)
                    if last:
                        group(n0 + GE - 1, last=True)
                        split_result(e)
                        add_result(e)
                    else:
                        group(n0 + GE, before_down=lambda: split_result(e), after=lambda: add_result(e))

                for t in range(NT):
                    for half in range(2):
                        dve.memset(y[:, t, half * 512:(half + 1) * 512], 0.0).then_inc(added, 1)
                dve.wait_ge(got["iota"], 16)
                place_tokens(0)
                group(0)
                with dve.Fori(0, N_EXP - 1) as e:
                    expert(e)
                expert(N_EXP - 1, last=True)
                dve.wait_ge(added, 4 * N_EXP + 4)

            def hidden_lo(par, i, hb):
                dve.wait_ge(hh_ready, i + (hb + 1))
                dve.tensor_tensor(h_lo[:, par], h_f[:, par, :].rearrange("p (f s) -> p f s", f=2),
                                  h_hi[:, par].bitcast(F32), ALU.subtract).then_inc(hl_ready, 1)

            def swiglu(l):
                g, hb = groups(l), GRP0[l]
                (sg_, tg), (su, tu), (sd, td) = PLAN[l][2]

                def hidden(i):
                    dve.wait_ge(act_done, i + (hb + 1))
                    if not isinstance(i, int) or i > 0:
                        dve.wait_ge(hl_ready, i + hb)
                    dve.tensor_tensor(h_f[:, 0], sg[:], bank[1][:, :], ALU.mult).then_inc(h_mid, 1)

                lo((sg_, tg + 1))
                hidden(0)
                lo((su, tu + 1))
                hidden_lo(0, 0, hb)
                with dve.Fori(1, g - 1) as i:
                    lo((sg_, i + (tg + 1)))
                    hidden(i)
                    lo((su, i + (tu + 1)))
                    hidden_lo(0, i, hb)
                    lo((sd, i + td))
                hidden(g - 1)
                hidden_lo(0, g - 1, hb)
                lo((sd, td + g - 1))

            def mlp(l):
                g, hb = groups(l), GRP0[l]
                (s0, t0), (s1, t1), (sd, td) = PLAN[l][2]

                def square(par, i):
                    dve.wait_ge(act_done, i + (hb + 1))
                    if not isinstance(i, int) or i >= 2:
                        dve.wait_ge(hl_ready, i + (hb - 1))
                    dve.tensor_tensor(h_f[:, par], sg[:], sg[:], ALU.mult).then_inc(h_mid, 1)

                square(0, 0)
                lo((s0, t0 + 1))
                hidden_lo(0, 0, hb)
                with dve.Fori(0, 6) as j:
                    square(1, j * 2 + 1)
                    lo((s1, j + (t1 + 1)))
                    hidden_lo(1, j * 2 + 1, hb)
                    lo((sd, j * 2 + (td + 1)))
                    square(0, j * 2 + 2)
                    lo((s0, j + (t0 + 2)))
                    hidden_lo(0, j * 2 + 2, hb)
                    lo((sd, j * 2 + (td + 2)))
                for i in range(g - 3, g):
                    square(i % 2, i)
                    if i == g - 3:
                        lo((s1, t1 + g // 2 - 1))
                    hidden_lo(i % 2, i, hb)
                    lo((sd, td + i))

            for l in range(NL):
                proj, outp, first = PLAN[l]
                to_t(3 * l)
                if l == 0:
                    for c in range(2):
                        lo(proj[c])
                lo(proj[2])
                if KIND[l] == SWA:
                    dve.wait_ge(got["swa_bias"], 16)
                for c in range(len(proj) - 2):
                    if KIND[l] == SWA:
                        add_bias(l, c)
                    if c + 3 < len(proj):
                        lo(proj[c + 3])
                if l == 0:
                    dve.wait_ge(cst_loaded, 16)
                    setup()
                if KIND[l] == HYB:
                    dve.wait_ge(got["pool_scale"], 16)
                    dve.wait_ge(pool_out, l + 1)
                    dve.tensor_tensor(y[:, :, 0:D_POOL], bank[2][:, :].rearrange("p (t c) -> p t c", t=NT),
                                      pool_scale[:, l].rearrange("p c -> p () c").broadcast_to([P, NT, D_POOL]),
                                      ALU.mult).then_inc(pool_read, 1)
                    dve.wait_ge(pool_read, l + 1)
                else:
                    if l == 2:
                        dve.wait_ge(rope_sin, 1)
                    dve.wait_ge(proj_ev, PROJ0[l + 1] - 2)
                    rotate(dve, link, l, False).then_inc(rope_done, 1)
                soft_heads(l)
                if KIND[l] == HYB:
                    stick_heads(l)
                    mixer_norm(l)
                elif KIND[l] == DIFF:
                    norm_head(l, 7, last=True)
                else:
                    y_in_place()
                to_t(3 * l + 1)
                lo(outp[3])
                for i in range(2):
                    lo(first[i])
                if KIND[l] == HYB:
                    if l == 0:
                        for t in range(NT):
                            dve.wait_ge(x_loaded[t], 16)
                    residual_norm(2 * l)
                else:
                    rms_norm(2 * l)
                to_t(3 * l + 2)
                if l != 1:
                    lo(first[2])
                    (swiglu if KIND[l] == HYB else mlp)(l)
                else:
                    gates_of(l)
                    moe()
                if l + 1 < NL:
                    for c in range(2):
                        lo(PLAN[l + 1][0][c])
                if KIND[l] == HYB:
                    residual_norm(2 * l + 1, to_turn=(l == 0))
                if l >= 1:
                    rms_norm(None if l == 1 else 2 * l + 1, final=(l == NL - 1))


def constants():
    import numpy as np
    f = np.float32
    c = np.zeros((P, C_N), f)
    i = np.arange(P)[:, None]
    j = np.arange(P)[None, :]
    c[:, C_ID:C_ID + P] = i == j
    c[:, C_TRI:C_TRI + P] = i >= j
    c[:, C_ONE:C_ONE + P] = 1
    c[:, C_FLIP:C_FLIP + P] = 8.0 * (i + j == P - 1)
    kt = np.arange(S)[None, :]

    def two_tiles(ok):
        return np.where(np.concatenate([ok(i, kt[:, :P]), ok(i + P, kt)], axis=1), 0.0, NEG).astype(f)

    c[:, C_CAUSAL:C_CAUSAL + 384] = two_tiles(lambda q, k: k <= q)
    c[:, C_CHUNK:C_CHUNK + 384] = two_tiles(lambda q, k: k // 64 <= q // 64)
    c[:, C_WINDOW:C_WINDOW + 384] = two_tiles(lambda q, k: (k <= q) & (q - k < 128))
    strict = np.concatenate([i < kt, (i + P) < kt[:, P:]], axis=1)
    c[:, C_STRICT:C_STRICT + 384] = strict
    c[:, C_STRICTNEG:C_STRICTNEG + 384] = np.where(strict, 0.0, NEG)
    c[:, C_IOTA:C_IOTA + 8] = np.arange(8)
    c[:, C_INV:C_INV + 8] = (f(500000.0) ** (-np.arange(0, 16, 2, dtype=f) / f(16))).astype(f)
    c[:, C_HALF:C_HALF + 16] = -0.5
    c[:, C_ONECOL] = 1
    tq, ts = np.arange(S)[None, :], np.arange(S)[:, None]
    pm = np.zeros((P, NT, 4, S), f)
    for g, w in enumerate((2, 4, 8, 16)):
        m = ((tq >= ts) & (tq - ts < w)) / np.minimum(tq + 1.0, w) - (tq == ts)
        pm[:, :, g, :] = m.astype(f).reshape(NT, P, S).transpose(1, 0, 2)
    iota = np.broadcast_to(np.arange(S, dtype=f), (P, S)).copy()
    return {"cst": c, "pool_m": pm, "iota": iota}


_INS = ["x", "w_in", "pool_w", "pool_scale", "rel_bias", "g_mix", "w_out", "ln1_g", "ln1_b", "ln2_g", "ln2_b",
        "ffn_wg", "ffn_wu", "ffn_wd", "moe_router", "moe_wg", "moe_wu", "moe_wd", "positions_2", "attn_norm_g_2",
        "mlp_norm_g_2", "diff_w_in_2", "diff_w_out_2", "diff_lam_q1_2", "diff_lam_k1_2", "diff_lam_q2_2",
        "diff_lam_k2_2", "diff_subln_g_2", "moba_w_in_2", "moba_w_out_2", "swa_w_in_2", "swa_b_in_2", "swa_sinks_2",
        "swa_w_out_2", "mlp_w_up_2", "mlp_w_down_2", "final_norm_g_2"]


def kernel(**inputs):
    import numpy as np
    import concourse.bacc as bacc
    from concourse.bass_utils import run_bass_kernel_spmd as run

    nc = bacc.Bacc("TRN2", target_bir_lowering=False, num_devices=1)
    arrays = {name: np.ascontiguousarray(inputs[name]) for name in _INS}
    arrays.update(constants())
    aps = {name: nc.dram_tensor("in_" + name, a.shape, mybir.dt.from_np(a.dtype), kind="ExternalInput").ap()
           for name, a in arrays.items()}
    out = nc.dram_tensor("out", (1, S, D), F32, kind="ExternalOutput").ap()
    scratch = nc.dram_tensor("bias_scratch", (12, REVW), F32, kind="Internal").ap()
    build(nc, aps, out, scratch)
    r = run(nc, [{"in_" + n: a for n, a in arrays.items()}], core_ids=[0])
    return r.results[0]["out"]
```
